# Optimizing a Trainium2 kernel written in Bass

```python
import math
import jax, jax.numpy as jnp
from jax import lax
import numpy as np

D_MODEL = 1024
BATCH = 1
SEQ = 256
DEPTH = 2

N_A_LAYERS = DEPTH // 2
N_B_LAYERS = DEPTH - N_A_LAYERS
HEAD_DIM = 64
N_HEADS = D_MODEL // HEAD_DIM
DECAY_LORA = 64
AAA_LORA = 64
GATE_LORA = 160
N_SHIFT_MIX = 6
GN_EPS = 64e-5
RMS_EPS = 1e-6
SB_BLOCK = 128
N_GROUPS = 4
EXPERTS_PER_GROUP = 4
N_EXPERTS = N_GROUPS * EXPERTS_PER_GROUP
TOP_K_INNER = 2
D_EXPERT = 256

kernel_name = "yoco_rwkv7_stickbreak_hmoe"

def rmsnorm(x, g):
    xf = x.astype(jnp.float32)
    y = xf * lax.rsqrt(jnp.mean(xf * xf, axis=-1, keepdims=True) + RMS_EPS)
    return (y * g.astype(jnp.float32)).astype(x.dtype)

def token_shift(x):
    return jnp.pad(x[:, :-1], ((0, 0), (1, 0), (0, 0)))

def wkv7_scan(r, decay, k, v, a, b):
    Bsz, T, H, N = r.shape

    def step(S, inp):
        r_t, w_t, k_t, v_t, a_t, b_t = inp
        sa = jnp.einsum('bhij,bhj->bhi', S, a_t)
        S = (S * w_t[:, :, None, :] + sa[..., None] * b_t[:, :, None, :]
             + v_t[..., None] * k_t[:, :, None, :])
        y = jnp.einsum('bhij,bhj->bhi', S, r_t)
        return S, y

    xs = tuple(jnp.moveaxis(t, 1, 0) for t in (r, decay, k, v, a, b))
    S0 = jnp.zeros((Bsz, H, N, N), jnp.float32)
    _, ys = lax.scan(step, S0, xs)
    return jnp.moveaxis(ys, 0, 1)

def rwkv7_time_mix(x, mix, w_rkv, w0, w1, w2, a0, a1, a2, g1, g2, k_k, k_a, r_k,
                   lnx_w, lnx_b, w_out):
    Bsz, T, C = x.shape
    H, N = N_HEADS, HEAD_DIM
    xx = token_shift(x) - x
    xs = x[None] + xx[None] * mix[:, None, None, :]
    rkv = jnp.einsum('nbtc,ncd->nbtd', xs[:3], w_rkv)
    r, k, v = rkv[0], rkv[1], rkv[2]
    xw, xa, xg = xs[3], xs[4], xs[5]
    w = -jax.nn.softplus(-(w0 + jnp.tanh(xw @ w1) @ w2)) - 0.5
    a = jax.nn.sigmoid(a0 + (xa @ a1) @ a2)
    g = jax.nn.sigmoid(xg @ g1) @ g2

    heads = lambda t: t.reshape(Bsz, T, H, N).astype(jnp.float32)
    kk = heads(k * k_k)
    kk = kk / jnp.maximum(jnp.sqrt(jnp.sum(kk * kk, axis=-1, keepdims=True)), 1e-12)
    k = k * (1.0 + (a - 1.0) * k_a)
    rh, kh, vh, ah = heads(r), heads(k), heads(v), heads(a)
    decay = jnp.exp(-jnp.exp(heads(w)))
    y = wkv7_scan(rh, decay, kh, vh, -kk, kk * ah)

    mu = jnp.mean(y, axis=-1, keepdims=True)
    var = jnp.mean(jnp.square(y - mu), axis=-1, keepdims=True)
    y = ((y - mu) * lax.rsqrt(var + GN_EPS)).reshape(Bsz, T, C)
    y = y * lnx_w.astype(jnp.float32) + lnx_b.astype(jnp.float32)
    bonus = jnp.sum(rh * kh * r_k.astype(jnp.float32), axis=-1, keepdims=True) * vh
    y = (y + bonus.reshape(Bsz, T, C)).astype(x.dtype)
    return (y * g) @ w_out

def stick_breaking_attention(q, k, v):
    Bsz, H, S, N = q.shape
    nb = S // SB_BLOCK
    scale = 1.0 / math.sqrt(N)
    qb = q.reshape(Bsz, H, nb, SB_BLOCK, N).transpose(2, 0, 1, 3, 4)
    kpos = jnp.arange(S)

    def block(args):
        i, q_blk = args
        qpos = i * SB_BLOCK + jnp.arange(SB_BLOCK)
        z = jnp.einsum('bhqd,bhkd->bhqk', q_blk, k).astype(jnp.float32) * scale
        mask = kpos[None, :] < qpos[:, None]
        u = jnp.where(mask, jax.nn.softplus(z), 0.0)
        suffix = lax.cumsum(u, axis=3, reverse=True) - u
        att = jnp.where(mask, jnp.exp(jax.nn.log_sigmoid(z) - suffix), 0.0)
        return jnp.einsum('bhqk,bhkd->bhqd', att.astype(v.dtype), v)

    o = lax.map(block, (jnp.arange(nb), qb))
    return o.transpose(1, 2, 0, 3, 4).reshape(Bsz, H, S, N)

def hier_moe(x, w_group, b_group, w_inner, b_inner, w_gate, w_up, w_down):
    gl = jnp.einsum('btd,dg->btg', x, w_group).astype(jnp.float32) + b_group.astype(jnp.float32)
    pg = jax.nn.softmax(gl, axis=-1)
    gval, gidx = lax.top_k(pg, 1)
    il = jnp.einsum('btd,dge->btge', x, w_inner).astype(jnp.float32) + b_inner.astype(jnp.float32)
    il_sel = jnp.einsum('btge,btg->bte', il, jax.nn.one_hot(gidx[..., 0], N_GROUPS, dtype=jnp.float32))
    pi = jax.nn.softmax(il_sel, axis=-1)
    ival, iidx = lax.top_k(pi, TOP_K_INNER)
    weight = gval * ival / jnp.sum(ival, axis=-1, keepdims=True)
    eidx = gidx * EXPERTS_PER_GROUP + iidx
    gates = jnp.sum(jax.nn.one_hot(eidx, N_EXPERTS, dtype=jnp.float32) * weight[..., None], axis=-2)
    h = (jax.nn.silu(jnp.einsum('btd,edf->btef', x, w_gate))
         * jnp.einsum('btd,edf->btef', x, w_up))
    h = h * gates.astype(h.dtype)[..., None]
    return jnp.einsum('btef,efd->btd', h, w_down)

def setup_inputs(seed: int = 0) -> dict:
    key = jax.random.key(seed)
    ks = iter(jax.random.split(key, 48))
    C, H, N = D_MODEL, N_HEADS, HEAD_DIM
    nA, nB = N_A_LAYERS, N_B_LAYERS
    G, E, NE, F = N_GROUPS, EXPERTS_PER_GROUP, N_EXPERTS, D_EXPERT

    def nrm(shape, scale):
        return jax.random.normal(next(ks), shape, jnp.float32) * scale

    def unif(shape, lo, hi):
        return jax.random.uniform(next(ks), shape, jnp.float32, lo, hi)

    return {
        "x": nrm((BATCH, SEQ, C), 1.0),
        "norm_mix": 1.0 + nrm((DEPTH, C), 0.02),
        "norm_ffn": 1.0 + nrm((DEPTH, C), 0.02),
        "norm_kv": 1.0 + nrm((C,), 0.02),
        "norm_final": 1.0 + nrm((C,), 0.02),
        "rw_mix": unif((nA, N_SHIFT_MIX, C), 0.0, 1.0),
        "rw_w_rkv": nrm((nA, 3, C, C), C ** -0.5),
        "rw_w0": unif((nA, C), -5.0, -1.0),
        "rw_w1": nrm((nA, C, DECAY_LORA), C ** -0.5),
        "rw_w2": nrm((nA, DECAY_LORA, C), 0.1 * DECAY_LORA ** -0.5),
        "rw_a0": nrm((nA, C), 0.1),
        "rw_a1": nrm((nA, C, AAA_LORA), C ** -0.5),
        "rw_a2": nrm((nA, AAA_LORA, C), 0.1 * AAA_LORA ** -0.5),
        "rw_g1": nrm((nA, C, GATE_LORA), C ** -0.5),
        "rw_g2": nrm((nA, GATE_LORA, C), GATE_LORA ** -0.5),
        "rw_k_k": 0.85 + nrm((nA, C), 0.05),
        "rw_k_a": 1.0 + nrm((nA, C), 0.05),
        "rw_r_k": nrm((nA, H, N), 0.1),
        "rw_lnx_w": 1.0 + nrm((nA, C), 0.02),
        "rw_lnx_b": nrm((nA, C), 0.02),
        "rw_w_out": nrm((nA, C, C), C ** -0.5),
        "w_kv": nrm((C, 2 * C), C ** -0.5),
        "sb_w_q": nrm((nB, C, C), C ** -0.5),
        "sb_w_out": nrm((nB, C, C), C ** -0.5),
        "moe_w_group": nrm((DEPTH, C, G), C ** -0.5),
        "moe_b_group": nrm((DEPTH, G), 0.01),
        "moe_w_inner": nrm((DEPTH, C, G, E), C ** -0.5),
        "moe_b_inner": nrm((DEPTH, G, E), 0.01),
        "moe_w_gate": nrm((DEPTH, NE, C, F), C ** -0.5),
        "moe_w_up": nrm((DEPTH, NE, C, F), C ** -0.5),
        "moe_w_down": nrm((DEPTH, NE, F, C), F ** -0.5),
    }

def reference(x, norm_mix, norm_ffn, norm_kv, norm_final,
              rw_mix, rw_w_rkv, rw_w0, rw_w1, rw_w2, rw_a0, rw_a1, rw_a2, rw_g1, rw_g2,
              rw_k_k, rw_k_a, rw_r_k, rw_lnx_w, rw_lnx_b, rw_w_out,
              w_kv, sb_w_q, sb_w_out,
              moe_w_group, moe_b_group, moe_w_inner, moe_b_inner,
              moe_w_gate, moe_w_up, moe_w_down):
    Bsz, S, C = x.shape
    H, N = N_HEADS, HEAD_DIM
    h = x
    k_shared = None
    v_shared = None
    for l in range(DEPTH):
        hn = rmsnorm(h, norm_mix[l])
        if l < N_A_LAYERS:
            i = l
            h = h + rwkv7_time_mix(hn, rw_mix[i], rw_w_rkv[i], rw_w0[i], rw_w1[i], rw_w2[i],
                                   rw_a0[i], rw_a1[i], rw_a2[i], rw_g1[i], rw_g2[i],
                                   rw_k_k[i], rw_k_a[i], rw_r_k[i], rw_lnx_w[i], rw_lnx_b[i],
                                   rw_w_out[i])
        else:
            j = l - N_A_LAYERS
            q = (hn @ sb_w_q[j]).reshape(Bsz, S, H, N).transpose(0, 2, 1, 3)
            o = stick_breaking_attention(q, k_shared, v_shared)
            h = h + o.transpose(0, 2, 1, 3).reshape(Bsz, S, C) @ sb_w_out[j]
        h = h + hier_moe(rmsnorm(h, norm_ffn[l]), moe_w_group[l], moe_b_group[l],
                         moe_w_inner[l], moe_b_inner[l], moe_w_gate[l], moe_w_up[l],
                         moe_w_down[l])
        if l == N_A_LAYERS - 1:
            kv = (rmsnorm(h, norm_kv) @ w_kv).reshape(Bsz, S, 2, H, N)
            k_shared = kv[:, :, 0].transpose(0, 2, 1, 3)
            v_shared = kv[:, :, 1].transpose(0, 2, 1, 3)
    return rmsnorm(h, norm_final)


_drawn_inputs = setup_inputs


def setup_inputs(seed=0):
    import zlib

    import numpy as np

    out = dict(_drawn_inputs(seed))
    spreads = {}
    factors = {'norm_kv': 3.517,
     'norm_final': 8.281,
     'rw_w1': 6.683,
     'rw_w2': 6.596,
     'rw_lnx_w': 2.965,
     'rw_lnx_b': 2.845,
     'moe_b_group': 3.046,
     'moe_b_inner': 7.629}
    for name, (base, spread) in spreads.items():
        noise = np.random.default_rng([zlib.crc32(name.encode()), seed]).standard_normal(out[name].shape)
        drawn = base * np.exp(spread * noise) if base else spread * noise
        out[name] = __import__('jax').numpy.asarray(drawn.astype(out[name].dtype))
    for name, factor in factors.items():
        out[name] = (out[name] * factor).astype(out[name].dtype)
    return out
```

```python
import concourse.bass as bass
from concourse import mybir
from contextlib import ExitStack

PHASES = ["rwkv", "moe0", "attn", "moe1"]


def trunk_program(nc, x, norm_mix, norm_ffn, norm_kv, norm_final,
                  rw_mix, rw_w_rkv, rw_w0, rw_w1, rw_w2, rw_a0, rw_a1, rw_a2, rw_g1, rw_g2,
                  rw_k_k, rw_k_a, rw_r_k, rw_lnx_w, rw_lnx_b, rw_w_out,
                  w_kv, sb_w_q, sb_w_out,
                  moe_w_group, moe_b_group, moe_w_inner, moe_b_inner,
                  moe_w_gate, moe_w_up, moe_w_down, out):
    f32, f32r = mybir.dt.float32, mybir.dt.float32r
    ALU, ACT, AX = mybir.AluOpType, mybir.ActivationFunctionType, mybir.AxisListType

    P = 128
    T, C = x.shape[1], x.shape[2]
    NT = T // P
    NC = C // P
    HALF = 512
    E = moe_w_gate.shape[1]
    G = moe_w_group.shape[2]
    EG = E // G
    F = moe_w_gate.shape[3]
    NF = F // P
    NR = G + E
    RMS_EPS = 1e-6
    GN_EPS = 64e-5
    HD = rw_r_k.shape[2]
    CH = 64
    LOG_DECAY = 0.6065306597126334
    LW, LG = rw_w1.shape[2], rw_g1.shape[2]
    HH = 8

    def dense_piece(w, n, g):
        v = w[g * HALF:(g + 1) * HALF, n * HALF:(n + 1) * HALF].rearrange("(b p) c -> p b c", p=P)
        return [(0, v)]

    def load_dense(sp, dst, w, n, g, sem):
        v = w[g * HALF:(g + 1) * HALF, n * HALF:(n + 1) * HALF].rearrange("(b p) c -> p b c", p=P)
        for a in range(2):
            sp.dma_start(dst[:, 2 * a:2 * a + 2, :], v[:, 2 * a:2 * a + 2, :]).then_inc(sem, 16)

    dense_pieces = {}
    base = {}
    n_pieces = 0
    for ph in PHASES:
        base[ph] = n_pieces
        mats = {"rwkv": [(rw_w_rkv[0, 1], 2), (rw_w_rkv[0, 0], 2), (rw_w_rkv[0, 2], 2), (rw_w_out[0], 2)],
                "attn": [(w_kv, 4), (sb_w_q[0], 2), (sb_w_out[0], 2)]}.get(ph)
        if mats is None:
            n_pieces += 3 * E
        else:
            for w, halves in mats:
                for n in range(halves):
                    for g in range(2):
                        dense_pieces[n_pieces] = (w, n, g)
                        n_pieces += 1
    TOTAL = n_pieces

    ctx = ExitStack()
    with ctx:
        def sem(name):
            return ctx.enter_context(nc.semaphore(name))

        fence = ctx.enter_context(nc.sbuf_tensor("arena", [P, 51200], f32))
        ARENA = 16512
        SIZE = 51200 * 4
        cursor = [0]

        def place(name, shape, dt=f32, at=None):
            size = 4
            for s in shape[1:]:
                size *= s
            size = (size + 31) // 32 * 32
            if at is None:
                at = cursor[0]
                cursor[0] += size
            assert at + size <= SIZE, (name, at, size)
            return nc.alloc_sbuf_tensor_at(name, shape, dt, offset=ARENA + at)

        KB = 1024
        w_ring = [place(f"w_ring{i}", [P, 4, HALF]) for i in range(3)]
        whi = [place(f"w_hi{i}", [P, 4, HALF], f32r) for i in range(3)]
        wlo = [place(f"w_lo{i}", [P, 4, HALF], f32r) for i in range(3)]
        h_at = cursor[0]
        h = place("h", [P, NT, C])
        ident = place("ident", [P, P])
        causal = place("causal", [P, P])
        from_s = place("from_s", [P, P])
        ones = place("ones", [P, P])
        n_rows = 88
        cols = place("cols", [P, n_rows])
        wr = [place(f"wr{k}", [P, NC, NR]) for k in range(2)]
        wr_hi = place("wr_hi", [P, NC, NR], f32r)
        wr_lo = place("wr_lo", [P, NC, NR], f32r)
        br = [place(f"br{k}", [P, NR]) for k in range(2)]
        ss = place("ss", [P, NT])
        ms = place("ms", [P, NT])
        rec = place("rec", [P, NT])
        rstd = place("rstd", [P, NT])
        R0 = cursor[0]

        XA_AT = R0
        xa_hi = place("xa_hi", [P, NC, T], f32r, at=XA_AT)
        xa_lo = place("xa_lo", [P, NC, T], f32r, at=XA_AT + 8 * KB)
        xb_hi = place("xb_hi", [P, NC, T], f32r, at=XA_AT + 16 * KB)
        xb_lo = place("xb_lo", [P, NC, T], f32r, at=XA_AT + 24 * KB)
        gain_row = place("gain_row", [P, C], at=XA_AT + 16 * KB)
        xs = place("xs", [P, NT, C], at=XA_AT + 32 * KB)
        prow = place("prow", [n_rows, P], at=XA_AT + 40 * KB)
        M0 = XA_AT + 40 * KB
        off = [M0]

        def mplace(name, shape, dt=f32):
            size = 4
            for s in shape[1:]:
                size *= s
            size = (size + 31) // 32 * 32
            t = place(name, shape, dt, at=off[0])
            off[0] += size
            return t

        lg = mplace("lg", [P, NT, NR])
        rev = mplace("rev", [P, EG])
        gates = mplace("gates", [P, NT, E])
        r_gs = mplace("r_gs", [P, NT, G])
        r_eg = mplace("r_eg", [P, NT, G])
        r_eq = mplace("r_eq", [P, NT, G])
        r_fg = mplace("r_fg", [P, NT, G])
        r_ilm = mplace("r_ilm", [P, NT, G, EG])
        r_il = mplace("r_il", [P, NT, EG])
        r_d = mplace("r_d", [P, NT, EG])
        r_d2 = mplace("r_d2", [P, NT, EG])
        r_f1 = mplace("r_f1", [P, NT, EG])
        r_f2 = mplace("r_f2", [P, NT, EG])
        r_s = mplace("r_s", [P, 10, NT])
        silu_g = mplace("silu_g", [P, NT, F])
        hact = mplace("hact", [P, NT, F])
        hT_hi = mplace("hT_hi", [P, NF, T], f32r)
        hT_lo = mplace("hT_lo", [P, NF, T], f32r)

        off[0] = M0
        kT = mplace("kT", [P, NC, T])
        qT = mplace("qT", [P, NC, T])
        v_att = mplace("v_att", [P, NT, C])
        ZW = T + P
        z_sb = [mplace(f"z_sb{i}", [P, 2, ZW]) for i in range(3)]
        z_abs = mplace("z_abs", [P, 2, ZW])
        z_exp = mplace("z_exp", [P, 2, ZW])
        z_ln = [mplace(f"z_ln{i}", [P, 2, ZW]) for i in range(2)]
        u_sp = [mplace(f"u_sp{i}", [P, 2, ZW]) for i in range(2)]
        log_a = [mplace(f"log_a{i}", [P, 2, ZW]) for i in range(2)]
        att = [mplace(f"att{i}", [P, 2, ZW]) for i in range(3)]

        def rplace(name, shape, kb, dt=f32):
            return place(name, shape, dt, at=R0 + int(kb * KB))

        k_s = rplace("k_s", [P, NT, C], 32)
        r_s_ = rplace("r_tok", [P, NT, C], 40)
        v_s = rplace("v_s", [P, NT, C], 48)
        sig = rplace("sig", [P, NT, C], 56)
        a_s = rplace("a_s", [P, NT, C], 64)
        kk = rplace("kk", [P, NT, C], 72)
        hnT = rplace("hnT", [P, NC, T], 80)
        dxT = rplace("dxT", [P, NC, T], 88)
        z_tok = rplace("z_tok", [P, NT, C], 56)
        mixed_ = [rplace("mix_k", [P, NC, T], 72), rplace("mix_w", [P, NC, T], 40), rplace("mix_a", [P, NC, T], 48),
                  rplace("mix_g", [P, NC, T], 72), rplace("mix_r", [P, NC, T], 40), rplace("mix_v", [P, NC, T], 48)]
        MIX_ROW = [2, 3, 4, 5, 0, 1]
        MIX_ROW = [1, 3, 4, 5, 0, 2]
        lora1 = rplace("lora1", [P, NC, 2 * LW + LG], 56)
        w2x = rplace("w2x", [LW + 1, C], 96)
        a2x = rplace("a2x", [LW + 1, C], 100)
        rk_row = rplace("rk_row", [P, C], 96)
        g2a = rplace("g2a", [P, C], 96)
        g2b = rplace("g2b", [LG - P, C], 100)
        zw = rplace("zw", [LW + 1, T], 104)
        za = rplace("za", [LW + 1, T], 105)
        zg = rplace("zg", [P, T], 106)
        zg2 = rplace("zg2", [LG - P, T], 107)
        kk_row = place("kk_row", [P, C], at=h_at)
        ka_row = place("ka_row", [P, C], at=h_at + 4 * KB)
        off[0] = R0 + 108 * KB
        to_t = mplace("to_t", [P, P])
        before_t = mplace("before_t", [P, P])
        LEVELS = 6
        level = [mplace(f"level{i}", [P, P]) for i in range(LEVELS)]
        level0T = mplace("level0T", [P, P])
        in_chunk = mplace("in_chunk", [P, 2])
        chunk_decay = mplace("chunk_decay", [P, NC, T // CH])
        n2 = mplace("n2", [P, NT, HH])
        n2i = mplace("n2i", [P, NT, HH])
        bonus = mplace("bonus", [P, NT, 2 * HH])
        e0 = rplace("e0", [P, NT, HALF], 80)
        e1 = rplace("e1", [P, NT, HALF], 84)
        tmp = rplace("tmp", [P, NT, HALF], 88)
        yb = rplace("yb", [P, NT, HALF], 92)
        AT = rplace("AT", [P, 4, T], 0)
        BT = rplace("BT", [P, 4, T], 4)
        KT = rplace("KT", [P, 4, T], 8)
        RT = rplace("RT", [P, 4, T], 12)
        lnw_row = rplace("lnw_row", [P, C], 16)
        lnb_row = rplace("lnb_row", [P, C], 20)
        vb = rplace("vb", [P, HALF], 24)
        y_sq = rplace("y_sq", [P, HALF], 26)
        y_m = rplace("y_m", [P, 4, HH], 28)
        off[0] = 24 * KB
        NT_ = [mplace(f"n_t{j}", [P, 4, P]) for j in range(NT)]
        X = [mplace(f"inv{j}", [P, 4, P]) for j in range(NT)]
        XT = [mplace(f"inv_t{j}", [P, 4, P]) for j in range(NT)]
        W_ = [mplace(f"w_lev{j}", [P, 4, P]) for j in range(NT)]
        AakT = [mplace(f"aak_t{j}", [P, 4, P]) for j in range(NT)]
        ArkT = [mplace(f"ark_t{j}", [P, 4, P]) for j in range(NT)]
        ArbT = [[mplace(f"arb_t{q}{j}", [P, 4, P]) for j in range(NT)] for q in range(2)]
        XaT = [mplace(f"xa_t{j}", [P, 4, P]) for j in range(NT)]
        U = mplace("u_rows", [P, NT, HH, HD])
        Y0 = mplace("y_own", [P, NT, HH, HD])
        S = [mplace(f"state{c}", [P, 4, HD]) for c in range(4)]
        assert off[0] <= 72 * KB

        PS = ctx.enter_context(nc.psum_tensor("ps", [P, 8, HALF], f32))

        x_loaded = sem("x_loaded")
        params_loaded = sem("params_loaded")
        router_loaded = sem("router_loaded")
        w_loaded = [sem(f"w_loaded{i}") for i in range(3)]
        hi_ready = sem("hi_ready")
        lo_ready = sem("lo_ready")
        piece_used = sem("piece_used")
        ident_ready = sem("ident_ready")
        cols_psum = sem("cols_psum")
        cols_ready = sem("cols_ready")
        dve_step = sem("dve_step")
        out_written = sem("out_written")
        final_ready = sem("final_ready")
        gain_loaded = sem("gain_loaded")

        norm_sems = {q: sem(f"norm_{q}") for q in ("squares", "recip", "rstd", "scaled", "turned", "hi", "lo")}
        norm_counts = dict.fromkeys(norm_sems, 0)

        class Norm:

            def __init__(s, h_ready, gains, turned=True):
                s.h_ready = h_ready
                s.gains = gains
                s.before = dict(norm_counts)
                for q, n in (("squares", NT), ("recip", 1), ("rstd", 1), ("scaled", NT),
                             ("turned", 4 * turned), ("hi", 4 * bool(gains)), ("lo", 4 * bool(gains))):
                    norm_counts[q] += n

            def at(s, q, n):
                return norm_sems[q], s.before[q] + n

        h_done = {}
        prev = (x_loaded, 32)
        norms = {}
        PER = dict(wr_hi=1, wr_lo=1, logits=1, gs=1, eg=1, m2=1, e2=1, gates=1, silu=NT * E, hact=NT * E,
                   hT_psum=E, hT_hi=E, hT_lo=E)
        moe_sems = {q: sem(f"moe_{q}") for q in PER}
        for ph in PHASES:
            h_done[ph] = sem(f"{ph}_h_done")
            if ph.startswith("moe"):
                k = int(ph[3])
                norms[ph] = Norm(prev, [(16 + 8 * k, xa_hi, xa_lo)])
            if ph == "rwkv":
                norms[ph] = Norm(prev, [])
                rw = {q: sem(f"rw_{q}") for q in
                      ("hn_act", "hn_dve", "lora_loaded", "rows_loaded", "rk_loaded", "late_loaded", "x_again",
                       "mixed", "x_hi", "x_lo", "lora1", "z", "zones", "lora2", "sig", "a", "k", "r", "v",
                       "cum", "decay", "decay_used", "kk0", "sq", "n2", "inv", "kk", "kmod", "rk", "rk_step",
                       "bonus", "masks", "mask_step", "cd_psum", "cd", "turned", "t_act", "t_dve",
                       "m_psum", "m_out", "x1", "w_psum", "w_out", "p_psum", "pt_psum", "x_out", "xt_out",
                       "xa_psum", "cy_psum", "xa_out", "cy_out", "u0_psum", "u0_out",
                       "u_psum", "u_out", "s_psum", "s_out", "y_psum", "y_out", "g_psum", "y_cent", "y_sq",
                       "y_var", "y_std", "vb", "z_tok", "zt_psum", "zt_hi", "zt_lo", "vb_used")}
            if ph == "attn":
                norms[ph] = Norm(prev, [(32, xa_hi, xa_lo), (8, xb_hi, xb_lo)])
                at_ = {q: sem(f"attn_{q}") for q in
                       ("k", "v", "q", "z_psum", "z", "abs_exp", "ln", "u", "cs_psum", "log_a", "exp", "att",
                        "o_psum", "o_hi", "o_lo")}
            prev = (h_done[ph], 4)
        norms["final"] = Norm(prev, [], turned=False)

        block = ctx.enter_context(nc.Block())

        @block.sync
        def _(sp):
            for j in range(NT):
                sp.dma_start(h[:, j, :], x[0, j * P:(j + 1) * P, :]).then_inc(x_loaded, 16)

            def slot_free(n):
                if n >= 3:
                    sp.wait_ge(lo_ready, n - 2)

            def load_gate_up(k, e, n):
                dst = w_ring[n % 3]
                return dst

            def dense(n):
                slot_free(n)
                w, half, g = dense_pieces[n]
                load_dense(sp, w_ring[n % 3], w, half, g, w_loaded[n % 3])

            def gate_up(k, e, g, n, slot):
                for a, w in ((0, moe_w_gate), (1, moe_w_up)):
                    src = w[k, e, g * HALF:(g + 1) * HALF, :] if isinstance(e, int) else \
                        w[k, bass.ds(e, 1), g * HALF:(g + 1) * HALF, :].rearrange("o r f -> (o r) f")
                    sp.dma_start(w_ring[slot][:, :, a * F:(a + 1) * F],
                                 src.rearrange("(b p) f -> p b f", p=P)).then_inc(w_loaded[slot], 16)

            def down(k, e, n, slot):
                dst = w_ring[slot][:, :, :].rearrange("p (f a) c -> p f (a c)", f=NF)
                src = moe_w_down[k, e] if isinstance(e, int) else \
                    moe_w_down[k, bass.ds(e, 1)].rearrange("o r c -> (o r) c")
                src = src.rearrange("(f p) c -> p f c", p=P)
                for a in range(NF):
                    sp.dma_start(dst[:, a, :], src[:, a, :]).then_inc(w_loaded[slot], 16)

            def moe_loads(k):
                nb = base[f"moe{k}"]
                order = [(0, "A"), (0, "B"), (1, "A"), (1, "B"), (0, "D")]
                for i, (e, kind) in enumerate(order):
                    slot_free(nb + i)
                    if kind == "D":
                        down(k, e, nb + i, (nb + i) % 3)
                    else:
                        gate_up(k, e, "AB".index(kind), nb + i, (nb + i) % 3)
                with sp.Fori(2, E) as e:
                    n0 = nb - 1
                    for i in range(3):
                        sp.wait_ge(lo_ready, e * 3 + (n0 + i - 2))
                        if i < 2:
                            gate_up(k, e, i, None, (n0 + i) % 3)
                        else:
                            down(k, e - 1, None, (n0 + i) % 3)
                slot_free(nb + 3 * E - 1)
                down(k, E - 1, None, (nb + 3 * E - 1) % 3)

            def rwkv_loads():
                for n in range(3):
                    dense(n)
                sp.wait_ge(*norms["rwkv"].at("scaled", NT))
                sp.dma_start(kk_row[:, :], rw_k_k[0].partition_broadcast(P)).then_inc(rw["rows_loaded"], 16)
                sp.dma_start(ka_row[:, :], rw_k_a[0].partition_broadcast(P)).then_inc(rw["rows_loaded"], 16)
                for n in range(3, 9):
                    dense(n)
                sp.wait_ge(rw["lora2"], 2)
                sp.dma_start(rk_row[:, :], rw_r_k[0].rearrange("h n -> (h n)").partition_broadcast(P)
                             ).then_inc(rw["rk_loaded"], 16)
                for n in range(9, 12):
                    dense(n)
                sp.wait_ge(rw["kmod"], 2)
                for j in range(NT):
                    sp.dma_start(h[:, j, :], x[0, j * P:(j + 1) * P, :]).then_inc(rw["x_again"], 16)
                for n in range(12, 15):
                    dense(n)
                sp.wait_ge(rw["rk"], 2)
                sp.wait_ge(piece_used, 12)
                sp.dma_start(g2a[:, :], rw_g2[0, 0:P, :]).then_inc(rw["late_loaded"], 16)
                sp.dma_start(g2b[:, :], rw_g2[0, P:LG, :]).then_inc(rw["late_loaded"], 16)
                sp.dma_start(lnw_row[:, :], rw_lnx_w[0].partition_broadcast(P)).then_inc(rw["late_loaded"], 16)
                sp.dma_start(lnb_row[:, :], rw_lnx_b[0].partition_broadcast(P)).then_inc(rw["late_loaded"], 16)
                dense(15)

            for ph in PHASES:
                if ph == PHASES[-1]:
                    if "attn" in PHASES[:-1]:
                        sp.wait_ge(piece_used, base["attn"] + 12)
                    else:
                        sp.wait_ge(*norms[ph].at("lo", NC // 2))
                    sp.dma_start(gain_row[:, :], norm_final.partition_broadcast(P)).then_inc(gain_loaded, 16)
                if ph.startswith("moe"):
                    moe_loads(int(ph[3]))
                elif ph == "attn":
                    for n in range(base[ph], base[ph] + 16):
                        dense(n)
                else:
                    rwkv_loads()
            for j in range(NT):
                for a in range(2):
                    sp.wait_ge(final_ready, 2 * j + a + 1)
                    sp.dma_start(out[0, j * P:(j + 1) * P, a * HALF:(a + 1) * HALF],
                                 xs[:, j, a * HALF:(a + 1) * HALF]).then_inc(out_written, 16)
            sp.wait_ge(out_written, 64)

        @block.gpsimd
        def _(pool):
            pool.dma_start(prow[0:16, :], norm_mix.rearrange("l (b p) -> (l b) p", p=P)).then_inc(params_loaded, 16)
            pool.dma_start(prow[16:32, :], norm_ffn.rearrange("l (b p) -> (l b) p", p=P)).then_inc(params_loaded, 16)
            pool.dma_start(prow[32:40, :], norm_kv.rearrange("(b p) -> b p", p=P)).then_inc(params_loaded, 16)
            pool.dma_start(prow[40:88, :], rw_mix.rearrange("o m (b p) -> (o m b) p", p=P)).then_inc(params_loaded, 16)
            if "rwkv" in PHASES:
                for a, w in ((0, rw_w1), (LW, rw_a1), (2 * LW, rw_g1)):
                    pool.dma_start(lora1[:, :, a:a + w.shape[2]], w[0].rearrange("(b p) c -> p b c", p=P)
                                   ).then_inc(rw["lora_loaded"], 16)
                pool.dma_start(w2x[0:LW, :], rw_w2[0]).then_inc(rw["lora_loaded"], 16)
                pool.dma_start(w2x[LW:LW + 1, :], rw_w0).then_inc(rw["lora_loaded"], 16)
                pool.dma_start(a2x[0:LW, :], rw_a2[0]).then_inc(rw["lora_loaded"], 16)
                pool.dma_start(a2x[LW:LW + 1, :], rw_a0).then_inc(rw["lora_loaded"], 16)
            nc.gpsimd.memset(ident[:, :], 0.0).then_inc(ident_ready, 1)
            pool.wait_ge(ident_ready, 1)
            nc.gpsimd.affine_select(out=ident[:, :], in_=ident[:, :], compare_op=ALU.not_equal, fill=1.0,
                                    base=0, pattern=[[-1, P]], channel_multiplier=1).then_inc(ident_ready, 1)
            nc.gpsimd.memset(ones[:, :], 1.0).then_inc(ident_ready, 1)
            pool.wait_ge(ident_ready, 3)
            nc.gpsimd.affine_select(out=causal[:, :], in_=ones[:, :], compare_op=ALU.is_gt, fill=0.0,
                                    base=0, pattern=[[1, P]], channel_multiplier=-1).then_inc(ident_ready, 1)
            nc.gpsimd.affine_select(out=from_s[:, :], in_=ones[:, :], compare_op=ALU.is_ge, fill=0.0,
                                    base=0, pattern=[[-1, P]], channel_multiplier=1).then_inc(ident_ready, 1)
            for k in range(2):
                pool.dma_start(wr[k][:, :, 0:G], moe_w_group[k].rearrange("(b p) g -> p b g", p=P)
                               ).then_inc(router_loaded, 16)
                pool.dma_start(wr[k][:, :, G:NR], moe_w_inner[k].rearrange("(b p) g e -> p b (g e)", p=P)
                               ).then_inc(router_loaded, 16)
                pool.dma_start(br[k][:, 0:G], moe_b_group[k].partition_broadcast(P)).then_inc(router_loaded, 16)
                pool.dma_start(br[k][:, G:NR], moe_b_inner[k].rearrange("g e -> (g e)").partition_broadcast(P)
                               ).then_inc(router_loaded, 16)

            def rwkv_masks():
                steps = [0]

                def link(ins):
                    steps[0] += 1
                    ins.then_inc(rw["mask_step"], 1)
                    pool.wait_ge(rw["mask_step"], steps[0])

                sel = nc.gpsimd.affine_select
                link(sel(out=to_t[:, :], in_=ones[:, :], compare_op=ALU.is_ge, fill=0.0, base=0,
                         pattern=[[1, P]], channel_multiplier=-1))
                link(sel(out=before_t[:, :], in_=causal[:, :], compare_op=ALU.is_ge, fill=0.0, base=0,
                         pattern=[[-CH, P // CH], [0, CH]], channel_multiplier=1))
                link(sel(out=to_t[:, :], in_=to_t[:, :], compare_op=ALU.is_ge, fill=0.0, base=0,
                         pattern=[[-CH, P // CH], [0, CH]], channel_multiplier=1))
                link(sel(out=in_chunk[:, 0:1], in_=ones[:, 0:1], compare_op=ALU.is_ge, fill=0.0, base=CH - 1,
                         pattern=[[0, 1]], channel_multiplier=-1))
                link(sel(out=in_chunk[:, 1:2], in_=ones[:, 0:1], compare_op=ALU.is_ge, fill=0.0, base=-CH,
                         pattern=[[0, 1]], channel_multiplier=1))
                for i in range(LEVELS):
                    m = 1 << i
                    nb = P // (2 * m)
                    link(nc.gpsimd.memset(level[i][:, :], 0.0))
                    v = level[i][:, :].rearrange("p (b c) -> p b c", c=2 * m)[:, :, 0:m]
                    link(nc.gpsimd.memset(v, -1.0))
                    link(sel(out=v, in_=v, compare_op=ALU.is_ge, fill=0.0, base=-m,
                             pattern=[[-2 * m, nb], [0, m]], channel_multiplier=1))
                    link(sel(out=v, in_=v, compare_op=ALU.is_ge, fill=0.0, base=2 * m - 1,
                             pattern=[[2 * m, nb], [0, m]], channel_multiplier=-1))
                    link(sel(out=level[i][:, :], in_=level[i][:, :], compare_op=ALU.not_equal, fill=1.0, base=0,
                             pattern=[[-1, P]], channel_multiplier=1))
                v = level0T[:, :].rearrange("p (b c) -> p b c", c=2)[:, :, 1:2]
                link(nc.gpsimd.tensor_copy(level0T[:, :], ident[:, :]))
                sel(out=v, in_=v, compare_op=ALU.not_equal, fill=-1.0, base=0,
                    pattern=[[-2, P // 2], [0, 1]], channel_multiplier=1).then_inc(rw["masks"], 1)

            def rwkv_phase():
                for a in range(2):
                    c = slice(a * HALF, (a + 1) * HALF)
                    pool.wait_ge(rw["r"], a + 1)
                    pool.wait_ge(rw["kmod"], a + 1)
                    if a:
                        pool.wait_ge(rw["bonus"], a)
                    for j in range(NT):
                        m = nc.gpsimd.tensor_tensor(yb[:, j, :], r_s_[:, j, c], k_s[:, j, c], ALU.mult)
                    m.then_inc(rw["rk_step"], 1)
                    pool.wait_ge(rw["rk_step"], a + 1)
                    if a == 0:
                        pool.wait_ge(rw["rk_loaded"], 16)
                    for j in range(NT):
                        m = nc.gpsimd.tensor_tensor(yb[:, j, :], yb[:, j, :], rk_row[:, c], ALU.mult)
                    m.then_inc(rw["rk"], 1)
                for a in range(2):
                    for j in range(NT):
                        if a + j:
                            pool.wait_ge(rw["vb_used"], 2 * a + j)
                        else:
                            pool.wait_ge(rw["v"], 2)
                            pool.wait_ge(rw["bonus"], 2)
                            pool.wait_ge(piece_used, 12)
                        c = slice(a * HALF, (a + 1) * HALF)
                        nc.gpsimd.tensor_tensor(
                            vb[:, :].rearrange("p (h n) -> p h n", n=HD),
                            v_s[:, j, c].rearrange("p (h n) -> p h n", n=HD),
                            bonus[:, j, a * HH:(a + 1) * HH].unsqueeze(2).broadcast_to([P, HH, HD]), ALU.mult
                            ).then_inc(rw["vb"], 1)

            if "rwkv" in PHASES:
                rwkv_masks()
                rwkv_phase()

            def attn_phase():
                s = at_
                for pr in range(NC):
                    pool.wait_ge(s["exp"], pr + 1)
                    a = att[pr % 3][:, :, :].rearrange("p h (b t) -> p h b t", t=P)[:, :, 0:3:2, :]
                    for hh in range(2):
                        m = nc.gpsimd.tensor_tensor(a[:, hh], a[:, hh],
                                                    causal[:, :].unsqueeze(1).broadcast_to([P, 2, P]), ALU.mult)
                    m.then_inc(s["att"], 1)

            for ph in PHASES:
                if ph == "attn":
                    attn_phase()

        @block.scalar
        def _(act):
            def split_hi(n):
                act.wait_ge(w_loaded[n % 3], 32 * (n // 3 + 1))
                if n >= 3:
                    act.wait_ge(piece_used, n - 2)
                nc.scalar.activation(whi[n % 3][:, :, :], w_ring[n % 3][:, :, :], ACT.Copy).then_inc(hi_ready, 1)

            def split_next(m):
                if m + 3 < TOTAL:
                    split_hi(m + 3)

            def norm_stats(nm):
                act.wait_ge(*nm.h_ready)
                for j in range(NT):
                    nc.scalar.activation(PS[:, 4 + 2 * j:6 + 2 * j, :],
                                         h[:, j, :].rearrange("p (a c) -> p a c", a=2), ACT.Square,
                                         accum_out=ss[:, j:j + 1]).then_inc(norm_sems["squares"], 1)
                act.wait_ge(*nm.at("recip", 1))
                nc.scalar.activation(rstd[:, :], rec[:, :], ACT.Sqrt).then_inc(norm_sems["rstd"], 1)

            def norm(nm):
                norm_stats(nm)
                for bank in range(NC // 2):
                    act.wait_ge(*nm.at("turned", bank + 1))
                    for col, hi, lo in nm.gains:
                        for b in (2 * bank, 2 * bank + 1):
                            m = nc.scalar.activation(hi[:, b, :], PS[:, 4 + bank, (b % 2) * T:(b % 2 + 1) * T],
                                                     ACT.Copy, scale=cols[:, col + b:col + b + 1])
                    m.then_inc(norm_sems["hi"], 1)

            def moe_phase(k):
                s, nb = moe_sems, base[f"moe{k}"]
                if k == 0 or "moe0" not in PHASES:
                    act.wait_ge(router_loaded, 16 * 8)
                nc.scalar.activation(wr_hi[:, :, :], wr[k][:, :, :], ACT.Copy).then_inc(s["wr_hi"], 1)
                norm(norms[f"moe{k}"])
                act.wait_ge(s["gs"], k * PER["gs"] + 1)
                nc.scalar.activation(r_eg[:, :, :], r_gs[:, :, :], ACT.Exp).then_inc(s["eg"], 1)
                act.wait_ge(s["m2"], k * PER["m2"] + 1)
                nc.scalar.activation(r_s[:, 4, :], r_s[:, 3, :], ACT.Exp).then_inc(s["e2"], 1)

                def silu(e, b_piece):
                    act.wait_ge(piece_used, b_piece + 1)
                    for j in range(NT):
                        nc.scalar.activation(silu_g[:, j, :], PS[:, 4 + j, 0:F], ACT.Silu).then_inc(s["silu"], 1)

                def h_hi(e):
                    act.wait_ge(s["hT_psum"], e + k * PER["hT_psum"])
                    nc.scalar.activation(hT_hi[:, :, :], PS[:, 6, :].rearrange("p (f t) -> p f t", f=NF),
                                         ACT.Copy).then_inc(s["hT_hi"], 1)

                split_next(nb)
                silu(0, nb + 1)
                split_next(nb + 1)

                def step(e, n0, known):
                    h_hi(e)
                    for i in range(3):
                        if i == 1:
                            act.wait_ge(piece_used, n0 + 2)
                            act.wait_ge(s["hact"], e * 2 + k * PER["hact"])
                            for j in range(NT):
                                nc.scalar.activation(silu_g[:, j, :], PS[:, 4 + j, 0:F], ACT.Silu
                                                     ).then_inc(s["silu"], 1)
                        slot = (nb - 1 + i) % 3
                        if known:
                            split_next(n0 + i)
                        else:
                            act.wait_ge(w_loaded[slot], (e + (nb - 1 + i + 3) // 3 + 1) * 32)
                            act.wait_ge(piece_used, n0 + (i + 1))
                            nc.scalar.activation(whi[slot][:, :, :], w_ring[slot][:, :, :], ACT.Copy
                                                 ).then_inc(hi_ready, 1)

                step(1, nb + 2, True)
                with act.Fori(2, E - 1) as e:
                    step(e, e * 3 + (nb - 1), False)
                step(E - 1, nb - 1 + 3 * (E - 1), True)
                h_hi(E)
                split_next(nb + 3 * E - 1)

            def rwkv_phase():
                nm = norms["rwkv"]
                norm_stats(nm)
                act.wait_ge(cols_ready, 1)
                for bank in range(2):
                    act.wait_ge(*nm.at("turned", bank + 1))
                    for b in (2 * bank, 2 * bank + 1):
                        m = nc.scalar.activation(hnT[:, b, :], PS[:, 4 + bank, (b % 2) * T:(b % 2 + 1) * T],
                                                 ACT.Copy, scale=cols[:, b:b + 1])
                    m.then_inc(rw["hn_act"], 1)

                def x_hi(i, dst, n):
                    act.wait_ge(rw["mixed"], i + 1)
                    for g in range(2):
                        nc.scalar.activation(dst[:, 4 * g:4 * g + 4, :], mixed_[i][:, 4 * g:4 * g + 4, :], ACT.Copy
                                             ).then_inc(rw["x_hi"], 1)

                def out(dst, n, bank0, name, piece):
                    act.wait_ge(piece_used, piece + 1)
                    nc.scalar.activation(dst[:, :, n * HALF:(n + 1) * HALF], PS[:, bank0:bank0 + 2, :], ACT.Copy
                                         ).then_inc(rw[name], 1)

                x_hi(0, xa_hi, 0)
                split_next(0)
                split_next(1)
                out(k_s, 0, 0, "k", 1)
                split_next(2)
                split_next(3)
                out(k_s, 1, 2, "k", 3)
                act.wait_ge(rw["lora1"], 1)
                nc.scalar.activation(zw[0:LW, :], PS[0:LW, 4, 0:T], ACT.Tanh).then_inc(rw["z"], 1)
                act.wait_ge(rw["lora1"], 2)
                nc.scalar.activation(za[0:LW, :], PS[0:LW, 5, 0:T], ACT.Copy).then_inc(rw["z"], 1)
                act.wait_ge(rw["lora1"], 3)
                nc.scalar.activation(zg[:, :], PS[:, 6, 0:T], ACT.Sigmoid).then_inc(rw["z"], 1)
                nc.scalar.activation(zg2[:, :], PS[0:LG - P, 7, 0:T], ACT.Sigmoid).then_inc(rw["z"], 1)
                x_hi(4, xb_hi, 1)
                for i, (dst, name) in enumerate(((sig, "sig"), (a_s, "a"))):
                    act.wait_ge(rw["lora2"], i + 1)
                    for j in range(NT):
                        nc.scalar.activation(dst[:, j, :].rearrange("p (a c) -> p a c", a=2),
                                             PS[:, 4 * i + 2 * j:4 * i + 2 * j + 2, :], ACT.Sigmoid
                                             ).then_inc(rw[name], 1)
                x_hi(5, xa_hi, 2)
                for a in range(2):
                    act.wait_ge(rw["kk0"], a + 1)
                    if a:
                        act.wait_ge(rw["n2"], a)
                    nc.scalar.activation(tmp[:, :, :], kk[:, :, a * HALF:(a + 1) * HALF], ACT.Square
                                         ).then_inc(rw["sq"], 1)
                    act.wait_ge(rw["n2"], a + 1)
                    nc.scalar.activation(n2i[:, :, :], n2[:, :, :], ACT.Sqrt).then_inc(rw["inv"], 1)
                split_next(4)
                split_next(5)
                out(r_s_, 0, 0, "r", 5)
                split_next(6)
                split_next(7)
                out(r_s_, 1, 2, "r", 7)
                split_next(8)

                def decays(a):
                    act.wait_ge(rw["cum"], a + 1)
                    for i, (dst, bank, sc) in enumerate(((e0, 4, -LOG_DECAY), (e1, 4, LOG_DECAY), (e0, 6, -LOG_DECAY))):
                        if i == 2:
                            act.wait_ge(rw["decay_used"], 3 * a + 1)
                        if i < 2 and a:
                            act.wait_ge(rw["decay_used"], 3 * a)
                        nc.scalar.activation(dst[:, :, :], PS[:, bank:bank + 2, :], ACT.Exp, scale=sc
                                             ).then_inc(rw["decay"], 1)

                decays(0)
                out(v_s, 0, 0, "v", 9)
                out(v_s, 1, 2, "v", 11)
                decays(1)
                act.wait_ge(rw["cd_psum"], 1)
                nc.scalar.activation(chunk_decay[:, :, :].rearrange("p b c -> p (b c)"), PS[:, 0, 0:4 * NC], ACT.Exp,
                                     scale=-LOG_DECAY).then_inc(rw["cd"], 1)

                for a in range(2):
                    act.wait_ge(rw["turned"], 4 * a + 1)
                    nc.scalar.activation(AT[:, :, :].rearrange("p (a b) t -> p a (b t)", a=2), PS[:, 0:2, :],
                                         ACT.Copy).then_inc(rw["t_act"], 1)
                    act.wait_ge(rw["turned"], 4 * a + 3)
                    nc.scalar.activation(KT[:, :, :].rearrange("p (a b) t -> p a (b t)", a=2), PS[:, 4:6, :],
                                         ACT.Copy).then_inc(rw["t_act"], 1)
                    for q in (2 * a, 2 * a + 1):
                        for l in range(1, LEVELS):
                            for j in range(NT):
                                if l < LEVELS - 1:
                                    act.wait_ge(rw["p_psum"], 8 * q + 2 * (l - 1) + j + 1)
                                    nc.scalar.activation(X[j][:, :, :].rearrange("p h s -> p (h s)"),
                                                         PS[:, 2 + j, :], ACT.Copy).then_inc(rw["x_out"], 1)
                                act.wait_ge(rw["pt_psum"], 10 * q + 2 * (l - 1) + j + 1)
                                nc.scalar.activation(XT[j][:, :, :].rearrange("p h s -> p (h s)"),
                                                     PS[:, 4 + j, :], ACT.Copy).then_inc(rw["xt_out"], 1)
                        for j in range(NT):
                            act.wait_ge(rw["cy_psum"], 2 * q + j + 1)
                            nc.scalar.activation(W_[j][:, 0:2, :].rearrange("p a s -> p (a s)"), PS[:, 6 + j, 0:256],
                                                 ACT.Copy)
                            nc.scalar.activation(Y0[:, j, q % 2::2, :],
                                                 PS[:, 6 + j, 256:512].rearrange("p (h n) -> p h n", n=HD),
                                                 ACT.Copy).then_inc(rw["cy_out"], 1)
                            act.wait_ge(rw["xa_psum"], 2 * q + j + 1)
                            o = HD * (q % 2)
                            nc.scalar.activation(XaT[j][o:o + HD, :, :].rearrange("p a s -> p (a s)"),
                                                 PS[o:o + HD, 2 + j, :], ACT.Copy).then_inc(rw["xa_out"], 1)
                    for j in range(NT):
                        i = 2 * a + j
                        act.wait_ge(rw["y_cent"], i + 1)
                        nc.scalar.activation(y_sq[:, :], yb[:, j, :], ACT.Square).then_inc(rw["y_sq"], 1)
                        act.wait_ge(rw["y_var"], i + 1)
                        nc.scalar.activation(y_m[:, 3, :], y_m[:, 2, :], ACT.Sqrt).then_inc(rw["y_std"], 1)
                for i in range(4):
                    act.wait_ge(rw["zt_psum"], i + 1)
                    a, j = i // 2, i % 2
                    nc.scalar.activation(xa_hi[:, 4 * a:4 * a + 4, j * P:(j + 1) * P],
                                         PS[:, 4 + i, :].rearrange("p (b t) -> p b t", t=P), ACT.Copy
                                         ).then_inc(rw["zt_hi"], 1)
                for m in range(9, 16):
                    split_next(m)

            def attn_phase():
                s, nb = at_, base["attn"]
                norm(norms["attn"])
                for m in range(12):
                    if m in (1, 3):
                        act.wait_ge(piece_used, nb + m + 1)
                        n = m // 2
                        nc.scalar.activation(kT[:, 4 * n:4 * n + 4, :].rearrange("p (a b) t -> p a (b t)", a=2),
                                             PS[:, 2 * n:2 * n + 2, :], ACT.Copy).then_inc(s["k"], 1)
                    split_next(nb + m)

                def softplus_tail(pr):
                    act.wait_ge(s["z"], pr + 1)
                    nc.scalar.activation(z_abs[:, :, :], z_sb[pr % 3][:, :, :], ACT.Abs).then_inc(s["abs_exp"], 1)
                    act.wait_ge(s["abs_exp"], 2 * pr + 1)
                    nc.scalar.activation(z_exp[:, :, :], z_abs[:, :, :], ACT.Exp, scale=-1.0
                                         ).then_inc(s["abs_exp"], 1)
                    act.wait_ge(s["abs_exp"], 2 * pr + 2)
                    if pr >= 2:
                        act.wait_ge(s["u"], pr - 1)
                    nc.scalar.activation(z_ln[pr % 2][:, :, :], z_exp[:, :, :], ACT.Ln, bias=1.0
                                         ).then_inc(s["ln"], 1)

                def att_exp(pr):
                    act.wait_ge(s["log_a"], pr + 1)
                    if pr >= 3:
                        act.wait_ge(s["o_psum"], pr - 2)
                    nc.scalar.activation(att[pr % 3][:, :, :], log_a[pr % 2][:, :, :], ACT.Exp
                                         ).then_inc(s["exp"], 1)

                def o_hi(pr):
                    act.wait_ge(s["o_psum"], pr + 1)
                    nc.scalar.activation(xa_hi[:, pr, :], PS[:, 6 + pr % 2, 0:T], ACT.Copy).then_inc(s["o_hi"], 1)

                softplus_tail(0)
                for i in range(NC):
                    if i + 1 < NC:
                        softplus_tail(i + 1)
                    att_exp(i)
                    if i >= 1:
                        o_hi(i - 1)
                o_hi(NC - 1)
                for m in range(12, 16):
                    split_next(nb + m)

            for n in range(3):
                split_hi(n)
            for ph in PHASES:
                if ph.startswith("moe"):
                    moe_phase(int(ph[3]))
                if ph == "attn":
                    attn_phase()
                if ph == "rwkv":
                    rwkv_phase()
            norm_stats(norms["final"])

        @block.vector
        def _(dve):
            steps = [0]

            def link(ins):
                steps[0] += 1
                ins.then_inc(dve_step, 1)
                dve.wait_ge(dve_step, steps[0])

            def split_lo(n):
                dve.wait_ge(hi_ready, n + 1)
                nc.vector.tensor_tensor(wlo[n % 3][:, :, :], w_ring[n % 3][:, :, :], whi[n % 3][:, :, :].bitcast(f32),
                                        ALU.subtract).then_inc(lo_ready, 1)

            def split_next(m):
                if m + 3 < TOTAL:
                    split_lo(m + 3)

            def norm_scale(nm):
                dve.wait_ge(*nm.at("squares", NT))
                link(nc.vector.tensor_scalar(ms[:, :], ss[:, :], 1.0 / C, RMS_EPS, ALU.mult, ALU.add))
                nc.vector.reciprocal(rec[:, :], ms[:, :]).then_inc(norm_sems["recip"], 1)
                dve.wait_ge(*nm.at("rstd", 1))
                for j in range(NT):
                    nc.vector.tensor_scalar(xs[:, j, :], h[:, j, :], rstd[:, j:j + 1], None, ALU.mult
                                            ).then_inc(norm_sems["scaled"], 1)

            def norm(nm):
                norm_scale(nm)
                for bank in range(NC // 2):
                    dve.wait_ge(*nm.at("hi", bank + 1))
                    for col, hi, lo in nm.gains:
                        for b in (2 * bank, 2 * bank + 1):
                            m = nc.vector.scalar_tensor_tensor(
                                out=lo[:, b, :], in0=PS[:, 4 + bank, (b % 2) * T:(b % 2 + 1) * T],
                                scalar=cols[:, col + b:col + b + 1], in1=hi[:, b, :].bitcast(f32),
                                op0=ALU.mult, op1=ALU.subtract)
                    m.then_inc(norm_sems["lo"], 1)

            def residual(ph, m, halves=(0, 1)):
                dve.wait_ge(piece_used, m + 1)
                for j in range(NT):
                    for a in halves:
                        sl = h[:, j, a * HALF:(a + 1) * HALF]
                        nc.vector.tensor_tensor(sl, PS[:, 2 * j + a, :], sl, ALU.add).then_inc(h_done[ph], 1)

            def moe_phase(k):
                s, nb = moe_sems, base[f"moe{k}"]
                dve.wait_ge(s["wr_hi"], k * PER["wr_hi"] + 1)
                nc.vector.tensor_tensor(wr_lo[:, :, :], wr[k][:, :, :], wr_hi[:, :, :].bitcast(f32), ALU.subtract
                                        ).then_inc(s["wr_lo"], 1)
                for i in range(EG):
                    last = nc.vector.memset(rev[:, i:i + 1], float(EG - i))
                link(last)
                norm(norms[f"moe{k}"])

                def bc(v, n):
                    return v.unsqueeze(2).broadcast_to([P, NT, n])

                def first_of(eq, out_):
                    link(nc.vector.tensor_tensor(eq, eq, rev[:, :].unsqueeze(1).broadcast_to([P, NT, EG]), ALU.mult))
                    link(nc.vector.tensor_reduce(r_s[:, 9, :], eq, AX.X, ALU.max))
                    link(nc.vector.tensor_tensor(out_, eq, bc(r_s[:, 9, :], EG), ALU.is_equal))

                dve.wait_ge(s["logits"], k * PER["logits"] + 1)
                link(nc.vector.tensor_tensor(lg[:, :, :], PS[:, 0, 0:NT * NR].rearrange("p (j r) -> p j r", j=NT),
                                             br[k][:, :].unsqueeze(1).broadcast_to([P, NT, NR]), ALU.add))
                link(nc.vector.tensor_reduce(r_s[:, 0, :], lg[:, :, 0:G], AX.X, ALU.max))
                nc.vector.tensor_tensor(r_gs[:, :, :], lg[:, :, 0:G], bc(r_s[:, 0, :], G), ALU.subtract
                                        ).then_inc(s["gs"], 1)
                dve.wait_ge(s["gs"], k * PER["gs"] + 1)
                link(nc.vector.tensor_scalar(r_eq[:, :, :], r_gs[:, :, :], 0.0, None, ALU.is_equal))
                first_of(r_eq[:, :, :], r_fg[:, :, :])
                link(nc.vector.tensor_tensor(
                    r_ilm[:, :, :, :], lg[:, :, G:NR].rearrange("p j (g e) -> p j g e", g=G),
                    r_fg[:, :, :].unsqueeze(3).broadcast_to([P, NT, G, EG]), ALU.mult))
                link(nc.vector.tensor_reduce(r_il[:, :, :], r_ilm[:, :, :, :].rearrange("p j g e -> p j e g"),
                                             AX.X, ALU.add))
                link(nc.vector.tensor_reduce(r_s[:, 2, :], r_il[:, :, :], AX.X, ALU.max))
                link(nc.vector.tensor_tensor(r_d[:, :, :], r_il[:, :, :], bc(r_s[:, 2, :], EG), ALU.subtract))
                link(nc.vector.tensor_scalar(r_f1[:, :, :], r_d[:, :, :], 0.0, None, ALU.is_equal))
                first_of(r_f1[:, :, :], r_f1[:, :, :])
                link(nc.vector.scalar_tensor_tensor(out=r_d2[:, :, :], in0=r_f1[:, :, :], scalar=-3.0e38,
                                                    in1=r_d[:, :, :], op0=ALU.mult, op1=ALU.add))
                nc.vector.tensor_reduce(r_s[:, 3, :], r_d2[:, :, :], AX.X, ALU.max).then_inc(s["m2"], 1)
                dve.wait_ge(s["m2"], k * PER["m2"] + 1)
                link(nc.vector.tensor_tensor(r_f2[:, :, :], r_d2[:, :, :], bc(r_s[:, 3, :], EG), ALU.is_equal))
                first_of(r_f2[:, :, :], r_f2[:, :, :])
                dve.wait_ge(s["eg"], k * PER["eg"] + 1)
                link(nc.vector.tensor_reduce(r_s[:, 1, :], r_eg[:, :, :], AX.X, ALU.add))
                dve.wait_ge(s["e2"], k * PER["e2"] + 1)
                link(nc.vector.tensor_scalar(r_s[:, 5, :], r_s[:, 4, :], 1.0, None, ALU.add))
                link(nc.vector.tensor_tensor(r_s[:, 6, :], r_s[:, 5, :], r_s[:, 1, :], ALU.mult))
                link(nc.vector.reciprocal(r_s[:, 7, :], r_s[:, 6, :]))
                link(nc.vector.tensor_tensor(r_s[:, 8, :], r_s[:, 7, :], r_s[:, 4, :], ALU.mult))
                link(nc.vector.tensor_tensor(r_f1[:, :, :], r_f1[:, :, :], bc(r_s[:, 7, :], EG), ALU.mult))
                link(nc.vector.tensor_tensor(r_f2[:, :, :], r_f2[:, :, :], bc(r_s[:, 8, :], EG), ALU.mult))
                link(nc.vector.tensor_tensor(r_f1[:, :, :], r_f1[:, :, :], r_f2[:, :, :], ALU.add))
                nc.vector.tensor_tensor(gates[:, :, :].rearrange("p j (g e) -> p j g e", g=G),
                                        r_fg[:, :, :].unsqueeze(3).broadcast_to([P, NT, G, EG]),
                                        r_f1[:, :, :].unsqueeze(2).broadcast_to([P, NT, G, EG]), ALU.mult
                                        ).then_inc(s["gates"], 1)
                dve.wait_ge(s["gates"], k * PER["gates"] + 1)

                def gated(e):
                    for j in range(NT):
                        dve.wait_ge(s["silu"], e * 2 + k * PER["silu"] + (j + 1))
                        g = gates[:, j, e:e + 1] if isinstance(e, int) else gates[:, j, bass.ds(e, 1)]
                        nc.vector.scalar_tensor_tensor(out=hact[:, j, :], in0=silu_g[:, j, :], scalar=g,
                                                       in1=PS[:, 4 + j, F:2 * F], op0=ALU.mult, op1=ALU.mult
                                                       ).then_inc(s["hact"], 1)

                def h_lo(e):
                    dve.wait_ge(s["hT_hi"], e + k * PER["hT_hi"])
                    nc.vector.tensor_tensor(hT_lo[:, :, :], PS[:, 6, :].rearrange("p (f t) -> p f t", f=NF),
                                            hT_hi[:, :, :].bitcast(f32), ALU.subtract).then_inc(s["hT_lo"], 1)

                split_next(nb)
                gated(0)
                split_next(nb + 1)

                def step(e, n0, known):
                    h_lo(e)
                    for i in range(3):
                        if i == 1:
                            gated(e)
                        slot = (nb - 1 + i) % 3
                        if known:
                            split_next(n0 + i)
                        else:
                            dve.wait_ge(hi_ready, n0 + (i + 4))
                            nc.vector.tensor_tensor(wlo[slot][:, :, :], w_ring[slot][:, :, :],
                                                    whi[slot][:, :, :].bitcast(f32), ALU.subtract
                                                    ).then_inc(lo_ready, 1)

                step(1, nb + 2, True)
                with dve.Fori(2, E - 1) as e:
                    step(e, e * 3 + (nb - 1), False)
                step(E - 1, nb - 1 + 3 * (E - 1), True)
                h_lo(E)
                residual(f"moe{k}", nb + 3 * E - 1)
                split_next(nb + 3 * E - 1)

            def rwkv_phase():
                nm = norms["rwkv"]
                nc.vector.memset(zw[LW:LW + 1, :], 1.0)
                nc.vector.memset(za[LW:LW + 1, :], 1.0).then_inc(rw["zones"], 1)
                norm_scale(nm)
                for bank in (2, 3):
                    dve.wait_ge(*nm.at("turned", bank + 1))
                    for b in (2 * bank, 2 * bank + 1):
                        m = nc.vector.tensor_scalar(hnT[:, b, :], PS[:, 4 + bank, (b % 2) * T:(b % 2 + 1) * T],
                                                    cols[:, b:b + 1], None, ALU.mult)
                    m.then_inc(rw["hn_dve"], 1)
                dve.wait_ge(rw["hn_act"], 2)
                dve.wait_ge(rw["hn_dve"], 2)
                nc.vector.tensor_scalar(dxT[:, :, 0:1], hnT[:, :, 0:1], -1.0, None, ALU.mult)
                link(nc.vector.tensor_tensor(dxT[:, :, 1:T], hnT[:, :, 0:T - 1], hnT[:, :, 1:T], ALU.subtract))

                def mix(i):
                    for b in range(NC):
                        col = 40 + NC * MIX_ROW[i] + b
                        m = nc.vector.scalar_tensor_tensor(out=mixed_[i][:, b, :], in0=dxT[:, b, :],
                                                           scalar=cols[:, col:col + 1], in1=hnT[:, b, :],
                                                           op0=ALU.mult, op1=ALU.add)
                    m.then_inc(rw["mixed"], 1)

                def x_lo(i, dst_hi, dst, n):
                    for g in range(2):
                        dve.wait_ge(rw["x_hi"], 2 * n + g + 1)
                        b = slice(4 * g, 4 * g + 4)
                        nc.vector.tensor_tensor(dst[:, b, :], mixed_[i][:, b, :], dst_hi[:, b, :].bitcast(f32),
                                                ALU.subtract).then_inc(rw["x_lo"], 1)

                mix(0)
                x_lo(0, xa_hi, xa_lo, 0)
                mix(1)
                mix(2)
                dve.wait_ge(rw["x_lo"], 2)
                mix(3)
                for m in range(4):
                    split_next(m)
                dve.wait_ge(rw["lora1"], 1)
                mix(4)
                x_lo(4, xb_hi, xb_lo, 1)
                dve.wait_ge(rw["lora1"], 2)
                mix(5)
                x_lo(5, xa_hi, xa_lo, 2)

                def half(t, a):
                    return t[:, :, a * HALF:(a + 1) * HALF]

                def row(t, a):
                    return t[:, a * HALF:(a + 1) * HALF].unsqueeze(1).broadcast_to([P, NT, HALF])

                dve.wait_ge(rw["rows_loaded"], 32)
                dve.wait_ge(rw["lora1"], 3)
                for a in range(2):
                    dve.wait_ge(rw["k"], a + 1)
                    nc.vector.tensor_tensor(half(kk, a), half(k_s, a), row(kk_row, a), ALU.mult
                                            ).then_inc(rw["kk0"], 1)
                for a in range(2):
                    dve.wait_ge(rw["sq"], a + 1)
                    if a:
                        dve.wait_ge(rw["inv"], a)
                    link(nc.vector.tensor_reduce(n2[:, :, :], tmp[:, :, :].rearrange("p j (h n) -> p j h n", n=HD),
                                                 AX.X, ALU.add))
                    link(nc.vector.tensor_scalar(n2[:, :, :], n2[:, :, :], 1e-24, None, ALU.max))
                    nc.vector.reciprocal(n2[:, :, :], n2[:, :, :]).then_inc(rw["n2"], 1)
                    dve.wait_ge(rw["inv"], a + 1)
                    for j in range(NT):
                        v = kk[:, j, a * HALF:(a + 1) * HALF].rearrange("p (h n) -> p h n", n=HD)
                        m = nc.vector.tensor_tensor(v, v, n2i[:, j, :].unsqueeze(2).broadcast_to([P, HH, HD]),
                                                    ALU.mult)
                    link(m)
                split_next(4)
                split_next(5)
                dve.wait_ge(rw["a"], NT)
                for a in range(2):
                    if a:
                        dve.wait_ge(rw["kmod"], a)
                    link(nc.vector.scalar_tensor_tensor(out=tmp[:, :, :], in0=half(a_s, a), scalar=-1.0,
                                                        in1=row(ka_row, a), op0=ALU.add, op1=ALU.mult))
                    nc.vector.scalar_tensor_tensor(out=half(k_s, a), in0=tmp[:, :, :], scalar=1.0, in1=half(k_s, a),
                                                   op0=ALU.add, op1=ALU.mult).then_inc(rw["kmod"], 1)
                    link(nc.vector.tensor_tensor(half(a_s, a), half(kk, a), half(a_s, a), ALU.mult))
                split_next(6)
                split_next(7)
                split_next(8)
                for a in range(2):
                    dve.wait_ge(rw["rk"], a + 1)
                    nc.vector.tensor_reduce(bonus[:, :, a * HH:(a + 1) * HH],
                                            yb[:, :, :].rearrange("p j (h n) -> p j h n", n=HD), AX.X, ALU.add
                                            ).then_inc(rw["bonus"], 1)
                    dve.wait_ge(rw["decay"], 3 * a + 1)
                    nc.vector.tensor_tensor(half(r_s_, a), half(r_s_, a), e0[:, :, :], ALU.mult
                                            ).then_inc(rw["decay_used"], 1)
                    dve.wait_ge(rw["decay"], 3 * a + 2)
                    nc.vector.tensor_tensor(half(a_s, a), half(a_s, a), e1[:, :, :], ALU.mult)
                    nc.vector.tensor_tensor(half(k_s, a), half(k_s, a), e1[:, :, :], ALU.mult
                                            ).then_inc(rw["decay_used"], 1)
                    dve.wait_ge(rw["decay"], 3 * a + 3)
                    nc.vector.scalar_tensor_tensor(out=half(kk, a), in0=half(kk, a), scalar=-1.0, in1=e0[:, :, :],
                                                   op0=ALU.mult, op1=ALU.mult).then_inc(rw["decay_used"], 1)

                def by_head(m):
                    return m[:, :].unsqueeze(1).broadcast_to([P, 4, P])

                def heads(bank):
                    return PS[:, bank, :].rearrange("p (h s) -> p h s", s=P)

                dve.wait_ge(rw["masks"], 1)
                for a in range(2):
                    dve.wait_ge(rw["turned"], 4 * a + 2)
                    nc.vector.tensor_copy(BT[:, :, :].rearrange("p (a b) t -> p a (b t)", a=2), PS[:, 2:4, :]
                                          ).then_inc(rw["t_dve"], 1)
                    dve.wait_ge(rw["turned"], 4 * a + 4)
                    nc.vector.tensor_copy(RT[:, :, :].rearrange("p (a b) t -> p a (b t)", a=2), PS[:, 6:8, :]
                                          ).then_inc(rw["t_dve"], 1)
                    for q in (2 * a, 2 * a + 1):
                        for j in range(NT):
                            dve.wait_ge(rw["m_psum"], 8 * q + 4 * j + 1)
                            link(nc.vector.scalar_tensor_tensor(out=NT_[j][:, :, :], in0=heads(4 * j), scalar=-1.0,
                                                                in1=by_head(before_t), op0=ALU.mult, op1=ALU.mult))
                            nc.vector.tensor_tensor(NT_[j][:, :, :], NT_[j][:, :, :], by_head(ident), ALU.add
                                                    ).then_inc(rw["m_out"], 1)
                            for i, (dst, mask) in enumerate(((AakT[j], before_t), (ArbT[q % 2][j], to_t),
                                                             (ArkT[j], to_t))):
                                dve.wait_ge(rw["m_psum"], 8 * q + 4 * j + 2 + i)
                                nc.vector.tensor_tensor(dst[:, :, :], heads(4 * j + 1 + i), by_head(mask), ALU.mult
                                                        ).then_inc(rw["m_out"], 1)
                            dve.wait_ge(rw["m_out"], 8 * q + 4 * j + 1)
                            nc.vector.tensor_tensor(XT[j][:, :, :], NT_[j][:, :, :], by_head(level0T), ALU.mult
                                                    ).then_inc(rw["x1"], 1)
                        for l in range(LEVELS):
                            for j in range(NT):
                                dve.wait_ge(rw["w_psum"], 12 * q + 2 * l + j + 1)
                                dst = X[j] if l == 0 else W_[j]
                                nc.vector.tensor_tensor(dst[:, :, :], heads(j), by_head(level[l]), ALU.mult
                                                        ).then_inc(rw["w_out"], 1)
                        for j in range(NT):
                            dve.wait_ge(rw["u0_psum"], 2 * q + j + 1)
                            nc.vector.tensor_copy(U[:, j, q % 2::2, :],
                                                  PS[:, 6 + j, 0:256].rearrange("p (h n) -> p h n", n=HD)
                                                  ).then_inc(rw["u0_out"], 1)
                    if a == 0:
                        link(nc.vector.memset(S[0][:, :, :], 0.0))
                    dve.wait_ge(rw["cd"], 1)
                    for c in range(4):
                        j, p0 = c // 2, CH * (c % 2)
                        if c:
                            dve.wait_ge(rw["u_psum"], 3 * a + c)
                            for par, bank in ((0, 0), (1, 7)):
                                u = U[p0:p0 + CH, j, par::2, :]
                                m = nc.vector.tensor_tensor(
                                    u, u, PS[p0:p0 + CH, bank, 0:256].rearrange("p (h n) -> p h n", n=HD), ALU.add)
                            m.then_inc(rw["u_out"], 1)
                        if c < 3:
                            dve.wait_ge(rw["s_psum"], 3 * a + c + 1)
                            src = PS[:, 1, 0:256].rearrange("p (b n) -> p b n", n=HD)
                            if c:
                                link(nc.vector.tensor_tensor(S[c + 1][:, :, :], S[c][:, :, :], src, ALU.add))
                                src = S[c + 1][:, :, :]
                            nc.vector.tensor_tensor(
                                S[c + 1][:, :, :], src,
                                chunk_decay[:, 4 * a:4 * a + 4, c:c + 1].broadcast_to([P, 4, HD]), ALU.mult
                                ).then_inc(rw["s_out"], 1)
                    dve.wait_ge(rw["late_loaded"], 64)
                    for j in range(NT):
                        i = 2 * a + j
                        y = yb[:, j, :]
                        y3 = y.rearrange("p (h n) -> p h n", n=HD)
                        dve.wait_ge(rw["y_psum"], i + 1)
                        for par in range(2):
                            m = nc.vector.tensor_tensor(
                                y3[:, par::2, :], PS[:, 2 + 2 * par + j, 0:256].rearrange("p (h n) -> p h n", n=HD),
                                Y0[:, j, par::2, :], ALU.add)
                        link(m)
                        link(nc.vector.tensor_reduce(y_m[:, 0, :], y3, AX.X, ALU.add))
                        link(nc.vector.tensor_scalar(y_m[:, 1, :], y_m[:, 0, :], 1.0 / HD, None, ALU.mult))
                        nc.vector.tensor_tensor(y3, y3, y_m[:, 1, :].unsqueeze(2).broadcast_to([P, HH, HD]),
                                                ALU.subtract).then_inc(rw["y_cent"], 1)
                        dve.wait_ge(rw["y_sq"], i + 1)
                        link(nc.vector.tensor_reduce(y_m[:, 0, :], y_sq[:, :].rearrange("p (h n) -> p h n", n=HD),
                                                     AX.X, ALU.add))
                        link(nc.vector.tensor_scalar(y_m[:, 1, :], y_m[:, 0, :], 1.0 / HD, GN_EPS, ALU.mult, ALU.add))
                        nc.vector.reciprocal(y_m[:, 2, :], y_m[:, 1, :]).then_inc(rw["y_var"], 1)
                        dve.wait_ge(rw["y_std"], i + 1)
                        link(nc.vector.tensor_tensor(y3, y3, y_m[:, 3, :].unsqueeze(2).broadcast_to([P, HH, HD]),
                                                     ALU.mult))
                        link(nc.vector.tensor_tensor(y, y, lnw_row[:, a * HALF:(a + 1) * HALF], ALU.mult))
                        link(nc.vector.tensor_tensor(y, y, lnb_row[:, a * HALF:(a + 1) * HALF], ALU.add))
                        dve.wait_ge(rw["vb"], i + 1)
                        nc.vector.tensor_tensor(y, y, vb[:, :], ALU.add).then_inc(rw["vb_used"], 1)
                        dve.wait_ge(rw["vb_used"], i + 1)
                        dve.wait_ge(rw["g_psum"], i + 1)
                        nc.vector.tensor_tensor(z_tok[:, j, a * HALF:(a + 1) * HALF], y, PS[:, 6 + j, :], ALU.mult
                                                ).then_inc(rw["z_tok"], 1)
                for i in range(4):
                    dve.wait_ge(rw["zt_hi"], i + 1)
                    a, j = i // 2, i % 2
                    dst = (slice(None), slice(4 * a, 4 * a + 4), slice(j * P, (j + 1) * P))
                    nc.vector.tensor_tensor(xa_lo[dst], PS[:, 4 + i, :].rearrange("p (b t) -> p b t", t=P),
                                            xa_hi[dst].bitcast(f32), ALU.subtract).then_inc(rw["zt_lo"], 1)
                for m in range(9, 12):
                    split_next(m)
                dve.wait_ge(rw["x_again"], 32)
                for m in range(12, 16):
                    if m % 2:
                        residual("rwkv", m, (m // 2 % 2,))
                    split_next(m)

            def attn_phase():
                s, nb = at_, base["attn"]
                norm(norms["attn"])
                for m in range(12):
                    if m in (5, 7):
                        dve.wait_ge(piece_used, nb + m + 1)
                        n = (m - 4) // 2
                        nc.vector.tensor_copy(v_att[:, :, n * HALF:(n + 1) * HALF], PS[:, 4 + 2 * n:6 + 2 * n, :]
                                              ).then_inc(s["v"], 1)
                    if m in (9, 11):
                        dve.wait_ge(piece_used, nb + m + 1)
                        n = (m - 8) // 2
                        nc.vector.tensor_scalar(qT[:, 4 * n:4 * n + 4, :].rearrange("p (a b) t -> p a (b t)", a=2),
                                                PS[:, 2 * n:2 * n + 2, :], HD ** -0.5, None, ALU.mult
                                                ).then_inc(s["q"], 1)
                    split_next(nb + m)

                def diag(v):
                    return v.rearrange("p h (b t) -> p h b t", t=P)[:, :, 0:3:2, :]

                mask = causal[:, :].unsqueeze(1).unsqueeze(1).broadcast_to([P, 2, 2, P])

                def z_out(pr):
                    dve.wait_ge(s["z_psum"], pr + 1)
                    zb = 2 * (pr % 2)
                    nc.vector.tensor_tensor(diag(z_sb[pr % 3][:, :, :]), diag(PS[:, zb:zb + 2, 0:ZW]), mask, ALU.mult)
                    nc.vector.tensor_copy(z_sb[pr % 3][:, :, P:2 * P], PS[:, zb:zb + 2, P:2 * P]).then_inc(s["z"], 1)

                def softplus(pr):
                    dve.wait_ge(s["ln"], pr + 1)
                    if pr >= 2:
                        dve.wait_ge(s["cs_psum"], pr - 1)
                    u = u_sp[pr % 2][:, :, :]
                    link(nc.vector.scalar_tensor_tensor(out=u, in0=z_sb[pr % 3][:, :, :], scalar=0.0,
                                                        in1=z_ln[pr % 2][:, :, :], op0=ALU.max, op1=ALU.add))
                    nc.vector.tensor_tensor(diag(u), diag(u), mask, ALU.mult).then_inc(s["u"], 1)

                def log_att(pr):
                    dve.wait_ge(s["cs_psum"], pr + 1)
                    if pr >= 2:
                        dve.wait_ge(s["exp"], pr - 1)
                    nc.vector.tensor_tensor(log_a[pr % 2][:, :, :], z_sb[pr % 3][:, :, :], PS[:, 4:6, 0:ZW],
                                            ALU.subtract).then_inc(s["log_a"], 1)

                def o_lo(pr):
                    dve.wait_ge(s["o_hi"], pr + 1)
                    nc.vector.tensor_tensor(xa_lo[:, pr, :], PS[:, 6 + pr % 2, 0:T], xa_hi[:, pr, :].bitcast(f32),
                                            ALU.subtract).then_inc(s["o_lo"], 1)

                z_out(0)
                softplus(0)
                for i in range(NC):
                    if i + 1 < NC:
                        z_out(i + 1)
                    log_att(i)
                    if i + 1 < NC:
                        softplus(i + 1)
                    if i >= 1:
                        o_lo(i - 1)
                o_lo(NC - 1)
                for m in range(12, 16):
                    if m % 2:
                        residual("attn", nb + m, (m // 2 % 2,))
                    split_next(nb + m)

            dve.wait_ge(cols_psum, 1)
            nc.vector.tensor_copy(cols[:, :], PS[:, 0, 0:n_rows]).then_inc(cols_ready, 1)
            for n in range(3):
                split_lo(n)
            for ph in PHASES:
                if ph.startswith("moe"):
                    moe_phase(int(ph[3]))
                if ph == "attn":
                    attn_phase()
                if ph == "rwkv":
                    rwkv_phase()
            norm_scale(norms["final"])
            dve.wait_ge(gain_loaded, 16)
            for j in range(NT):
                dve.wait_ge(*norms["final"].at("scaled", j + 1))
                for a in range(2):
                    sl = xs[:, j, a * HALF:(a + 1) * HALF]
                    nc.vector.tensor_tensor(sl, sl, gain_row[:, a * HALF:(a + 1) * HALF], ALU.mult
                                            ).then_inc(final_ready, 1)

        @block.tensor
        def _(pe):
            pe.wait_ge(params_loaded, 64)
            pe.wait_ge(ident_ready, 5)
            nc.tensor.transpose(PS[:, 0, 0:n_rows], prow[:, :], ident[0:n_rows, 0:n_rows]).then_inc(cols_psum, 1)
            pe.wait_ge(cols_ready, 1)

            def norm(nm):
                for j in range(NT):
                    pe.wait_ge(*nm.at("scaled", j + 1))
                    for b in range(NC):
                        m = nc.tensor.transpose(PS[:, 4 + b // 2, (b % 2) * T + j * P:(b % 2) * T + (j + 1) * P],
                                                xs[:, j, b * P:(b + 1) * P], ident[:, :])
                        if j == NT - 1 and b % 2:
                            m.then_inc(norm_sems["turned"], 1)

            def three(dst, xh, xl, wh, wl, start, stop):
                nc.tensor.matmul(dst, xh, wh, start=start, stop=False)
                nc.tensor.matmul(dst, xh, wl, start=False, stop=False)
                return nc.tensor.matmul(dst, xl, wh, start=False, stop=stop)

            def token_major(n, xh, xl, bank):
                pe.wait_ge(lo_ready, n + 1)
                g = dense_pieces[n][2]
                for j in range(NT):
                    for i in range(4):
                        b = 4 * g + i
                        m = three(PS[:, bank(j), :], xh[:, b, j * P:(j + 1) * P], xl[:, b, j * P:(j + 1) * P],
                                  whi[n % 3][:, i, :], wlo[n % 3][:, i, :], b == 0, b == NC - 1)
                m.then_inc(piece_used, 1)

            def channel_major(n, xh, xl, bank0):
                pe.wait_ge(lo_ready, n + 1)
                g = dense_pieces[n][2]
                for co in range(4):
                    dst = PS[:, bank0 + co // 2, (co % 2) * T:(co % 2 + 1) * T]
                    for i in range(4):
                        b = 4 * g + i
                        wh = whi[n % 3][:, i, co * P:(co + 1) * P]
                        wl = wlo[n % 3][:, i, co * P:(co + 1) * P]
                        m = three(dst, wh, wl, xh[:, b, :], xl[:, b, :], b == 0 and co % 2 == 0,
                                  b == NC - 1 and co % 2 == 1)
                m.then_inc(piece_used, 1)

            def rwkv_phase():
                norm(norms["rwkv"])
                pe.wait_ge(rw["x_lo"], 2)
                for m in range(4):
                    token_major(m, xa_hi, xa_lo, lambda j: 2 * (m // 2) + j)
                pe.wait_ge(rw["lora_loaded"], 16 * 7)
                for i, (bank, c0, n) in enumerate(((4, 0, LW), (5, LW, LW), (6, 2 * LW, P), (7, 2 * LW + P, LG - P))):
                    pe.wait_ge(rw["mixed"], min(i, 2) + 2)
                    if i == 0:
                        pe.wait_ge(rw["hn_act"], 2)
                        pe.wait_ge(rw["hn_dve"], 2)
                    src = mixed_[1 + min(i, 2)]
                    for b in range(NC):
                        mm = nc.tensor.matmul(PS[0:n, bank, 0:T], lora1[:, b, c0:c0 + n], src[:, b, :],
                                              start=b == 0, stop=b == NC - 1)
                    if i != 2:
                        mm.then_inc(rw["lora1"], 1)
                pe.wait_ge(rw["zones"], 1)
                for i, (zz, w2) in enumerate(((zw, w2x), (za, a2x))):
                    if i == 0:
                        pe.wait_ge(rw["z"], 1)
                        pe.wait_ge(rw["k"], 2)
                    else:
                        pe.wait_ge(rw["z"], 4)
                    for j in range(NT):
                        for a in range(2):
                            mm = nc.tensor.matmul(PS[:, 4 * i + 2 * j + a, :], zz[:, j * P:(j + 1) * P],
                                                  w2[:, a * HALF:(a + 1) * HALF], start=True, stop=True)
                    mm.then_inc(rw["lora2"], 1)
                pe.wait_ge(rw["sig"], NT)
                pe.wait_ge(rw["x_lo"], 4)
                pe.wait_ge(rw["masks"], 1)
                for m in range(4, 8):
                    token_major(m, xb_hi, xb_lo, lambda j: 2 * ((m - 4) // 2) + j)

                def cumulate(a):
                    for i, mask in enumerate((to_t, before_t)):
                        for j in range(NT):
                            mm = nc.tensor.matmul(PS[:, 4 + 2 * i + j, :], mask[:, :],
                                                  sig[:, j, a * HALF:(a + 1) * HALF], start=True, stop=True)
                    mm.then_inc(rw["cum"], 1)

                pe.wait_ge(rw["a"], NT)
                cumulate(0)
                pe.wait_ge(rw["x_lo"], 6)
                for m in range(8, 12):
                    pe.wait_ge(rw["r"], (m - 8) // 2 + 1)
                    token_major(m, xa_hi, xa_lo, lambda j: 2 * ((m - 8) // 2) + j)
                pe.wait_ge(rw["decay"], 3)
                cumulate(1)
                pe.wait_ge(rw["v"], 2)
                for b in range(NC):
                    for j in range(NT):
                        mm = nc.tensor.matmul(PS[:, 0, 4 * b + 2 * j:4 * b + 2 * j + 2], sig[:, j, b * P:(b + 1) * P],
                                              in_chunk[:, :], start=True, stop=True)
                mm.then_inc(rw["cd_psum"], 1)
                pe.wait_ge(rw["cd"], 1)
                pe.wait_ge(rw["decay"], 6)

                for a in range(2):
                    pe.wait_ge(rw["decay_used"], 3 * a + 3)
                    for i, src in enumerate((kk, a_s, k_s, r_s_)):
                        for bl in range(4):
                            for j in range(NT):
                                mm = nc.tensor.transpose(
                                    PS[:, 2 * i + bl // 2, (bl % 2) * T + j * P:(bl % 2) * T + (j + 1) * P],
                                    src[:, j, (4 * a + bl) * P:(4 * a + bl + 1) * P], ident[:, :])
                        mm.then_inc(rw["turned"], 1)
                    pe.wait_ge(rw["t_act"], 2 * a + 2)
                    pe.wait_ge(rw["t_dve"], 2 * a + 2)
                    for q in (2 * a, 2 * a + 1):
                        quad(a, q)
                    chunks(a)

                for i in range(4):
                    a, j = i // 2, i % 2
                    pe.wait_ge(rw["z_tok"], i + 1 if i < 2 else 4)
                    for bl in range(4):
                        mm = nc.tensor.transpose(PS[:, 4 + i, bl * P:(bl + 1) * P],
                                                 z_tok[:, j, (4 * a + bl) * P:(4 * a + bl + 1) * P], ident[:, :])
                    mm.then_inc(rw["zt_psum"], 1)
                pe.wait_ge(rw["zt_lo"], 4)
                for m in range(12, 16):
                    token_major(m, xa_hi, xa_lo, lambda j: 2 * j + (m - 12) // 2)

            def quad(a, q):
                o = HD * (q % 2)
                if q % 2:
                    pe.wait_ge(rw["u0_out"], 2 * q)
                    pe.wait_ge(rw["xa_out"], 2 * q)
                for j in range(NT):
                    t = slice(j * P, (j + 1) * P)
                    for i, (left, right) in enumerate(((BT, AT), (KT, AT), (BT, RT), (KT, RT))):
                        for hd in range(4):
                            mm = nc.tensor.matmul(PS[:, 4 * j + i, hd * P:(hd + 1) * P], left[o:o + HD, hd, t],
                                                  right[o:o + HD, hd, t], start=True, stop=True)
                        mm.then_inc(rw["m_psum"], 1)
                for l in range(LEVELS):
                    for j in range(NT):
                        if l == 0:
                            pe.wait_ge(rw["m_out"], 8 * q + 8)
                        elif l == 1:
                            pe.wait_ge(rw["w_out"], 12 * q + j + 1)
                        else:
                            pe.wait_ge(rw["x_out"], 8 * q + 2 * (l - 2) + j + 1)
                        for hd in range(4):
                            mm = nc.tensor.matmul(PS[:, j, hd * P:(hd + 1) * P], NT_[j][:, hd, :],
                                                  ident[:, :] if l == 0 else X[j][:, hd, :], start=True, stop=True)
                        mm.then_inc(rw["w_psum"], 1)
                    if l == 0:
                        continue
                    for j in range(NT):
                        pe.wait_ge(rw["w_out"], 12 * q + 2 * l + j + 1)
                        if l == 1:
                            pe.wait_ge(rw["x1"], 2 * q + j + 1)
                        else:
                            pe.wait_ge(rw["xt_out"], 10 * q + 2 * (l - 2) + j + 1)
                        if l < LEVELS - 1:
                            for hd in range(4):
                                mm = nc.tensor.matmul(PS[:, 2 + j, hd * P:(hd + 1) * P], XT[j][:, hd, :],
                                                      W_[j][:, hd, :], start=True, stop=True)
                            mm.then_inc(rw["p_psum"], 1)
                        for hd in range(4):
                            mm = nc.tensor.matmul(PS[:, 4 + j, hd * P:(hd + 1) * P], W_[j][:, hd, :],
                                                  XT[j][:, hd, :], start=True, stop=True)
                        mm.then_inc(rw["pt_psum"], 1)
                for j in range(NT):
                    for i, left in enumerate((AakT, ArkT)):
                        for hd in range(4):
                            c = (HH * a + 2 * hd + q % 2) * HD
                            mm = nc.tensor.matmul(PS[:, 6 + j, 256 * i + hd * HD:256 * i + (hd + 1) * HD],
                                                  left[j][:, hd, :], v_s[:, j, c:c + HD], start=True, stop=True)
                    mm.then_inc(rw["cy_psum"], 1)
                for j in range(NT):
                    pe.wait_ge(rw["xt_out"], 10 * q + 2 * (LEVELS - 2) + j + 1)
                    for hd in range(4):
                        c = (HH * a + 2 * hd + q % 2) * HD
                        mm = nc.tensor.matmul(PS[o:o + HD, 2 + j, hd * P:(hd + 1) * P],
                                              kk[:, j, c:c + HD], XT[j][:, hd, :], start=True, stop=True)
                    mm.then_inc(rw["xa_psum"], 1)
                for j in range(NT):
                    pe.wait_ge(rw["cy_out"], 2 * q + j + 1)
                    for hd in range(4):
                        mm = nc.tensor.matmul(PS[:, 6 + j, hd * HD:(hd + 1) * HD], XT[j][:, hd, :],
                                              W_[j][:, hd // 2, (hd % 2) * HD:(hd % 2 + 1) * HD],
                                              start=True, stop=True)
                    mm.then_inc(rw["u0_psum"], 1)

            def chunks(a):
                pe.wait_ge(rw["u0_out"], 4 * a + 4)
                pe.wait_ge(rw["xa_out"], 4 * a + 4)
                for c in range(4):
                    j, p0 = c // 2, CH * (c % 2)
                    t = slice(p0, p0 + CH)
                    if c:
                        pe.wait_ge(rw["s_out"], 3 * a + c)
                        for hl in range(HH):
                            o, b = HD * (hl % 2), hl // 2
                            mm = nc.tensor.matmul(PS[t, 7 * (hl % 2), b * HD:(b + 1) * HD],
                                                  XaT[j][o:o + HD, b, t], S[c][o:o + HD, b, :],
                                                  start=True, stop=True)
                        mm.then_inc(rw["u_psum"], 1)
                    if c < 3:
                        if c:
                            pe.wait_ge(rw["u_out"], 3 * a + c)
                        for hl in range(HH):
                            o, b, ch = HD * (hl % 2), hl // 2, (HH * a + hl) * HD
                            dst = PS[o:o + HD, 1, b * HD:(b + 1) * HD]
                            nc.tensor.matmul(dst, a_s[t, j, ch:ch + HD], U[t, j, hl, :], start=True, stop=False)
                            mm = nc.tensor.matmul(dst, k_s[t, j, ch:ch + HD], v_s[t, j, ch:ch + HD],
                                                  start=False, stop=True)
                        mm.then_inc(rw["s_psum"], 1)
                pe.wait_ge(rw["u_out"], 3 * a + 3)
                for j in range(NT):
                    for hl in range(HH):
                        o, b = HD * (hl % 2), hl // 2
                        dst = PS[:, 2 + 2 * (hl % 2) + j, b * HD:(b + 1) * HD]
                        for c in (2 * j, 2 * j + 1):
                            t0 = CH * (c % 2)
                            nc.tensor.matmul(dst[t0:t0 + CH, :], RT[o:o + HD, b, c * CH:(c + 1) * CH],
                                             S[c][o:o + HD, b, :], start=True, stop=False)
                        mm = nc.tensor.matmul(dst, ArbT[hl % 2][j][:, b, :], U[:, j, hl, :], start=False, stop=True)
                    mm.then_inc(rw["y_psum"], 1)
                if a == 0:
                    pe.wait_ge(rw["late_loaded"], 64)
                else:
                    pe.wait_ge(rw["z_tok"], 2)
                for j in range(NT):
                    c = slice(a * HALF, (a + 1) * HALF)
                    nc.tensor.matmul(PS[:, 6 + j, :], zg[:, j * P:(j + 1) * P], g2a[:, c], start=True, stop=False)
                    mm = nc.tensor.matmul(PS[:, 6 + j, :], zg2[:, j * P:(j + 1) * P], g2b[:, c], start=False, stop=True)
                    mm.then_inc(rw["g_psum"], 1)
                pe.wait_ge(rw["z_tok"], 2 * a + 2)

            def attn_phase():
                s, nb = at_, base["attn"]
                nm = norms["attn"]
                norm(nm)
                pe.wait_ge(*nm.at("lo", NC // 2))
                for m in range(4):
                    channel_major(nb + m, xa_hi, xa_lo, 2 * (m // 2))
                for m in range(4, 8):
                    token_major(nb + m, xa_hi, xa_lo, lambda j: 4 + 2 * ((m - 4) // 2) + j)
                for m in range(8, 12):
                    if m % 2 == 0:
                        pe.wait_ge(s["k"], (m - 8) // 2 + 1)
                    channel_major(nb + m, xb_hi, xb_lo, 2 * ((m - 8) // 2))

                def z(pr):
                    if pr >= 2:
                        pe.wait_ge(s["z"], pr - 1)
                    for hh in range(2):
                        o = hh * HD
                        bank = 2 * (pr % 2) + hh
                        nc.tensor.matmul(PS[:, bank, 0:T], kT[o:o + HD, pr, 0:P], qT[o:o + HD, pr, :],
                                         start=True, stop=True)
                        m = nc.tensor.matmul(PS[:, bank, T:ZW], kT[o:o + HD, pr, P:T], qT[o:o + HD, pr, P:T],
                                             start=True, stop=True)
                    m.then_inc(s["z_psum"], 1)

                def suffix_sums(pr):
                    pe.wait_ge(s["u"], pr + 1)
                    if pr >= 1:
                        pe.wait_ge(s["log_a"], pr)
                    for hh in range(2):
                        u = u_sp[pr % 2][:, hh, :]
                        nc.tensor.matmul(PS[:, 4 + hh, 0:ZW], from_s[:, :], u, start=True, stop=False)
                        m = nc.tensor.matmul(PS[:, 4 + hh, P:T], ones[:, :], u[:, T:ZW], start=False, stop=True)
                    m.then_inc(s["cs_psum"], 1)

                def mix_values(pr):
                    pe.wait_ge(s["att"], pr + 1)
                    if pr >= 2:
                        pe.wait_ge(s["o_lo"], pr - 1)
                    for hh in range(2):
                        o, c = hh * HD, (2 * pr + hh) * HD
                        a = att[pr % 3][:, hh, :]
                        dst = PS[o:o + HD, 6 + pr % 2, :]
                        nc.tensor.matmul(dst[:, 0:T], v_att[:, 0, c:c + HD], a[:, 0:T], start=True, stop=False)
                        m = nc.tensor.matmul(dst[:, P:T], v_att[:, 1, c:c + HD], a[:, T:ZW], start=False, stop=True)
                    m.then_inc(s["o_psum"], 1)

                pe.wait_ge(s["v"], 2)
                pe.wait_ge(s["q"], 2)
                z(0)
                for i in range(NC):
                    if i + 1 < NC:
                        z(i + 1)
                    suffix_sums(i)
                    if i >= 1:
                        mix_values(i - 1)
                mix_values(NC - 1)
                pe.wait_ge(s["o_lo"], NC)
                for m in range(12, 16):
                    token_major(nb + m, xa_hi, xa_lo, lambda j: 2 * j + (m - 12) // 2)

            def moe_phase(k):
                s, nb = moe_sems, base[f"moe{k}"]
                nm = norms[f"moe{k}"]
                norm(nm)
                pe.wait_ge(s["wr_lo"], k * PER["wr_lo"] + 1)
                pe.wait_ge(*nm.at("lo", NC // 2))
                for j in range(NT):
                    for b in range(NC):
                        m = three(PS[:, 0, j * NR:(j + 1) * NR], xa_hi[:, b, j * P:(j + 1) * P],
                                  xa_lo[:, b, j * P:(j + 1) * P], wr_hi[:, b, :], wr_lo[:, b, :], b == 0, b == NC - 1)
                m.then_inc(s["logits"], 1)

                def gate_up(slot, g):
                    for j in range(NT):
                        for i in range(4):
                            b = 4 * g + i
                            m = three(PS[:, 4 + j, :], xa_hi[:, b, j * P:(j + 1) * P], xa_lo[:, b, j * P:(j + 1) * P],
                                      whi[slot][:, i, :], wlo[slot][:, i, :], b == 0, b == NC - 1)
                    m.then_inc(piece_used, 1)

                def down(slot, first, last):
                    wh = whi[slot][:, :, :].rearrange("p (f a) c -> p f a c", f=NF)
                    wl = wlo[slot][:, :, :].rearrange("p (f a) c -> p f a c", f=NF)
                    for j in range(NT):
                        for a in range(2):
                            for f in range(NF):
                                m = three(PS[:, 2 * j + a, :], hT_hi[:, f, j * P:(j + 1) * P],
                                          hT_lo[:, f, j * P:(j + 1) * P], wh[:, f, a, :], wl[:, f, a, :],
                                          first and f == 0, last and f == NF - 1)
                    m.then_inc(piece_used, 1)

                def turn(e):
                    for j in range(NT):
                        pe.wait_ge(s["hact"], e * 2 + k * PER["hact"] + (j + 1))
                        for f in range(NF):
                            m = nc.tensor.transpose(PS[:, 6, f * T + j * P:f * T + (j + 1) * P],
                                                    hact[:, j, f * P:(f + 1) * P], ident[:, :])
                    m.then_inc(s["hT_psum"], 1)

                def piece(n):
                    pe.wait_ge(lo_ready, n + 1)
                    return None

                for g in range(2):
                    pe.wait_ge(lo_ready, nb + g + 1)
                    gate_up((nb + g) % 3, g)
                turn(0)

                def step(e, n0, first):
                    for i in range(3):
                        slot = (nb - 1 + i) % 3
                        pe.wait_ge(lo_ready, n0 + (i + 1))
                        if i < 2:
                            gate_up(slot, i)
                        else:
                            pe.wait_ge(s["hT_lo"], e + k * PER["hT_lo"])
                            if first:
                                pe.wait_ge(s["gates"], k * PER["gates"] + 1)
                            down(slot, first, False)
                    turn(e)

                step(1, nb + 2, True)
                with pe.Fori(2, E) as e:
                    step(e, e * 3 + (nb - 1), False)
                pe.wait_ge(lo_ready, nb + 3 * E)
                pe.wait_ge(s["hT_lo"], k * PER["hT_lo"] + E)
                down((nb + 3 * E - 1) % 3, False, True)

            for ph in PHASES:
                if ph.startswith("moe"):
                    moe_phase(int(ph[3]))
                if ph == "rwkv":
                    rwkv_phase()
                if ph == "attn":
                    attn_phase()


_INS = ["x", "norm_mix", "norm_ffn", "norm_kv", "norm_final", "rw_mix", "rw_w_rkv", "rw_w0", "rw_w1", "rw_w2",
        "rw_a0", "rw_a1", "rw_a2", "rw_g1", "rw_g2", "rw_k_k", "rw_k_a", "rw_r_k", "rw_lnx_w", "rw_lnx_b",
        "rw_w_out", "w_kv", "sb_w_q", "sb_w_out", "moe_w_group", "moe_b_group", "moe_w_inner", "moe_b_inner",
        "moe_w_gate", "moe_w_up", "moe_w_down"]


def kernel(**inputs):
    import numpy as _np
    import concourse.bacc as _bacc
    from concourse import mybir as _mybir
    from concourse.bass_utils import run_bass_kernel_spmd as _run

    nc = _bacc.Bacc("TRN2", target_bir_lowering=False, num_devices=1)
    arrays, args = {}, []
    for name in _INS:
        a = _np.ascontiguousarray(inputs[name])
        arrays[f"in_{name}_dram"] = a
        args.append(nc.dram_tensor(f"in_{name}_dram", a.shape, _mybir.dt.from_np(a.dtype), kind="ExternalInput").ap())
    args.append(nc.dram_tensor("out_0_dram", inputs["x"].shape, _mybir.dt.float32, kind="ExternalOutput").ap())
    trunk_program(nc, *args)
    r = _run(nc, [arrays], core_ids=[0])
    return r.results[0]["out_0_dram"]
```

```python
import concourse.bass as bass
from concourse import mybir
from contextlib import ExitStack

PHASES = ["rwkv", "moe0", "attn", "moe1"]


def trunk_program(nc, x, norm_mix, norm_ffn, norm_kv, norm_final,
                  rw_mix, rw_w_rkv, rw_w0, rw_w1, rw_w2, rw_a0, rw_a1, rw_a2, rw_g1, rw_g2,
                  rw_k_k, rw_k_a, rw_r_k, rw_lnx_w, rw_lnx_b, rw_w_out,
                  w_kv, sb_w_q, sb_w_out,
                  moe_w_group, moe_b_group, moe_w_inner, moe_b_inner,
                  moe_w_gate, moe_w_up, moe_w_down, out):
    f32, f32r = mybir.dt.float32, mybir.dt.float32r
    ALU, ACT, AX = mybir.AluOpType, mybir.ActivationFunctionType, mybir.AxisListType

    P = 128
    T, C = x.shape[1], x.shape[2]
    NT = T // P
    NC = C // P
    HALF = 512
    E = moe_w_gate.shape[1]
    G = moe_w_group.shape[2]
    EG = E // G
    F = moe_w_gate.shape[3]
    NF = F // P
    NR = G + E
    RMS_EPS = 1e-6
    GN_EPS = 64e-5
    HD = rw_r_k.shape[2]
    CH = 64
    LOG_DECAY = 0.6065306597126334
    LW, LG = rw_w1.shape[2], rw_g1.shape[2]
    HH = 8

    def load_dense(sp, dst, w, n, g, sem):
        v = w[g * HALF:(g + 1) * HALF, n * HALF:(n + 1) * HALF].rearrange("(b p) c -> p b c", p=P)
        for a in range(2):
            sp.dma_start(dst[:, 2 * a:2 * a + 2, :], v[:, 2 * a:2 * a + 2, :]).then_inc(sem, 16)

    dense_pieces = {}
    base = {}
    n_pieces = 0
    for ph in PHASES:
        base[ph] = n_pieces
        mats = {"rwkv": [(rw_w_rkv[0, 1], 2), (rw_w_rkv[0, 0], 2), (rw_w_rkv[0, 2], 2), (rw_w_out[0], 2)],
                "attn": [(w_kv, 4), (sb_w_q[0], 2), (sb_w_out[0], 2)]}.get(ph)
        if mats is None:
            n_pieces += 3 * E
        else:
            for w, halves in mats:
                for n in range(halves):
                    for g in range(2):
                        dense_pieces[n_pieces] = (w, n, g)
                        n_pieces += 1
    TOTAL = n_pieces

    ctx = ExitStack()
    with ctx:
        def sem(name):
            return ctx.enter_context(nc.semaphore(name))

        ctx.enter_context(nc.sbuf_tensor("arena", [P, 51200], f32))
        ARENA = 16512
        SIZE = 51200 * 4
        cursor = [0]

        def place(name, shape, dt=f32, at=None):
            size = 4
            for s in shape[1:]:
                size *= s
            size = (size + 31) // 32 * 32
            if at is None:
                at = cursor[0]
                cursor[0] += size
            assert at + size <= SIZE, (name, at, size)
            return nc.alloc_sbuf_tensor_at(name, shape, dt, offset=ARENA + at)

        KB = 1024
        RING, HI, LO = 4, 3, 2
        assert 3 * EG % (RING * HI) == 0
        w_ring = [place(f"w_ring{i}", [P, 4, HALF]) for i in range(RING)]
        whi = [place(f"w_hi{i}", [P, 4, HALF], f32r) for i in range(HI)]
        wlo = [place(f"w_lo{i}", [P, 4, HALF], f32r) for i in range(LO)]
        h_at = cursor[0]
        h = place("h", [P, NT, C])
        ident = place("ident", [P, P])
        causal = place("causal", [P, P])
        from_s = place("from_s", [P, P])
        ones = place("ones", [P, P])
        n_rows = 88
        cols = place("cols", [P, n_rows])
        wr = [place(f"wr{k}", [P, NC, NR]) for k in range(2)]
        ident_r = place("ident_r", [P, P], f32r)
        slot_no = place("slot_no", [P, P])
        slot_int = place("slot_int", [P, P], mybir.dt.int32)
        br = [place(f"br{k}", [P, NR]) for k in range(2)]
        ss = place("ss", [P, NT])
        ms = place("ms", [P, NT])
        rec = place("rec", [P, NT])
        rstd = place("rstd", [P, NT])
        R0 = cursor[0]

        XA_AT = R0
        xa_hi = place("xa_hi", [P, NC, T], f32r, at=XA_AT)
        xa_lo = place("xa_lo", [P, NC, T], f32r, at=XA_AT + 8 * KB)
        xb_hi = place("xb_hi", [P, NC, T], f32r, at=XA_AT + 16 * KB)
        xb_lo = place("xb_lo", [P, NC, T], f32r, at=XA_AT + 24 * KB)
        xt_hi = place("xt_hi", [P, NT, C], f32r, at=XA_AT + 16 * KB)
        xt_lo = place("xt_lo", [P, NT, C], f32r, at=XA_AT + 24 * KB)
        xs = place("xs", [P, NT, C], at=XA_AT + 32 * KB)
        prow = place("prow", [n_rows, P], at=XA_AT + 40 * KB)
        M0 = XA_AT + 40 * KB
        off = [M0]

        def mplace(name, shape, dt=f32):
            size = 4
            for s in shape[1:]:
                size *= s
            size = (size + 31) // 32 * 32
            t = place(name, shape, dt, at=off[0])
            off[0] += size
            return t

        lg = mplace("lg", [P, NT, NR])
        rev = mplace("rev", [P, EG])
        gates = mplace("gates", [P, NT, E])
        r_gs = mplace("r_gs", [P, NT, G])
        r_eg = mplace("r_eg", [P, NT, G])
        r_eq = mplace("r_eq", [P, NT, G])
        r_fg = mplace("r_fg", [P, NT, G])
        groups = mplace("groups", [P, NT, G])
        place_in = mplace("place_in", [P, NT, G])
        n_in = mplace("n_in", [P, G])
        n_max = mplace("n_max", [P, 1])
        n_max_int = mplace("n_max_int", [P, 1], mybir.dt.int32)
        gates_hi = mplace("gates_hi", [P, NT, E], f32r)
        gates_lo = mplace("gates_lo", [P, NT, E], f32r)
        ffn_row = mplace("ffn_row", [P, C])
        gain_row = mplace("gain_row", [P, C])
        xT = mplace("xT", [P, NC, T])
        pick = mplace("pick", [P, NT, P], f32r)
        pick_t = mplace("pick_t", [P, T], f32r)
        xe_hi = mplace("xe_hi", [P, NC, P], f32r)
        xe_lo = mplace("xe_lo", [P, NC, P], f32r)
        slot_gates = mplace("slot_gates", [P, E])
        silu_s = mplace("silu_s", [P, F])
        hact_s = mplace("hact_s", [P, F])
        hs_hi = mplace("hs_hi", [P, NF, P], f32r)
        hs_lo = mplace("hs_lo", [P, NF, P], f32r)
        y_hi = mplace("y_hi", [P, 2, HALF], f32r)
        y_lo = mplace("y_lo", [P, 2, HALF], f32r)
        r_ilm = mplace("r_ilm", [P, NT, G, EG])
        r_il = mplace("r_il", [P, NT, EG])
        r_d = mplace("r_d", [P, NT, EG])
        r_d2 = mplace("r_d2", [P, NT, EG])
        r_f1 = mplace("r_f1", [P, NT, EG])
        r_f2 = mplace("r_f2", [P, NT, EG])
        r_s = mplace("r_s", [P, 10, NT])
        silu_g = mplace("silu_g", [P, NT, F])
        hact = mplace("hact", [P, NT, F])
        hT_hi = mplace("hT_hi", [P, NF, T], f32r)
        hT_lo = mplace("hT_lo", [P, NF, T], f32r)

        off[0] = M0
        kT = mplace("kT", [P, NC, T])
        qT = mplace("qT", [P, NC, T])
        v_att = mplace("v_att", [P, NT, C])
        ZW = T + P
        z_sb = [mplace(f"z_sb{i}", [P, 2, ZW]) for i in range(3)]
        z_abs = mplace("z_abs", [P, 2, ZW])
        z_exp = mplace("z_exp", [P, 2, ZW])
        z_ln = [mplace(f"z_ln{i}", [P, 2, ZW]) for i in range(2)]
        u_sp = [mplace(f"u_sp{i}", [P, 2, ZW]) for i in range(2)]
        log_a = [mplace(f"log_a{i}", [P, 2, ZW]) for i in range(2)]
        att = [mplace(f"att{i}", [P, 2, ZW]) for i in range(3)]

        def rplace(name, shape, kb, dt=f32):
            return place(name, shape, dt, at=R0 + int(kb * KB))

        k_s = rplace("k_s", [P, NT, C], 32)
        r_s_ = rplace("r_tok", [P, NT, C], 40)
        v_s = rplace("v_s", [P, NT, C], 48)
        sig = rplace("sig", [P, NT, C], 56)
        a_s = rplace("a_s", [P, NT, C], 64)
        kk = rplace("kk", [P, NT, C], 72)
        hnT = rplace("hnT", [P, NC, T], 80)
        dxT = rplace("dxT", [P, NC, T], 88)
        z_tok = rplace("z_tok", [P, NT, C], 56)
        mixed_ = [rplace("mix_k", [P, NC, T], 72), rplace("mix_w", [P, NC, T], 40), rplace("mix_a", [P, NC, T], 48),
                  rplace("mix_g", [P, NC, T], 72), rplace("mix_r", [P, NC, T], 40), rplace("mix_v", [P, NC, T], 48)]
        MIX_ROW = [1, 3, 4, 5, 0, 2]
        lora1 = rplace("lora1", [P, NC, 2 * LW + LG], 56)
        w2x = rplace("w2x", [LW + 1, C], 96)
        a2x = rplace("a2x", [LW + 1, C], 100)
        rk_row = rplace("rk_row", [P, C], 96)
        g2a = rplace("g2a", [P, C], 96)
        g2b = rplace("g2b", [LG - P, C], 100)
        zw = rplace("zw", [LW + 1, T], 104)
        za = rplace("za", [LW + 1, T], 105)
        zg = rplace("zg", [P, T], 106)
        zg2 = rplace("zg2", [LG - P, T], 107)
        kk_row = place("kk_row", [P, C], at=h_at)
        ka_row = place("ka_row", [P, C], at=h_at + 4 * KB)
        off[0] = R0 + 108 * KB
        to_t = mplace("to_t", [P, P])
        before_t = mplace("before_t", [P, P])
        LEVELS = 6
        level = [mplace(f"level{i}", [P, P]) for i in range(LEVELS)]
        level0T = mplace("level0T", [P, P])
        in_chunk = mplace("in_chunk", [P, 2])
        chunk_decay = mplace("chunk_decay", [P, NC, T // CH])
        n2 = mplace("n2", [P, NT, HH])
        n2i = mplace("n2i", [P, NT, HH])
        bonus = mplace("bonus", [P, NT, 2 * HH])
        e0 = rplace("e0", [P, NT, HALF], 80)
        e1 = rplace("e1", [P, NT, HALF], 84)
        tmp = rplace("tmp", [P, NT, HALF], 88)
        yb = rplace("yb", [P, NT, HALF], 92)
        S = [rplace(f"state{c}", [P, 4, 2 * HD], 80 + 2 * c) for c in range(4)]
        AT = rplace("AT", [P, 4, T], 0)
        BT = rplace("BT", [P, 4, T], 4)
        KT = rplace("KT", [P, 4, T], 8)
        RT = rplace("RT", [P, 4, T], 12)
        lnw_row = rplace("lnw_row", [P, C], 16)
        lnb_row = rplace("lnb_row", [P, C], 20)
        vb = rplace("vb", [P, HALF], 24)
        y_sq = rplace("y_sq", [P, HALF], 26)
        y_m = rplace("y_m", [P, 4, HH], 28)
        off[0] = 24 * KB
        NT_ = [mplace(f"n_t{j}", [P, 4, P]) for j in range(NT)]
        X = [mplace(f"inv{j}", [P, 4, P]) for j in range(NT)]
        XT = [mplace(f"inv_t{j}", [P, 4, P]) for j in range(NT)]
        W_ = [mplace(f"w_lev{j}", [P, 4, P]) for j in range(NT)]
        AakT = [mplace(f"aak_t{j}", [P, 4, P]) for j in range(NT)]
        ArkT = [[mplace(f"ark_t{q}{j}", [P, 4, P]) for j in range(NT)] for q in range(2)]
        ArbT = [[mplace(f"arb_t{q}{j}", [P, 4, P]) for j in range(NT)] for q in range(2)]
        XaT = [mplace(f"xa_t{j}", [P, 4, P]) for j in range(NT)]
        U = mplace("u_rows", [P, NT, HH, HD])
        assert off[0] <= 72 * KB

        PS = ctx.enter_context(nc.psum_tensor("ps", [P, 8, HALF], f32))

        x_loaded = sem("x_loaded")
        params_loaded = sem("params_loaded")
        router_loaded = sem("router_loaded")
        w_loaded = [sem(f"w_loaded{i}") for i in range(RING)]
        hi_ready = sem("hi_ready")
        lo_ready = sem("lo_ready")
        piece_used = sem("piece_used")
        ident_ready = sem("ident_ready")
        cols_psum = sem("cols_psum")
        cols_ready = sem("cols_ready")
        dve_step = sem("dve_step")
        out_written = sem("out_written")
        final_ready = sem("final_ready")
        gain_loaded = sem("gain_loaded")
        slots_ready = sem("slots_ready")

        norm_sems = {q: sem(f"norm_{q}") for q in ("squares", "recip", "rstd", "scaled", "turned", "hi", "lo")}
        norm_counts = dict.fromkeys(norm_sems, 0)

        class Norm:

            def __init__(s, h_ready, gains, turned=True):
                s.h_ready = h_ready
                s.gains = gains
                s.before = dict(norm_counts)
                for q, n in (("squares", NT), ("recip", 1), ("rstd", 1), ("scaled", NT),
                             ("turned", 4 * turned), ("hi", 4 * len(gains)), ("lo", 4 * len(gains))):
                    norm_counts[q] += n

            def at(s, q, n):
                return norm_sems[q], s.before[q] + n

        h_done = {}
        prev = (x_loaded, [16 * NT] * NT)
        norms = {}
        PER = dict(xT_act=1, xT_dve=1, logits=1, gs=1, eg=1, m2=1, e2=1, groups=1, places=1, n_max=1, gates=1,
                   xt_hi=NT, xt_lo=NT, gates_parts=1, ffn_row=16)
        moe_sems = {q: sem(f"moe_{q}") for q in PER}
        EXPERT = dict(x_hi=G, x_lo=G, silu=2 * E, hact=2 * E, hT_psum=E, hT_hi=E, hT_lo=E)
        expert_sems = {q: sem(f"expert_{q}") for q in EXPERT}
        packed_sems = {}
        for ph in PHASES:
            h_done[ph] = sem(f"{ph}_h_done")
            if ph.startswith("moe"):
                k = int(ph[3])
                packed_sems[k] = {q: sem(f"packed{k}_{q}") for q in
                                  ("pick", "gather", "slot_gates", "y_psum", "y_hi", "y_lo", "pt_psum", "pt", "combined", "added")}
                norms[ph] = Norm(prev, [])
            if ph == "rwkv":
                norms[ph] = Norm(prev, [])
                rw = {q: sem(f"rw_{q}") for q in
                      ("hn_act", "hn_dve", "lora_loaded", "rows_loaded", "rk_loaded", "late_loaded", "x_again",
                       "mixed", "x_hi", "x_lo", "lora1", "z", "zones", "lora2", "sig", "a", "k", "r", "v",
                       "cum", "decay", "decay_used", "kk0", "sq", "n2", "inv", "kk", "kmod", "rk", "rk_step",
                       "bonus", "masks", "mask_step", "vb_step", "cd_psum", "cd", "turned", "t_act", "t_dve",
                       "m_psum", "m_out", "x1", "w_psum", "w_out", "p_psum", "pt_psum", "x_out", "xt_out",
                       "xa_psum", "cy_psum", "xa_out", "cy_out", "u0_psum", "u0_out",
                       "u_psum", "u_out", "s_psum", "s_out", "y_psum", "g_psum", "y_cent", "y_sq",
                       "y_var", "y_std", "vb", "z_tok", "zt_psum", "zt_hi", "zt_lo", "vb_used")}
            if ph == "attn":
                norms[ph] = Norm(prev, [(32, xa_hi, xa_lo), (8, xb_hi, xb_lo)])
                at_ = {q: sem(f"attn_{q}") for q in
                       ("k", "v", "q", "z_psum", "z", "abs_exp", "ln", "u", "cs_psum", "log_a", "exp", "att",
                        "o_psum", "o_hi", "o_lo")}
            prev = (h_done[ph], [3, 4])
        norms["final"] = Norm(prev, [], turned=False)

        def is_last(g):
            return isinstance(g, int) and g == G - 1

        def ex(k, q, n):
            return expert_sems[q], n + k * EXPERT[q]

        block = ctx.enter_context(nc.Block())

        @block.sync
        def _(sp):
            for j in range(NT):
                sp.dma_start(h[:, j, :], x[0, j * P:(j + 1) * P, :]).then_inc(x_loaded, 16)
            sp.dma_start(prow[0:16, :], norm_mix.rearrange("l (b p) -> (l b) p", p=P)).then_inc(params_loaded, 16)
            sp.dma_start(prow[16:32, :], norm_ffn.rearrange("l (b p) -> (l b) p", p=P)).then_inc(params_loaded, 16)
            sp.dma_start(prow[32:40, :], norm_kv.rearrange("(b p) -> b p", p=P)).then_inc(params_loaded, 16)
            sp.dma_start(prow[40:88, :], rw_mix.rearrange("o m (b p) -> (o m b) p", p=P)).then_inc(params_loaded, 16)

            def slot_free(n):
                if not isinstance(n, int) or n >= RING:
                    sp.wait_ge(lo_ready, n - (RING - 1))

            def dense(n):
                slot_free(n)
                w, half, g = dense_pieces[n]
                load_dense(sp, w_ring[n % RING], w, half, g, w_loaded[n % RING])

            def gate_up(k, e, g, slot):
                for a, w in ((0, moe_w_gate), (1, moe_w_up)):
                    src = w[k, e, g * HALF:(g + 1) * HALF, :] if isinstance(e, int) else \
                        w[k, bass.ds(e, 1), g * HALF:(g + 1) * HALF, :].rearrange("o r f -> (o r) f")
                    sp.dma_start(w_ring[slot][:, :, a * F:(a + 1) * F],
                                 src.rearrange("(b p) f -> p b f", p=P)).then_inc(w_loaded[slot], 16)

            def down(k, e, slot):
                dst = w_ring[slot][:, :, :].rearrange("p (f a) c -> p f (a c)", f=NF)
                src = moe_w_down[k, e] if isinstance(e, int) else \
                    moe_w_down[k, bass.ds(e, 1)].rearrange("o r c -> (o r) c")
                src = src.rearrange("(f p) c -> p f c", p=P)
                for a in range(NF):
                    sp.dma_start(dst[:, a, :], src[:, a, :]).then_inc(w_loaded[slot], 16)

            def moe_loads(k):
                nb = base[f"moe{k}"]

                def group(g):
                    for i in range(EG):
                        e = g * EG + i
                        first = isinstance(g, int) and i == 0
                        for c in range(3):
                            if first and c == 0:
                                continue
                            n = nb + c - 1 if first else nb - 1 + 3 * i + c
                            slot_free(g * (3 * EG) + n)
                            if first and c == 2:
                                if nb:
                                    sp.wait_ge(piece_used, nb - 2)
                                sp.dma_start(ffn_row[:, :], norm_ffn[k].partition_broadcast(P)
                                             ).then_inc(moe_sems["ffn_row"], 16)
                                if f"moe{k}" == PHASES[-1]:
                                    sp.dma_start(gain_row[:, :], norm_final.partition_broadcast(P)
                                                 ).then_inc(gain_loaded, 16)
                            if first:
                                gate_up(k, e, c - 1, n % RING)
                            elif c < 2:
                                gate_up(k, e, c, n % RING)
                            else:
                                down(k, e - 1, n % RING)

                group(0)
                with sp.Fori(1, G) as g:
                    group(g)
                slot_free(nb + 3 * E - 1)
                down(k, E - 1, (nb + 3 * E - 1) % RING)

            def rwkv_loads():
                for n in range(3):
                    dense(n)
                sp.wait_ge(*norms["rwkv"].at("scaled", NT))
                sp.dma_start(kk_row[:, :], rw_k_k[0].partition_broadcast(P)).then_inc(rw["rows_loaded"], 16)
                sp.dma_start(ka_row[:, :], rw_k_a[0].partition_broadcast(P)).then_inc(rw["rows_loaded"], 16)
                for n in range(3, 9):
                    dense(n)
                sp.wait_ge(rw["lora2"], 2)
                sp.dma_start(rk_row[:, :], rw_r_k[0].rearrange("h n -> (h n)").partition_broadcast(P)
                             ).then_inc(rw["rk_loaded"], 16)
                for n in range(9, 12):
                    dense(n)
                sp.wait_ge(rw["kmod"], 2)
                for j in range(NT):
                    sp.dma_start(h[:, j, :], x[0, j * P:(j + 1) * P, :]).then_inc(rw["x_again"], 16)
                for n in range(12, 15):
                    dense(n)
                sp.wait_ge(rw["rk"], 2)
                sp.wait_ge(piece_used, 12)
                sp.dma_start(g2a[:, :], rw_g2[0, 0:P, :]).then_inc(rw["late_loaded"], 16)
                sp.dma_start(g2b[:, :], rw_g2[0, P:LG, :]).then_inc(rw["late_loaded"], 16)
                sp.dma_start(lnw_row[:, :], rw_lnx_w[0].partition_broadcast(P)).then_inc(rw["late_loaded"], 16)
                sp.dma_start(lnb_row[:, :], rw_lnx_b[0].partition_broadcast(P)).then_inc(rw["late_loaded"], 16)
                sp.wait_ge(rw["y_psum"], 4)
                dense(15)

            for ph in PHASES:
                if ph.startswith("moe"):
                    moe_loads(int(ph[3]))
                elif ph == "attn":
                    for n in range(base[ph], base[ph] + 16):
                        dense(n)
                else:
                    rwkv_loads()
            for j in range(NT):
                for a in range(2):
                    sp.wait_ge(final_ready, 2 * j + a + 1)
                    sp.dma_start(out[0, j * P:(j + 1) * P, a * HALF:(a + 1) * HALF],
                                 xs[:, j, a * HALF:(a + 1) * HALF]).then_inc(out_written, 16)
            sp.wait_ge(out_written, 64)

        @block.gpsimd
        def _(pool):
            nc.gpsimd.memset(ident[:, :], 0.0).then_inc(ident_ready, 1)
            pool.wait_ge(ident_ready, 1)
            nc.gpsimd.affine_select(out=ident[:, :], in_=ident[:, :], compare_op=ALU.not_equal, fill=1.0,
                                    base=0, pattern=[[-1, P]], channel_multiplier=1).then_inc(ident_ready, 1)
            nc.gpsimd.iota(slot_int[:, :], pattern=[[1, P]], base=0, channel_multiplier=0).then_inc(slots_ready, 1)
            pool.wait_ge(slots_ready, 1)
            nc.gpsimd.tensor_copy(slot_no[:, :], slot_int[:, :]).then_inc(slots_ready, 1)
            nc.gpsimd.tensor_copy(ident_r[:, :], ident[:, :]).then_inc(slots_ready, 1)
            nc.gpsimd.memset(ones[:, :], 1.0).then_inc(ident_ready, 1)
            pool.wait_ge(ident_ready, 3)
            nc.gpsimd.affine_select(out=causal[:, :], in_=ones[:, :], compare_op=ALU.is_gt, fill=0.0,
                                    base=0, pattern=[[1, P]], channel_multiplier=-1).then_inc(ident_ready, 1)
            nc.gpsimd.affine_select(out=from_s[:, :], in_=ones[:, :], compare_op=ALU.is_ge, fill=0.0,
                                    base=0, pattern=[[-1, P]], channel_multiplier=1).then_inc(ident_ready, 1)
            for a, w in ((0, rw_w1), (LW, rw_a1), (2 * LW, rw_g1)):
                pool.dma_start(lora1[:, :, a:a + w.shape[2]], w[0].rearrange("(b p) c -> p b c", p=P)
                               ).then_inc(rw["lora_loaded"], 16)
            pool.dma_start(w2x[0:LW, :], rw_w2[0]).then_inc(rw["lora_loaded"], 16)
            pool.dma_start(w2x[LW:LW + 1, :], rw_w0).then_inc(rw["lora_loaded"], 16)
            pool.dma_start(a2x[0:LW, :], rw_a2[0]).then_inc(rw["lora_loaded"], 16)
            pool.dma_start(a2x[LW:LW + 1, :], rw_a0).then_inc(rw["lora_loaded"], 16)
            for k in range(2):
                pool.dma_start(wr[k][:, :, 0:G], moe_w_group[k].rearrange("(b p) g -> p b g", p=P)
                               ).then_inc(router_loaded, 16)
                pool.dma_start(wr[k][:, :, G:NR], moe_w_inner[k].rearrange("(b p) g e -> p b (g e)", p=P)
                               ).then_inc(router_loaded, 16)
                pool.dma_start(br[k][:, 0:G], moe_b_group[k].partition_broadcast(P)).then_inc(router_loaded, 16)
                pool.dma_start(br[k][:, G:NR], moe_b_inner[k].rearrange("g e -> (g e)").partition_broadcast(P)
                               ).then_inc(router_loaded, 16)

            def rwkv_masks():
                steps = [0]

                def link(ins):
                    steps[0] += 1
                    ins.then_inc(rw["mask_step"], 1)
                    pool.wait_ge(rw["mask_step"], steps[0])

                sel = nc.gpsimd.affine_select
                link(sel(out=to_t[:, :], in_=ones[:, :], compare_op=ALU.is_ge, fill=0.0, base=0,
                         pattern=[[1, P]], channel_multiplier=-1))
                link(sel(out=before_t[:, :], in_=causal[:, :], compare_op=ALU.is_ge, fill=0.0, base=0,
                         pattern=[[-CH, P // CH], [0, CH]], channel_multiplier=1))
                link(sel(out=to_t[:, :], in_=to_t[:, :], compare_op=ALU.is_ge, fill=0.0, base=0,
                         pattern=[[-CH, P // CH], [0, CH]], channel_multiplier=1))
                link(sel(out=in_chunk[:, 0:1], in_=ones[:, 0:1], compare_op=ALU.is_ge, fill=0.0, base=CH - 1,
                         pattern=[[0, 1]], channel_multiplier=-1))
                link(sel(out=in_chunk[:, 1:2], in_=ones[:, 0:1], compare_op=ALU.is_ge, fill=0.0, base=-CH,
                         pattern=[[0, 1]], channel_multiplier=1))
                for i in range(LEVELS):
                    m = 1 << i
                    nb = P // (2 * m)
                    link(nc.gpsimd.memset(level[i][:, :], 0.0))
                    v = level[i][:, :].rearrange("p (b c) -> p b c", c=2 * m)[:, :, 0:m]
                    link(nc.gpsimd.memset(v, -1.0))
                    link(sel(out=v, in_=v, compare_op=ALU.is_ge, fill=0.0, base=-m,
                             pattern=[[-2 * m, nb], [0, m]], channel_multiplier=1))
                    link(sel(out=v, in_=v, compare_op=ALU.is_ge, fill=0.0, base=2 * m - 1,
                             pattern=[[2 * m, nb], [0, m]], channel_multiplier=-1))
                    link(sel(out=level[i][:, :], in_=level[i][:, :], compare_op=ALU.not_equal, fill=1.0, base=0,
                             pattern=[[-1, P]], channel_multiplier=1))
                v = level0T[:, :].rearrange("p (b c) -> p b c", c=2)[:, :, 1:2]
                link(nc.gpsimd.tensor_copy(level0T[:, :], ident[:, :]))
                sel(out=v, in_=v, compare_op=ALU.not_equal, fill=-1.0, base=0,
                    pattern=[[-2, P // 2], [0, 1]], channel_multiplier=1).then_inc(rw["masks"], 1)

            def rwkv_phase():
                for a in range(2):
                    c = slice(a * HALF, (a + 1) * HALF)
                    pool.wait_ge(rw["r"], a + 1)
                    pool.wait_ge(rw["kmod"], a + 1)
                    if a:
                        pool.wait_ge(rw["bonus"], a)
                    for j in range(NT):
                        m = nc.gpsimd.tensor_tensor(yb[:, j, :], r_s_[:, j, c], k_s[:, j, c], ALU.mult)
                    m.then_inc(rw["rk_step"], 1)
                    pool.wait_ge(rw["rk_step"], a + 1)
                    if a == 0:
                        pool.wait_ge(rw["rk_loaded"], 16)
                    for j in range(NT):
                        m = nc.gpsimd.tensor_tensor(yb[:, j, :], yb[:, j, :], rk_row[:, c], ALU.mult)
                    m.then_inc(rw["rk"], 1)
                for a in range(2):
                    for j in range(NT):
                        if a + j:
                            pool.wait_ge(rw["vb_used"], 2 * a + j)
                        else:
                            pool.wait_ge(rw["v"], 2)
                            pool.wait_ge(rw["bonus"], 2)
                            pool.wait_ge(piece_used, 12)
                        c = slice(a * HALF, (a + 1) * HALF)
                        nc.gpsimd.tensor_tensor(
                            vb[:, :].rearrange("p (h n) -> p h n", n=HD),
                            v_s[:, j, c].rearrange("p (h n) -> p h n", n=HD),
                            bonus[:, j, a * HH:(a + 1) * HH].unsqueeze(2).broadcast_to([P, HH, HD]), ALU.mult
                            ).then_inc(rw["vb_step"], 1)
                        pool.wait_ge(rw["vb_step"], 2 * a + j + 1)
                        pool.wait_ge(rw["late_loaded"], 64)
                        nc.gpsimd.tensor_tensor(vb[:, :], vb[:, :], lnb_row[:, c], ALU.add).then_inc(rw["vb"], 1)

            rwkv_masks()
            rwkv_phase()

            def attn_phase():
                s = at_
                for pr in range(NC):
                    pool.wait_ge(s["exp"], pr + 1)
                    a = att[pr % 3][:, :, :].rearrange("p h (b t) -> p h b t", t=P)[:, :, 0:3:2, :]
                    for hh in range(2):
                        m = nc.gpsimd.tensor_tensor(a[:, hh], a[:, hh],
                                                    causal[:, :].unsqueeze(1).broadcast_to([P, 2, P]), ALU.mult)
                    m.then_inc(s["att"], 1)

            for ph in PHASES:
                if ph == "attn":
                    attn_phase()

        @block.scalar
        def _(act):
            def split_hi(n):
                act.wait_ge(w_loaded[n % RING], 32 * (n // RING + 1))
                if n >= HI:
                    act.wait_ge(piece_used, n - (HI - 1))
                nc.scalar.activation(whi[n % HI][:, :, :], w_ring[n % RING][:, :, :], ACT.Copy).then_inc(hi_ready, 1)

            def split_next(m):
                if m + HI < TOTAL:
                    split_hi(m + HI)

            def norm_stats(nm):
                act.preload_act_table(ACT.Sqrt)
                for j in range(NT):
                    act.wait_ge(nm.h_ready[0], nm.h_ready[1][j])
                    nc.scalar.activation(PS[:, 4 + 2 * j:6 + 2 * j, :],
                                         h[:, j, :].rearrange("p (a c) -> p a c", a=2), ACT.Square,
                                         accum_out=ss[:, j:j + 1]).then_inc(norm_sems["squares"], 1)
                act.wait_ge(*nm.at("recip", 1))
                nc.scalar.activation(rstd[:, :], rec[:, :], ACT.Sqrt).then_inc(norm_sems["rstd"], 1)

            def norm(nm):
                norm_stats(nm)
                for i, (col, hi, lo) in enumerate(nm.gains):
                    for bank in range(NC // 2):
                        if i == 0:
                            act.wait_ge(*nm.at("turned", bank + 1))
                        else:
                            act.wait_ge(*nm.at("lo", bank + 1))
                        for b in (2 * bank, 2 * bank + 1):
                            m = nc.scalar.activation(hi[:, b, :], PS[:, 4 + bank, (b % 2) * T:(b % 2 + 1) * T],
                                                     ACT.Copy, scale=cols[:, col + b:col + b + 1])
                        m.then_inc(norm_sems["hi"], 1)

            def moe_phase(k):
                s, nm = moe_sems, norms[f"moe{k}"]
                if k == 0:
                    act.wait_ge(router_loaded, 16 * 8)
                norm_stats(nm)
                for j in range(NT):
                    act.wait_ge(*nm.at("scaled", j + 1))
                    nc.scalar.activation(xt_hi[:, j, :], xs[:, j, :], ACT.Copy).then_inc(s["xt_hi"], 1)
                act.wait_ge(*nm.at("turned", 2))
                nc.scalar.activation(xT[:, 0:4, :].rearrange("p (a b) t -> p a (b t)", a=2), PS[:, 4:6, :], ACT.Copy
                                     ).then_inc(s["xT_act"], 1)
                act.wait_ge(s["gs"], k * PER["gs"] + 1)
                nc.scalar.activation(r_eg[:, :, :], r_gs[:, :, :], ACT.Exp).then_inc(s["eg"], 1)
                act.wait_ge(s["m2"], k * PER["m2"] + 1)
                nc.scalar.activation(r_s[:, 4, :], r_s[:, 3, :], ACT.Exp).then_inc(s["e2"], 1)
                act.preload_act_table(ACT.Silu)
                act.wait_ge(s["n_max"], k * PER["n_max"] + 1)
                most = act.value_load(n_max_int[0:1, 0:1])
                with act.If(most < P + 1):
                    packed_experts(k)
                with act.Else():
                    all_experts(k)

            def split_hi_in_loop(g, n):
                slot = n % RING
                act.wait_ge(w_loaded[slot], (g * (3 * EG // RING) + (n // RING + 1)) * 32)
                act.wait_ge(piece_used, g * (3 * EG) + (n - (HI - 1)))
                nc.scalar.activation(whi[n % HI][:, :, :], w_ring[slot][:, :, :], ACT.Copy).then_inc(hi_ready, 1)

            def split_ahead(g, n):
                if isinstance(g, int):
                    split_next(g * (3 * EG) + n)
                else:
                    split_hi_in_loop(g, n + HI)

            def packed_experts(k):
                s, nb = packed_sems[k], base[f"moe{k}"]

                def xe(g):
                    act.wait_ge(s["gather"], g + 1)
                    nc.scalar.activation(xe_hi[:, :, :].rearrange("p (a b) t -> p a (b t)", a=2), PS[:, 2:4, :],
                                         ACT.Copy).then_inc(expert_sems["x_hi"], 1)

                def silu(e, used):
                    act.wait_ge(piece_used, used)
                    nc.scalar.activation(silu_s[:, :], PS[:, 4, 0:F], ACT.Silu).then_inc(expert_sems["silu"], 2)

                def h_hi(done):
                    act.wait_ge(*ex(k, "hT_psum", done))
                    nc.scalar.activation(hs_hi[:, :, :].rearrange("p f t -> p (f t)"), PS[:, 5, 0:NF * P], ACT.Copy
                                         ).then_inc(expert_sems["hT_hi"], 1)

                def y_part():
                    nc.scalar.activation(y_hi[:, :, :], PS[:, 0:2, :], ACT.Copy).then_inc(s["y_hi"], 1)

                def group(g):
                    for i in range(EG):
                        e, n0 = g * EG + i, nb - 1 + 3 * i
                        if isinstance(g, int) and e == 0:
                            split_next(nb)
                            silu(0, nb + 2)
                            split_next(nb + 1)
                            continue
                        h_hi(e)
                        if i == 3:
                            act.wait_ge(s["pt_psum"], g + 1)
                            nc.scalar.activation(pick_t[:, :], PS[:, 3, 0:T], ACT.Copy).then_inc(s["pt"], 1)
                        split_ahead(g, n0)
                        act.wait_ge(*ex(k, "hact", e * 2))
                        silu(e, g * (3 * EG) + (n0 + 2))
                        split_ahead(g, n0 + 1)
                        if i == 3 and not is_last(g):
                            xe(g + 1)
                        split_ahead(g, n0 + 2)
                        if i == 0:
                            y_part()

                xe(0)
                group(0)
                with act.Fori(1, G - 1) as g:
                    group(g)
                group(G - 1)
                h_hi(E)
                for a in range(2):
                    act.wait_ge(*((s["y_psum"], 1) if a == 0 else (piece_used, nb + 3 * E)))
                    nc.scalar.activation(y_hi[:, a, :], PS[:, a, :], ACT.Copy).then_inc(s["y_hi"], 1)
                split_next(nb + 3 * E - 1)

            def all_experts(k):
                nb = base[f"moe{k}"]
                nc.scalar.activation(xa_hi[:, :, :], xT[:, :, :], ACT.Copy).then_inc(expert_sems["x_hi"], G)

                def silu():
                    for j in range(NT):
                        nc.scalar.activation(silu_g[:, j, :], PS[:, 4 + j, 0:F], ACT.Silu
                                             ).then_inc(expert_sems["silu"], 1)

                def h_hi(e):
                    act.wait_ge(*ex(k, "hT_psum", e))
                    nc.scalar.activation(hT_hi[:, :, :], PS[:, 6, :].rearrange("p (f t) -> p f t", f=NF),
                                         ACT.Copy).then_inc(expert_sems["hT_hi"], 1)

                def group(g):
                    for i in range(EG):
                        e, n0 = g * EG + i, nb - 1 + 3 * i
                        if isinstance(g, int) and e == 0:
                            split_next(nb)
                            act.wait_ge(piece_used, nb + 2)
                            silu()
                            split_next(nb + 1)
                            continue
                        h_hi(e)
                        split_ahead(g, n0)
                        act.wait_ge(piece_used, g * (3 * EG) + (n0 + 2))
                        act.wait_ge(*ex(k, "hact", e * 2))
                        silu()
                        split_ahead(g, n0 + 1)
                        split_ahead(g, n0 + 2)

                group(0)
                with act.Fori(1, G - 1) as g:
                    group(g)
                group(G - 1)
                h_hi(E)
                split_next(nb + 3 * E - 1)

            def rwkv_phase():
                nm = norms["rwkv"]
                norm_stats(nm)
                act.wait_ge(cols_ready, 1)
                for bank in range(2):
                    act.wait_ge(*nm.at("turned", bank + 1))
                    for b in (2 * bank, 2 * bank + 1):
                        m = nc.scalar.activation(hnT[:, b, :], PS[:, 4 + bank, (b % 2) * T:(b % 2 + 1) * T],
                                                 ACT.Copy, scale=cols[:, b:b + 1])
                    m.then_inc(rw["hn_act"], 1)

                def x_hi(i, dst, n, halves=(0, 1)):
                    act.wait_ge(rw["mixed"], i + 1 + halves[-1])
                    for g in halves:
                        nc.scalar.activation(dst[:, 4 * g:4 * g + 4, :], mixed_[i][:, 4 * g:4 * g + 4, :], ACT.Copy
                                             ).then_inc(rw["x_hi"], 1)

                def out(dst, n, bank0, name, piece):
                    act.wait_ge(piece_used, piece + 1)
                    nc.scalar.activation(dst[:, :, n * HALF:(n + 1) * HALF], PS[:, bank0:bank0 + 2, :], ACT.Copy
                                         ).then_inc(rw[name], 1)

                split_hi(0)
                x_hi(0, xa_hi, 0, (0,))
                x_hi(0, xa_hi, 0, (1,))
                split_hi(1)
                split_hi(2)
                split_next(0)
                split_next(1)
                out(k_s, 0, 0, "k", 1)
                split_next(2)
                split_next(3)
                out(k_s, 1, 2, "k", 3)
                act.wait_ge(rw["lora1"], 1)
                nc.scalar.activation(zw[0:LW, :], PS[0:LW, 4, 0:T], ACT.Tanh).then_inc(rw["z"], 1)
                act.wait_ge(rw["lora1"], 2)
                nc.scalar.activation(za[0:LW, :], PS[0:LW, 5, 0:T], ACT.Copy).then_inc(rw["z"], 1)
                act.wait_ge(rw["lora1"], 3)
                nc.scalar.activation(zg[:, :], PS[:, 6, 0:T], ACT.Sigmoid).then_inc(rw["z"], 1)
                nc.scalar.activation(zg2[:, :], PS[0:LG - P, 7, 0:T], ACT.Sigmoid).then_inc(rw["z"], 1)
                x_hi(4, xb_hi, 1)
                for i, (dst, name) in enumerate(((sig, "sig"), (a_s, "a"))):
                    act.wait_ge(rw["lora2"], i + 1)
                    for j in range(NT):
                        nc.scalar.activation(dst[:, j, :].rearrange("p (a c) -> p a c", a=2),
                                             PS[:, 4 * i + 2 * j:4 * i + 2 * j + 2, :], ACT.Sigmoid
                                             ).then_inc(rw[name], 1)
                x_hi(5, xa_hi, 2)
                for a in range(2):
                    act.wait_ge(rw["kk0"], a + 1)
                    if a:
                        act.wait_ge(rw["n2"], a)
                    nc.scalar.activation(tmp[:, :, :], kk[:, :, a * HALF:(a + 1) * HALF], ACT.Square
                                         ).then_inc(rw["sq"], 1)
                    act.wait_ge(rw["n2"], a + 1)
                    nc.scalar.activation(n2i[:, :, :], n2[:, :, :], ACT.Sqrt).then_inc(rw["inv"], 1)
                    if a == 0:
                        split_next(4)
                split_next(5)
                out(r_s_, 0, 0, "r", 5)
                split_next(6)
                split_next(7)
                out(r_s_, 1, 2, "r", 7)
                split_next(8)

                def decays(a):
                    act.wait_ge(rw["cum"], a + 1)
                    for i, (dst, bank, sc) in enumerate(((e0, 4, -LOG_DECAY), (e1, 4, LOG_DECAY), (e0, 6, -LOG_DECAY))):
                        if i == 2:
                            act.wait_ge(rw["decay_used"], 3 * a + 1)
                        if i < 2 and a:
                            act.wait_ge(rw["decay_used"], 3 * a)
                        nc.scalar.activation(dst[:, :, :], PS[:, bank:bank + 2, :], ACT.Exp, scale=sc
                                             ).then_inc(rw["decay"], 1)

                decays(0)
                out(v_s, 0, 0, "v", 9)
                out(v_s, 1, 2, "v", 11)
                decays(1)
                act.wait_ge(rw["cd_psum"], 1)
                nc.scalar.activation(chunk_decay[:, :, :].rearrange("p b c -> p (b c)"), PS[:, 0, 0:4 * NC], ACT.Exp,
                                     scale=-LOG_DECAY).then_inc(rw["cd"], 1)

                for a in range(2):
                    act.wait_ge(rw["turned"], 4 * a + 1)
                    nc.scalar.activation(AT[:, :, :].rearrange("p (a b) t -> p a (b t)", a=2), PS[:, 0:2, :],
                                         ACT.Copy).then_inc(rw["t_act"], 1)
                    act.wait_ge(rw["turned"], 4 * a + 2)
                    nc.scalar.activation(KT[:, :, :].rearrange("p (a b) t -> p a (b t)", a=2), PS[:, 4:6, :],
                                         ACT.Copy).then_inc(rw["t_act"], 1)
                    for q in (2 * a, 2 * a + 1):
                        for l in range(1, LEVELS):
                            if l < LEVELS - 1:
                                for j in range(NT):
                                    act.wait_ge(rw["p_psum"], 8 * q + 2 * (l - 1) + j + 1)
                                    nc.scalar.activation(X[j][:, :, :].rearrange("p h s -> p (h s)"),
                                                         PS[:, 2 + j, :], ACT.Copy).then_inc(rw["x_out"], 1)
                            for j in range(NT):
                                act.wait_ge(rw["pt_psum"], 10 * q + 2 * (l - 1) + j + 1)
                                nc.scalar.activation(XT[j][:, :, :].rearrange("p h s -> p (h s)"),
                                                     PS[:, 4 + j, :], ACT.Copy).then_inc(rw["xt_out"], 1)
                        for j in range(NT):
                            act.wait_ge(rw["cy_psum"], 2 * q + j + 1)
                            nc.scalar.activation(W_[j][:, 0:2, :].rearrange("p a s -> p (a s)"), PS[:, 6 + j, 0:256],
                                                 ACT.Copy).then_inc(rw["cy_out"], 1)
                            act.wait_ge(rw["xa_psum"], 2 * q + j + 1)
                            o = HD * (q % 2)
                            nc.scalar.activation(XaT[j][o:o + HD, :, :].rearrange("p a s -> p (a s)"),
                                                 PS[o:o + HD, 2 + j, :], ACT.Copy).then_inc(rw["xa_out"], 1)
                    act.preload_act_table(ACT.Sqrt)
                    for j in range(NT):
                        i = 2 * a + j
                        act.wait_ge(rw["y_cent"], i + 1)
                        nc.scalar.activation(y_sq[:, :], yb[:, j, :], ACT.Square).then_inc(rw["y_sq"], 1)
                        act.wait_ge(rw["y_var"], i + 1)
                        nc.scalar.activation(y_m[:, 3, :], y_m[:, 2, :], ACT.Sqrt).then_inc(rw["y_std"], 1)
                for i in range(4):
                    act.wait_ge(rw["zt_psum"], i + 1)
                    a, j = i // 2, i % 2
                    nc.scalar.activation(xa_hi[:, 4 * a:4 * a + 4, j * P:(j + 1) * P],
                                         PS[:, 4 + i, :].rearrange("p (b t) -> p b t", t=P), ACT.Copy
                                         ).then_inc(rw["zt_hi"], 1)
                for m in range(9, 16):
                    split_next(m)

            def attn_phase():
                s, nb = at_, base["attn"]
                norm(norms["attn"])
                for m in range(12):
                    if m in (1, 3):
                        act.wait_ge(piece_used, nb + m + 1)
                        n = m // 2
                        nc.scalar.activation(kT[:, 4 * n:4 * n + 4, :].rearrange("p (a b) t -> p a (b t)", a=2),
                                             PS[:, 2 * n:2 * n + 2, :], ACT.Copy).then_inc(s["k"], 1)
                    split_next(nb + m)

                def softplus_tail(pr):
                    act.wait_ge(s["z"], pr + 1)
                    nc.scalar.activation(z_abs[:, :, :], z_sb[pr % 3][:, :, :], ACT.Abs).then_inc(s["abs_exp"], 1)
                    act.wait_ge(s["abs_exp"], 2 * pr + 1)
                    nc.scalar.activation(z_exp[:, :, :], z_abs[:, :, :], ACT.Exp, scale=-1.0
                                         ).then_inc(s["abs_exp"], 1)
                    act.wait_ge(s["abs_exp"], 2 * pr + 2)
                    if pr >= 2:
                        act.wait_ge(s["u"], pr - 1)
                    nc.scalar.activation(z_ln[pr % 2][:, :, :], z_exp[:, :, :], ACT.Ln, bias=1.0
                                         ).then_inc(s["ln"], 1)

                def att_exp(pr):
                    act.wait_ge(s["log_a"], pr + 1)
                    if pr >= 3:
                        act.wait_ge(s["o_psum"], pr - 2)
                    nc.scalar.activation(att[pr % 3][:, :, :], log_a[pr % 2][:, :, :], ACT.Exp
                                         ).then_inc(s["exp"], 1)

                def o_hi(pr):
                    act.wait_ge(s["o_psum"], pr + 1)
                    nc.scalar.activation(xa_hi[:, pr, :], PS[:, 6 + pr % 2, 0:T], ACT.Copy).then_inc(s["o_hi"], 1)

                act.preload_act_table_set("natural_log_exp_and_others")
                softplus_tail(0)
                softplus_tail(1)
                for i in range(NC):
                    if i + 2 < NC:
                        softplus_tail(i + 2)
                    att_exp(i)
                    if i >= 1:
                        o_hi(i - 1)
                o_hi(NC - 1)
                for m in range(12, 16):
                    split_next(nb + m)

            for ph in PHASES:
                if ph.startswith("moe"):
                    moe_phase(int(ph[3]))
                if ph == "attn":
                    attn_phase()
                if ph == "rwkv":
                    rwkv_phase()
            norm_stats(norms["final"])

        @block.vector
        def _(dve):
            steps = [0]

            def link(ins):
                steps[0] += 1
                ins.then_inc(dve_step, 1)
                dve.wait_ge(dve_step, steps[0])

            def split_lo(n):
                dve.wait_ge(hi_ready, n + 1)
                if n >= LO:
                    dve.wait_ge(piece_used, n - (LO - 1))
                nc.vector.tensor_tensor(wlo[n % LO][:, :, :], w_ring[n % RING][:, :, :],
                                        whi[n % HI][:, :, :].bitcast(f32), ALU.subtract).then_inc(lo_ready, 1)

            def split_next(m):
                if m + LO < TOTAL:
                    split_lo(m + LO)

            def norm_rstd(nm):
                dve.wait_ge(*nm.at("squares", NT))
                link(nc.vector.tensor_scalar(ms[:, :], ss[:, :], 1.0 / C, RMS_EPS, ALU.mult, ALU.add))
                nc.vector.reciprocal(rec[:, :], ms[:, :]).then_inc(norm_sems["recip"], 1)
                dve.wait_ge(*nm.at("rstd", 1))

            def norm_scale(nm):
                norm_rstd(nm)
                for j in range(NT):
                    nc.vector.tensor_scalar(xs[:, j, :], h[:, j, :], rstd[:, j:j + 1], None, ALU.mult
                                            ).then_inc(norm_sems["scaled"], 1)

            def norm(nm):
                norm_scale(nm)
                for i, (col, hi, lo) in enumerate(nm.gains):
                    for bank in range(NC // 2):
                        dve.wait_ge(*nm.at("hi", i * (NC // 2) + bank + 1))
                        for b in (2 * bank, 2 * bank + 1):
                            m = nc.vector.scalar_tensor_tensor(
                                out=lo[:, b, :], in0=PS[:, 4 + bank, (b % 2) * T:(b % 2 + 1) * T],
                                scalar=cols[:, col + b:col + b + 1], in1=hi[:, b, :].bitcast(f32),
                                op0=ALU.mult, op1=ALU.subtract)
                        m.then_inc(norm_sems["lo"], 1)

            def residual(ph, m, halves=(0, 1)):
                dve.wait_ge(piece_used, m + 1)
                for j in range(NT):
                    for a in halves:
                        sl = h[:, j, a * HALF:(a + 1) * HALF]
                        nc.vector.tensor_tensor(sl, PS[:, 2 * j + a, :], sl, ALU.add).then_inc(h_done[ph], 1)

            def moe_phase(k):
                s, nm = moe_sems, norms[f"moe{k}"]
                for i in range(EG):
                    m = nc.vector.memset(rev[:, i:i + 1], float(EG - i))
                link(m)
                norm_rstd(nm)
                dve.wait_ge(s["ffn_row"], 16 * (k + 1))
                for j in range(NT):
                    nc.vector.scalar_tensor_tensor(out=xs[:, j, :], in0=h[:, j, :], scalar=rstd[:, j:j + 1],
                                                   in1=ffn_row[:, :], op0=ALU.mult, op1=ALU.mult
                                                   ).then_inc(norm_sems["scaled"], 1)
                for j in range(NT):
                    dve.wait_ge(s["xt_hi"], k * PER["xt_hi"] + j + 1)
                    nc.vector.tensor_tensor(xt_lo[:, j, :], xs[:, j, :], xt_hi[:, j, :].bitcast(f32), ALU.subtract
                                            ).then_inc(s["xt_lo"], 1)
                dve.wait_ge(*nm.at("turned", 4))
                nc.vector.tensor_copy(xT[:, 4:8, :].rearrange("p (a b) t -> p a (b t)", a=2), PS[:, 6:8, :]
                                      ).then_inc(s["xT_dve"], 1)

                def bc(v, n):
                    return v.unsqueeze(2).broadcast_to([P, NT, n])

                def first_of(eq, out_):
                    link(nc.vector.tensor_tensor(eq, eq, rev[:, :].unsqueeze(1).broadcast_to([P, NT, EG]), ALU.mult))
                    link(nc.vector.tensor_reduce(r_s[:, 9, :], eq, AX.X, ALU.max))
                    link(nc.vector.tensor_tensor(out_, eq, bc(r_s[:, 9, :], EG), ALU.is_equal))

                dve.wait_ge(s["logits"], k * PER["logits"] + 1)
                link(nc.vector.tensor_tensor(lg[:, :, :], PS[:, 0, 0:NT * NR].rearrange("p (j r) -> p j r", j=NT),
                                             br[k][:, :].unsqueeze(1).broadcast_to([P, NT, NR]), ALU.add))
                link(nc.vector.tensor_reduce(r_s[:, 0, :], lg[:, :, 0:G], AX.X, ALU.max))
                nc.vector.tensor_tensor(r_gs[:, :, :], lg[:, :, 0:G], bc(r_s[:, 0, :], G), ALU.subtract
                                        ).then_inc(s["gs"], 1)
                dve.wait_ge(s["gs"], k * PER["gs"] + 1)
                link(nc.vector.tensor_scalar(r_eq[:, :, :], r_gs[:, :, :], 0.0, None, ALU.is_equal))
                first_of(r_eq[:, :, :], r_fg[:, :, :])
                nc.vector.tensor_copy(groups[:, :, 0:G], r_fg[:, :, :]).then_inc(s["groups"], 1)
                link(nc.vector.tensor_tensor(
                    r_ilm[:, :, :, :], lg[:, :, G:NR].rearrange("p j (g e) -> p j g e", g=G),
                    r_fg[:, :, :].unsqueeze(3).broadcast_to([P, NT, G, EG]), ALU.mult))
                link(nc.vector.tensor_reduce(r_il[:, :, :], r_ilm[:, :, :, :].rearrange("p j g e -> p j e g"),
                                             AX.X, ALU.add))
                link(nc.vector.tensor_reduce(r_s[:, 2, :], r_il[:, :, :], AX.X, ALU.max))
                link(nc.vector.tensor_tensor(r_d[:, :, :], r_il[:, :, :], bc(r_s[:, 2, :], EG), ALU.subtract))
                link(nc.vector.tensor_scalar(r_f1[:, :, :], r_d[:, :, :], 0.0, None, ALU.is_equal))
                first_of(r_f1[:, :, :], r_f1[:, :, :])
                link(nc.vector.scalar_tensor_tensor(out=r_d2[:, :, :], in0=r_f1[:, :, :], scalar=-3.0e38,
                                                    in1=r_d[:, :, :], op0=ALU.mult, op1=ALU.add))
                nc.vector.tensor_reduce(r_s[:, 3, :], r_d2[:, :, :], AX.X, ALU.max).then_inc(s["m2"], 1)
                dve.wait_ge(s["m2"], k * PER["m2"] + 1)
                link(nc.vector.tensor_tensor(r_f2[:, :, :], r_d2[:, :, :], bc(r_s[:, 3, :], EG), ALU.is_equal))
                first_of(r_f2[:, :, :], r_f2[:, :, :])
                dve.wait_ge(s["places"], k * PER["places"] + 1)
                link(nc.vector.tensor_copy(place_in[:, :, 0:G],
                                           PS[:, 1, 0:NT * G].rearrange("p (j g) -> p j g", j=NT)))
                pick_group(k, 0)
                link(nc.vector.tensor_reduce(n_max[:, :], PS[:, 1, NT * G:(NT + 1) * G], AX.X, ALU.max))
                nc.vector.tensor_copy(n_max_int[:, :], n_max[:, :]).then_inc(s["n_max"], 1)
                dve.wait_ge(s["eg"], k * PER["eg"] + 1)
                link(nc.vector.tensor_reduce(r_s[:, 1, :], r_eg[:, :, :], AX.X, ALU.add))
                dve.wait_ge(s["e2"], k * PER["e2"] + 1)
                link(nc.vector.tensor_scalar(r_s[:, 5, :], r_s[:, 4, :], 1.0, None, ALU.add))
                link(nc.vector.tensor_tensor(r_s[:, 6, :], r_s[:, 5, :], r_s[:, 1, :], ALU.mult))
                link(nc.vector.reciprocal(r_s[:, 7, :], r_s[:, 6, :]))
                link(nc.vector.tensor_tensor(r_s[:, 8, :], r_s[:, 7, :], r_s[:, 4, :], ALU.mult))
                link(nc.vector.tensor_tensor(r_f1[:, :, :], r_f1[:, :, :], bc(r_s[:, 7, :], EG), ALU.mult))
                link(nc.vector.tensor_tensor(r_f2[:, :, :], r_f2[:, :, :], bc(r_s[:, 8, :], EG), ALU.mult))
                link(nc.vector.tensor_tensor(r_f1[:, :, :], r_f1[:, :, :], r_f2[:, :, :], ALU.add))
                nc.vector.tensor_tensor(gates[:, :, :].rearrange("p j (g e) -> p j g e", g=G),
                                        r_fg[:, :, :].unsqueeze(3).broadcast_to([P, NT, G, EG]),
                                        r_f1[:, :, :].unsqueeze(2).broadcast_to([P, NT, G, EG]), ALU.mult
                                        ).then_inc(s["gates"], 1)
                dve.wait_ge(s["gates"], k * PER["gates"] + 1)
                link(nc.vector.tensor_copy(gates_hi[:, :, :], gates[:, :, :]))
                nc.vector.tensor_tensor(gates_lo[:, :, :], gates[:, :, :], gates_hi[:, :, :].bitcast(f32),
                                        ALU.subtract).then_inc(s["gates_parts"], 1)
                most = dve.value_load(n_max_int[0:1, 0:1])
                with dve.If(most < P + 1):
                    packed_experts(k)
                with dve.Else():
                    all_experts(k)

            def pick_group(k, g):
                def column(t, j):
                    return t[:, j, g:g + 1] if isinstance(g, int) else t[:, j, bass.ds(g, 1)]

                for j in range(NT):
                    m = nc.vector.tensor_scalar(pick[:, j, :], slot_no[:, :], column(place_in, j),
                                                column(groups, j), ALU.is_equal, ALU.mult)
                m.then_inc(packed_sems[k]["pick"], 1)

            def split_lo_in_loop(g, n):
                dve.wait_ge(hi_ready, g * (3 * EG) + (n + 1))
                dve.wait_ge(piece_used, g * (3 * EG) + (n - (LO - 1)))
                nc.vector.tensor_tensor(wlo[n % LO][:, :, :], w_ring[n % RING][:, :, :],
                                        whi[n % HI][:, :, :].bitcast(f32), ALU.subtract).then_inc(lo_ready, 1)

            def split_ahead(g, n):
                if isinstance(g, int):
                    split_next(g * (3 * EG) + n)
                else:
                    split_lo_in_loop(g, n + LO)

            def packed_experts(k):
                s, nb = packed_sems[k], base[f"moe{k}"]

                def xe(g):
                    dve.wait_ge(*ex(k, "x_hi", g + 1))
                    if not (isinstance(g, int) and g == 0):
                        dve.wait_ge(*ex(k, "hact", g * (2 * EG)))
                    dve.wait_ge(s["slot_gates"], g + 1)
                    nc.vector.tensor_copy(slot_gates[:, :], PS[:, 6, 256:256 + E])
                    nc.vector.tensor_tensor(xe_lo[:, :, :].rearrange("p (a b) t -> p a (b t)", a=2), PS[:, 2:4, :],
                                            xe_hi[:, :, :].bitcast(f32).rearrange("p (a b) t -> p a (b t)", a=2),
                                            ALU.subtract).then_inc(expert_sems["x_lo"], 1)
                    dve.wait_ge(*ex(k, "x_lo", g + 1))

                def gated(e):
                    dve.wait_ge(*ex(k, "silu", e * 2 + 2))
                    gate = slot_gates[:, e:e + 1] if isinstance(e, int) else slot_gates[:, bass.ds(e, 1)]
                    nc.vector.scalar_tensor_tensor(out=hact_s[:, :], in0=silu_s[:, :], scalar=gate,
                                                   in1=PS[:, 4, F:2 * F], op0=ALU.mult, op1=ALU.mult
                                                   ).then_inc(expert_sems["hact"], 2)

                def h_lo(done):
                    dve.wait_ge(*ex(k, "hT_hi", done))
                    nc.vector.tensor_tensor(hs_lo[:, :, :].rearrange("p f t -> p (f t)"), PS[:, 5, 0:NF * P],
                                            hs_hi[:, :, :].bitcast(f32).rearrange("p f t -> p (f t)"), ALU.subtract
                                            ).then_inc(expert_sems["hT_lo"], 1)

                def y_part(done):
                    dve.wait_ge(s["y_hi"], done)
                    nc.vector.tensor_tensor(y_lo[:, :, :], PS[:, 0:2, :], y_hi[:, :, :].bitcast(f32), ALU.subtract
                                            ).then_inc(s["y_lo"], 1)

                def add_rows(g, j, signal):
                    for a in range(2):
                        dve.wait_ge(s["combined"], g * 4 + (2 * j + a + 1))
                        sl = h[:, j, a * HALF:(a + 1) * HALF]
                        nc.vector.tensor_tensor(sl, PS[:, 6 + a, :], sl, ALU.add).then_inc(signal, 1)

                def group(g):
                    known = isinstance(g, int)
                    for i in range(EG):
                        e, n0 = g * EG + i, nb - 1 + 3 * i
                        if known and e == 0:
                            split_next(nb)
                            gated(0)
                            split_next(nb + 1)
                            continue
                        h_lo(e)
                        if i == 3:
                            if not is_last(g):
                                dve.wait_ge(s["pt_psum"], g + 1)
                                pick_group(k, g + 1)
                        split_ahead(g, n0)
                        gated(e)
                        split_ahead(g, n0 + 1)
                        if i == 3 and not is_last(g):
                            xe(g + 1)
                        split_ahead(g, n0 + 2)
                        if not (known and g == 0):
                            if i == 0:
                                y_part(g)
                            if i in (1, 2):
                                add_rows(g - 1, i - 1, s["added"])

                xe(0)
                group(0)
                with dve.Fori(1, G - 1) as g:
                    group(g)
                group(G - 1)
                h_lo(E)
                for a in range(2):
                    dve.wait_ge(s["y_hi"], G + a)
                    nc.vector.tensor_tensor(y_lo[:, a, :], PS[:, a, :], y_hi[:, a, :].bitcast(f32), ALU.subtract
                                            ).then_inc(s["y_lo"], 1)
                for a in range(2):
                    for j in range(NT):
                        dve.wait_ge(s["combined"], (G - 1) * 4 + 2 * a + j + 1)
                        sl = h[:, j, a * HALF:(a + 1) * HALF]
                        nc.vector.tensor_tensor(sl, PS[:, 4 + 2 * j + a, :], sl, ALU.add
                                                ).then_inc(h_done[f"moe{k}"], 1)
                split_next(nb + 3 * E - 1)

            def all_experts(k):
                nb = base[f"moe{k}"]
                dve.wait_ge(*ex(k, "x_hi", G))
                nc.vector.tensor_tensor(xa_lo[:, :, :], xT[:, :, :], xa_hi[:, :, :].bitcast(f32), ALU.subtract
                                        ).then_inc(expert_sems["x_lo"], G)

                def gated(e):
                    for j in range(NT):
                        dve.wait_ge(*ex(k, "silu", e * 2 + (j + 1)))
                        g = gates[:, j, e:e + 1] if isinstance(e, int) else gates[:, j, bass.ds(e, 1)]
                        nc.vector.scalar_tensor_tensor(out=hact[:, j, :], in0=silu_g[:, j, :], scalar=g,
                                                       in1=PS[:, 4 + j, F:2 * F], op0=ALU.mult, op1=ALU.mult
                                                       ).then_inc(expert_sems["hact"], 1)

                def h_lo(e):
                    dve.wait_ge(*ex(k, "hT_hi", e))
                    nc.vector.tensor_tensor(hT_lo[:, :, :], PS[:, 6, :].rearrange("p (f t) -> p f t", f=NF),
                                            hT_hi[:, :, :].bitcast(f32), ALU.subtract
                                            ).then_inc(expert_sems["hT_lo"], 1)

                def group(g):
                    for i in range(EG):
                        e, n0 = g * EG + i, nb - 1 + 3 * i
                        if isinstance(g, int) and e == 0:
                            split_next(nb)
                            gated(0)
                            split_next(nb + 1)
                            continue
                        h_lo(e)
                        split_ahead(g, n0)
                        gated(e)
                        split_ahead(g, n0 + 1)
                        split_ahead(g, n0 + 2)

                group(0)
                with dve.Fori(1, G - 1) as g:
                    group(g)
                group(G - 1)
                h_lo(E)
                residual(f"moe{k}", nb + 3 * E - 1)
                split_next(nb + 3 * E - 1)

            def rwkv_phase():
                nm = norms["rwkv"]
                nc.vector.memset(zw[LW:LW + 1, :], 1.0)
                nc.vector.memset(za[LW:LW + 1, :], 1.0).then_inc(rw["zones"], 1)
                norm_scale(nm)
                dve.wait_ge(cols_psum, 1)
                nc.vector.tensor_copy(cols[:, :], PS[:, 0, 0:n_rows]).then_inc(cols_ready, 1)
                dve.wait_ge(cols_ready, 1)
                def shift(b):
                    nc.vector.tensor_scalar(dxT[:, b, 0:1], hnT[:, b, 0:1], -1.0, None, ALU.mult)
                    link(nc.vector.tensor_tensor(dxT[:, b, 1:T], hnT[:, b, 0:T - 1], hnT[:, b, 1:T], ALU.subtract))

                def mix(i, blocks=range(NC)):
                    for b in blocks:
                        col = 40 + NC * MIX_ROW[i] + b
                        m = nc.vector.scalar_tensor_tensor(out=mixed_[i][:, b, :], in0=dxT[:, b, :],
                                                           scalar=cols[:, col:col + 1], in1=hnT[:, b, :],
                                                           op0=ALU.mult, op1=ALU.add)
                    m.then_inc(rw["mixed"], 1)

                dve.wait_ge(rw["hn_act"], 2)
                shift(slice(0, 4))
                mix(0, range(4))
                for bank in (2, 3):
                    dve.wait_ge(*nm.at("turned", bank + 1))
                    for b in (2 * bank, 2 * bank + 1):
                        m = nc.vector.tensor_scalar(hnT[:, b, :], PS[:, 4 + bank, (b % 2) * T:(b % 2 + 1) * T],
                                                    cols[:, b:b + 1], None, ALU.mult)
                    m.then_inc(rw["hn_dve"], 1)
                dve.wait_ge(rw["hn_dve"], 2)

                def x_lo(i, dst_hi, dst, n, halves=(0, 1)):
                    for g in halves:
                        dve.wait_ge(rw["x_hi"], 2 * n + g + 1)
                        b = slice(4 * g, 4 * g + 4)
                        nc.vector.tensor_tensor(dst[:, b, :], mixed_[i][:, b, :], dst_hi[:, b, :].bitcast(f32),
                                                ALU.subtract).then_inc(rw["x_lo"], 1)

                split_lo(0)
                x_lo(0, xa_hi, xa_lo, 0, (0,))
                shift(slice(4, 8))
                mix(0, range(4, 8))
                x_lo(0, xa_hi, xa_lo, 0, (1,))
                split_lo(1)
                split_next(0)
                mix(1)
                split_next(1)
                mix(2)
                dve.wait_ge(rw["x_lo"], 2)
                mix(3)
                split_next(2)
                split_next(3)
                dve.wait_ge(rw["lora1"], 1)
                mix(4)
                x_lo(4, xb_hi, xb_lo, 1)
                dve.wait_ge(rw["lora1"], 2)
                mix(5)
                x_lo(5, xa_hi, xa_lo, 2)

                def half(t, a):
                    return t[:, :, a * HALF:(a + 1) * HALF]

                def row(t, a):
                    return t[:, a * HALF:(a + 1) * HALF].unsqueeze(1).broadcast_to([P, NT, HALF])

                dve.wait_ge(rw["rows_loaded"], 32)
                dve.wait_ge(rw["lora1"], 3)
                for a in range(2):
                    dve.wait_ge(rw["k"], a + 1)
                    nc.vector.tensor_tensor(half(kk, a), half(k_s, a), row(kk_row, a), ALU.mult
                                            ).then_inc(rw["kk0"], 1)
                split_next(4)
                for a in range(2):
                    dve.wait_ge(rw["sq"], a + 1)
                    if a:
                        dve.wait_ge(rw["inv"], a)
                    link(nc.vector.tensor_reduce(n2[:, :, :], tmp[:, :, :].rearrange("p j (h n) -> p j h n", n=HD),
                                                 AX.X, ALU.add))
                    link(nc.vector.tensor_scalar(n2[:, :, :], n2[:, :, :], 1e-24, None, ALU.max))
                    nc.vector.reciprocal(n2[:, :, :], n2[:, :, :]).then_inc(rw["n2"], 1)
                    dve.wait_ge(rw["inv"], a + 1)
                    for j in range(NT):
                        v = kk[:, j, a * HALF:(a + 1) * HALF].rearrange("p (h n) -> p h n", n=HD)
                        m = nc.vector.tensor_tensor(v, v, n2i[:, j, :].unsqueeze(2).broadcast_to([P, HH, HD]),
                                                    ALU.mult)
                    link(m)
                    if a == 0:
                        split_next(5)
                dve.wait_ge(rw["a"], NT)
                for a in range(2):
                    if a:
                        dve.wait_ge(rw["kmod"], a)
                    link(nc.vector.scalar_tensor_tensor(out=tmp[:, :, :], in0=half(a_s, a), scalar=-1.0,
                                                        in1=row(ka_row, a), op0=ALU.add, op1=ALU.mult))
                    nc.vector.scalar_tensor_tensor(out=half(k_s, a), in0=tmp[:, :, :], scalar=1.0, in1=half(k_s, a),
                                                   op0=ALU.add, op1=ALU.mult).then_inc(rw["kmod"], 1)
                    link(nc.vector.tensor_tensor(half(a_s, a), half(kk, a), half(a_s, a), ALU.mult))
                    if a == 0:
                        split_next(6)
                split_next(7)
                split_next(8)
                split_next(9)
                for a in range(2):
                    dve.wait_ge(rw["rk"], a + 1)
                    nc.vector.tensor_reduce(bonus[:, :, a * HH:(a + 1) * HH],
                                            yb[:, :, :].rearrange("p j (h n) -> p j h n", n=HD), AX.X, ALU.add
                                            ).then_inc(rw["bonus"], 1)
                    dve.wait_ge(rw["decay"], 3 * a + 1)
                    nc.vector.tensor_tensor(half(r_s_, a), half(r_s_, a), e0[:, :, :], ALU.mult
                                            ).then_inc(rw["decay_used"], 1)
                    dve.wait_ge(rw["decay"], 3 * a + 2)
                    nc.vector.tensor_tensor(half(a_s, a), half(a_s, a), e1[:, :, :], ALU.mult)
                    nc.vector.tensor_tensor(half(k_s, a), half(k_s, a), e1[:, :, :], ALU.mult
                                            ).then_inc(rw["decay_used"], 1)
                    dve.wait_ge(rw["decay"], 3 * a + 3)
                    nc.vector.scalar_tensor_tensor(out=half(kk, a), in0=half(kk, a), scalar=-1.0, in1=e0[:, :, :],
                                                   op0=ALU.mult, op1=ALU.mult).then_inc(rw["decay_used"], 1)

                def by_head(m):
                    return m[:, :].unsqueeze(1).broadcast_to([P, 4, P])

                def heads(bank):
                    return PS[:, bank, :].rearrange("p (h s) -> p h s", s=P)

                dve.wait_ge(rw["masks"], 1)
                for a in range(2):
                    dve.wait_ge(rw["turned"], 4 * a + 3)
                    nc.vector.tensor_copy(BT[:, :, :].rearrange("p (a b) t -> p a (b t)", a=2), PS[:, 2:4, :]
                                          ).then_inc(rw["t_dve"], 1)
                    dve.wait_ge(rw["turned"], 4 * a + 4)
                    nc.vector.tensor_copy(RT[:, :, :].rearrange("p (a b) t -> p a (b t)", a=2), PS[:, 6:8, :]
                                          ).then_inc(rw["t_dve"], 1)
                    for q in (2 * a, 2 * a + 1):
                        for j in range(NT):
                            dve.wait_ge(rw["m_psum"], 8 * q + 4 * j + 1)
                            link(nc.vector.scalar_tensor_tensor(out=NT_[j][:, :, :], in0=heads(4 * j), scalar=-1.0,
                                                                in1=by_head(before_t), op0=ALU.mult, op1=ALU.mult))
                            nc.vector.tensor_tensor(NT_[j][:, :, :], NT_[j][:, :, :], by_head(ident), ALU.add
                                                    ).then_inc(rw["m_out"], 1)
                            for i, (dst, mask) in enumerate(((AakT[j], before_t), (ArbT[q % 2][j], to_t),
                                                             (ArkT[q % 2][j], to_t))):
                                dve.wait_ge(rw["m_psum"], 8 * q + 4 * j + 2 + i)
                                nc.vector.tensor_tensor(dst[:, :, :], heads(4 * j + 1 + i), by_head(mask), ALU.mult
                                                        ).then_inc(rw["m_out"], 1)
                            dve.wait_ge(rw["m_out"], 8 * q + 4 * j + 1)
                            nc.vector.tensor_tensor(XT[j][:, :, :], NT_[j][:, :, :], by_head(level0T), ALU.mult
                                                    ).then_inc(rw["x1"], 1)
                        for l in range(LEVELS):
                            for j in range(NT):
                                dve.wait_ge(rw["w_psum"], 12 * q + 2 * l + j + 1)
                                dst = X[j] if l == 0 else W_[j]
                                nc.vector.tensor_tensor(dst[:, :, :], heads(j), by_head(level[l]), ALU.mult
                                                        ).then_inc(rw["w_out"], 1)
                        for j in range(NT):
                            dve.wait_ge(rw["u0_psum"], 2 * q + j + 1)
                            nc.vector.tensor_copy(U[:, j, q % 2::2, :],
                                                  PS[:, 6 + j, 0:256].rearrange("p (h n) -> p h n", n=HD)
                                                  ).then_inc(rw["u0_out"], 1)
                    if a == 0:
                        for c in range(4):
                            m = nc.vector.memset(S[c][:, :, :], 0.0)
                        link(m)
                    dve.wait_ge(rw["cd"], 1)
                    for c in range(4):
                        j, p0 = c // 2, CH * (c % 2)
                        if c:
                            dve.wait_ge(rw["u_psum"], 3 * a + c)
                            u = U[p0:p0 + CH, j, :, :]
                            nc.vector.tensor_tensor(u, u, PS[p0:p0 + CH, 0, :].rearrange("p (h n) -> p h n", n=HD),
                                                    ALU.add).then_inc(rw["u_out"], 1)
                        if c < 3:
                            dve.wait_ge(rw["s_psum"], 3 * a + c + 1)
                            blocks = [(slice(o, o + HD), slice(None), slice(o, o + HD)) for o in (0, HD)]
                            sums = PS[:, 1, :].rearrange("p (b n) -> p b n", n=2 * HD)
                            if c:
                                for blk in blocks:
                                    m = nc.vector.tensor_tensor(S[c + 1][blk], S[c][blk], sums[blk], ALU.add)
                                link(m)
                                sums = S[c + 1]
                            for blk in blocks:
                                m = nc.vector.tensor_tensor(
                                    S[c + 1][blk], sums[blk],
                                    chunk_decay[blk[0], 4 * a:4 * a + 4, c:c + 1].broadcast_to([HD, 4, HD]), ALU.mult)
                            m.then_inc(rw["s_out"], 1)
                    dve.wait_ge(rw["late_loaded"], 64)
                    for j in range(NT):
                        i = 2 * a + j
                        y = yb[:, j, :]
                        y3 = y.rearrange("p (h n) -> p h n", n=HD)
                        dve.wait_ge(rw["y_psum"], i + 1)
                        out_y = PS[:, 2 + j, :].rearrange("p (h n) -> p h n", n=HD)
                        link(nc.vector.tensor_reduce(y_m[:, 0, :], out_y, AX.X, ALU.add))
                        link(nc.vector.tensor_scalar(y_m[:, 1, :], y_m[:, 0, :], 1.0 / HD, None, ALU.mult))
                        nc.vector.tensor_tensor(y3, out_y, y_m[:, 1, :].unsqueeze(2).broadcast_to([P, HH, HD]),
                                                ALU.subtract).then_inc(rw["y_cent"], 1)
                        dve.wait_ge(rw["y_sq"], i + 1)
                        link(nc.vector.tensor_reduce(y_m[:, 0, :], y_sq[:, :].rearrange("p (h n) -> p h n", n=HD),
                                                     AX.X, ALU.add))
                        link(nc.vector.tensor_scalar(y_m[:, 1, :], y_m[:, 0, :], 1.0 / HD, GN_EPS, ALU.mult, ALU.add))
                        nc.vector.reciprocal(y_m[:, 2, :], y_m[:, 1, :]).then_inc(rw["y_var"], 1)
                        dve.wait_ge(rw["y_std"], i + 1)
                        link(nc.vector.tensor_tensor(y3, y3, y_m[:, 3, :].unsqueeze(2).broadcast_to([P, HH, HD]),
                                                     ALU.mult))
                        link(nc.vector.tensor_tensor(y, y, lnw_row[:, a * HALF:(a + 1) * HALF], ALU.mult))
                        dve.wait_ge(rw["vb"], i + 1)
                        nc.vector.tensor_tensor(y, y, vb[:, :], ALU.add).then_inc(rw["vb_used"], 1)
                        dve.wait_ge(rw["vb_used"], i + 1)
                        dve.wait_ge(rw["g_psum"], i + 1)
                        nc.vector.tensor_tensor(z_tok[:, j, a * HALF:(a + 1) * HALF], y, PS[:, 6 + j, :], ALU.mult
                                                ).then_inc(rw["z_tok"], 1)
                for i in range(4):
                    dve.wait_ge(rw["zt_hi"], i + 1)
                    a, j = i // 2, i % 2
                    dst = (slice(None), slice(4 * a, 4 * a + 4), slice(j * P, (j + 1) * P))
                    nc.vector.tensor_tensor(xa_lo[dst], PS[:, 4 + i, :].rearrange("p (b t) -> p b t", t=P),
                                            xa_hi[dst].bitcast(f32), ALU.subtract).then_inc(rw["zt_lo"], 1)
                for m in range(10, 12):
                    split_next(m)
                dve.wait_ge(rw["x_again"], 32)
                for m in range(12, 16):
                    if m % 2:
                        residual("rwkv", m, (m // 2 % 2,))
                    split_next(m)

            def attn_phase():
                s, nb = at_, base["attn"]
                norm(norms["attn"])
                for m in range(12):
                    if m in (5, 7):
                        dve.wait_ge(piece_used, nb + m + 1)
                        n = (m - 4) // 2
                        nc.vector.tensor_copy(v_att[:, :, n * HALF:(n + 1) * HALF], PS[:, 4 + 2 * n:6 + 2 * n, :]
                                              ).then_inc(s["v"], 1)
                    if m in (9, 11):
                        dve.wait_ge(piece_used, nb + m + 1)
                        n = (m - 8) // 2
                        nc.vector.tensor_scalar(qT[:, 4 * n:4 * n + 4, :].rearrange("p (a b) t -> p a (b t)", a=2),
                                                PS[:, 2 * n:2 * n + 2, :], HD ** -0.5, None, ALU.mult
                                                ).then_inc(s["q"], 1)
                    split_next(nb + m)

                def diag(v):
                    return v.rearrange("p h (b t) -> p h b t", t=P)[:, :, 0:3:2, :]

                mask = causal[:, :].unsqueeze(1).unsqueeze(1).broadcast_to([P, 2, 2, P])

                def z_out(pr):
                    dve.wait_ge(s["z_psum"], pr + 1)
                    zb = 2 * (pr % 2)
                    nc.vector.tensor_tensor(diag(z_sb[pr % 3][:, :, :]), diag(PS[:, zb:zb + 2, 0:ZW]), mask, ALU.mult)
                    nc.vector.tensor_copy(z_sb[pr % 3][:, :, P:2 * P], PS[:, zb:zb + 2, P:2 * P]).then_inc(s["z"], 1)

                def softplus(pr):
                    dve.wait_ge(s["ln"], pr + 1)
                    if pr >= 2:
                        dve.wait_ge(s["cs_psum"], pr - 1)
                    u = u_sp[pr % 2][:, :, :]
                    link(nc.vector.scalar_tensor_tensor(out=u, in0=z_sb[pr % 3][:, :, :], scalar=0.0,
                                                        in1=z_ln[pr % 2][:, :, :], op0=ALU.max, op1=ALU.add))
                    nc.vector.tensor_tensor(diag(u), diag(u), mask, ALU.mult).then_inc(s["u"], 1)

                def log_att(pr):
                    dve.wait_ge(s["cs_psum"], pr + 1)
                    if pr >= 2:
                        dve.wait_ge(s["exp"], pr - 1)
                    nc.vector.tensor_tensor(log_a[pr % 2][:, :, :], z_sb[pr % 3][:, :, :], PS[:, 4:6, 0:ZW],
                                            ALU.subtract).then_inc(s["log_a"], 1)

                def o_lo(pr):
                    dve.wait_ge(s["o_hi"], pr + 1)
                    nc.vector.tensor_tensor(xa_lo[:, pr, :], PS[:, 6 + pr % 2, 0:T], xa_hi[:, pr, :].bitcast(f32),
                                            ALU.subtract).then_inc(s["o_lo"], 1)

                z_out(0)
                z_out(1)
                softplus(0)
                for i in range(NC):
                    if i + 2 < NC:
                        z_out(i + 2)
                    log_att(i)
                    if i + 1 < NC:
                        softplus(i + 1)
                    if i >= 1:
                        o_lo(i - 1)
                o_lo(NC - 1)
                for m in range(12, 16):
                    if m % 2:
                        residual("attn", nb + m, (m // 2 % 2,))
                    split_next(nb + m)

            for ph in PHASES:
                if ph.startswith("moe"):
                    moe_phase(int(ph[3]))
                if ph == "attn":
                    attn_phase()
                if ph == "rwkv":
                    rwkv_phase()
            norm_rstd(norms["final"])
            dve.wait_ge(gain_loaded, 16)
            for j in range(NT):
                for a in range(2):
                    c = slice(a * HALF, (a + 1) * HALF)
                    nc.vector.scalar_tensor_tensor(out=xs[:, j, c], in0=h[:, j, c], scalar=rstd[:, j:j + 1],
                                                   in1=gain_row[:, c], op0=ALU.mult, op1=ALU.mult
                                                   ).then_inc(final_ready, 1)

        @block.tensor
        def _(pe):
            pe.wait_ge(params_loaded, 64)
            pe.wait_ge(ident_ready, 5)
            nc.tensor.transpose(PS[:, 0, 0:n_rows], prow[:, :], ident[0:n_rows, 0:n_rows]).then_inc(cols_psum, 1)
            pe.wait_ge(cols_ready, 1)

            def stay_warm(n, bank):
                for _ in range(n):
                    nc.tensor.matmul(PS[:, bank, 0:P], ident[:, :], ident[:, :], start=True, stop=True)

            def norm(nm):
                if nm is not norms[PHASES[0]]:
                    pe.wait_ge(nm.h_ready[0], nm.h_ready[1][0])
                    stay_warm(22, 2)
                for j in range(NT):
                    pe.wait_ge(*nm.at("scaled", j + 1))
                    for b in range(NC):
                        m = nc.tensor.transpose(PS[:, 4 + b // 2, (b % 2) * T + j * P:(b % 2) * T + (j + 1) * P],
                                                xs[:, j, b * P:(b + 1) * P], ident[:, :])
                        if j == NT - 1 and b % 2:
                            m.then_inc(norm_sems["turned"], 1)

            def three(dst, xh, xl, wh, wl, start, stop):
                nc.tensor.matmul(dst, xh, wh, start=start, stop=False)
                nc.tensor.matmul(dst, xh, wl, start=False, stop=False)
                return nc.tensor.matmul(dst, xl, wh, start=False, stop=stop)

            def token_major(n, xh, xl, bank):
                pe.wait_ge(lo_ready, n + 1)
                g = dense_pieces[n][2]
                for j in range(NT):
                    for i in range(4):
                        b = 4 * g + i
                        m = three(PS[:, bank(j), :], xh[:, b, j * P:(j + 1) * P], xl[:, b, j * P:(j + 1) * P],
                                  whi[n % HI][:, i, :], wlo[n % LO][:, i, :], b == 0, b == NC - 1)
                m.then_inc(piece_used, 1)

            def channel_major(n, xh, xl, bank0):
                pe.wait_ge(lo_ready, n + 1)
                g = dense_pieces[n][2]
                for co in range(4):
                    dst = PS[:, bank0 + co // 2, (co % 2) * T:(co % 2 + 1) * T]
                    for i in range(4):
                        b = 4 * g + i
                        wh = whi[n % HI][:, i, co * P:(co + 1) * P]
                        wl = wlo[n % LO][:, i, co * P:(co + 1) * P]
                        m = three(dst, wh, wl, xh[:, b, :], xl[:, b, :], b == 0 and co % 2 == 0,
                                  b == NC - 1 and co % 2 == 1)
                m.then_inc(piece_used, 1)

            def rwkv_phase():
                norm(norms["rwkv"])
                for m in range(4):
                    pe.wait_ge(rw["x_lo"], min(m + 1, 2))
                    token_major(m, xa_hi, xa_lo, lambda j: 2 * (m // 2) + j)
                pe.wait_ge(rw["lora_loaded"], 16 * 7)
                for i, (bank, c0, n) in enumerate(((4, 0, LW), (5, LW, LW), (6, 2 * LW, P), (7, 2 * LW + P, LG - P))):
                    pe.wait_ge(rw["mixed"], min(i, 2) + 3)
                    if i == 0:
                        pe.wait_ge(rw["hn_act"], 2)
                        pe.wait_ge(rw["hn_dve"], 2)
                    src = mixed_[1 + min(i, 2)]
                    for b in range(NC):
                        mm = nc.tensor.matmul(PS[0:n, bank, 0:T], lora1[:, b, c0:c0 + n], src[:, b, :],
                                              start=b == 0, stop=b == NC - 1)
                    if i != 2:
                        mm.then_inc(rw["lora1"], 1)
                pe.wait_ge(rw["zones"], 1)
                for i, (zz, w2) in enumerate(((zw, w2x), (za, a2x))):
                    if i == 0:
                        pe.wait_ge(rw["z"], 1)
                        pe.wait_ge(rw["k"], 2)
                    else:
                        pe.wait_ge(rw["z"], 4)
                    for j in range(NT):
                        for a in range(2):
                            mm = nc.tensor.matmul(PS[:, 4 * i + 2 * j + a, :], zz[:, j * P:(j + 1) * P],
                                                  w2[:, a * HALF:(a + 1) * HALF], start=True, stop=True)
                    mm.then_inc(rw["lora2"], 1)
                pe.wait_ge(rw["sig"], NT)
                pe.wait_ge(rw["x_lo"], 4)
                pe.wait_ge(rw["masks"], 1)
                for m in range(4, 8):
                    token_major(m, xb_hi, xb_lo, lambda j: 2 * ((m - 4) // 2) + j)

                def cumulate(a):
                    for i, mask in enumerate((to_t, before_t)):
                        for j in range(NT):
                            mm = nc.tensor.matmul(PS[:, 4 + 2 * i + j, :], mask[:, :],
                                                  sig[:, j, a * HALF:(a + 1) * HALF], start=True, stop=True)
                    mm.then_inc(rw["cum"], 1)

                pe.wait_ge(rw["a"], NT)
                cumulate(0)
                pe.wait_ge(rw["x_lo"], 6)
                for m in range(8, 12):
                    pe.wait_ge(rw["r"], (m - 8) // 2 + 1)
                    token_major(m, xa_hi, xa_lo, lambda j: 2 * ((m - 8) // 2) + j)
                pe.wait_ge(rw["decay"], 3)
                cumulate(1)
                pe.wait_ge(rw["v"], 2)
                for b in range(NC):
                    for j in range(NT):
                        mm = nc.tensor.matmul(PS[:, 0, 4 * b + 2 * j:4 * b + 2 * j + 2], sig[:, j, b * P:(b + 1) * P],
                                              in_chunk[:, :], start=True, stop=True)
                mm.then_inc(rw["cd_psum"], 1)
                stay_warm(8, 2)
                pe.wait_ge(rw["cd"], 1)
                pe.wait_ge(rw["decay"], 6)

                for a in range(2):
                    pe.wait_ge(rw["decay_used"], 3 * a + 3)
                    for i, src in ((0, kk), (2, k_s), (1, a_s), (3, r_s_)):
                        if a and i == 1:
                            pe.wait_ge(rw["z_tok"], 2 * a)
                        for bl in range(4):
                            for j in range(NT):
                                mm = nc.tensor.transpose(
                                    PS[:, 2 * i + bl // 2, (bl % 2) * T + j * P:(bl % 2) * T + (j + 1) * P],
                                    src[:, j, (4 * a + bl) * P:(4 * a + bl + 1) * P], ident[:, :])
                        mm.then_inc(rw["turned"], 1)
                    pe.wait_ge(rw["t_act"], 2 * a + 1)
                    stay_warm(5, 0)
                    pe.wait_ge(rw["t_act"], 2 * a + 2)
                    pe.wait_ge(rw["t_dve"], 2 * a + 2)
                    for q in (2 * a, 2 * a + 1):
                        quad(a, q)
                    chunks(a)

                for i in range(4):
                    a, j = i // 2, i % 2
                    pe.wait_ge(rw["z_tok"], i + 1 if i < 2 else 4)
                    for bl in range(4):
                        mm = nc.tensor.transpose(PS[:, 4 + i, bl * P:(bl + 1) * P],
                                                 z_tok[:, j, (4 * a + bl) * P:(4 * a + bl + 1) * P], ident[:, :])
                    mm.then_inc(rw["zt_psum"], 1)
                stay_warm(16, 0)
                pe.wait_ge(rw["zt_lo"], 4)
                for m in range(12, 16):
                    token_major(m, xa_hi, xa_lo, lambda j: 2 * j + (m - 12) // 2)

            def quad(a, q):
                o = HD * (q % 2)
                if q % 2:
                    pe.wait_ge(rw["u0_out"], 2 * q)
                    pe.wait_ge(rw["xa_out"], 2 * q)
                for j in range(NT):
                    t = slice(j * P, (j + 1) * P)
                    for i, (left, right) in enumerate(((BT, AT), (KT, AT), (BT, RT), (KT, RT))):
                        for hd in range(4):
                            mm = nc.tensor.matmul(PS[:, 4 * j + i, hd * P:(hd + 1) * P], left[o:o + HD, hd, t],
                                                  right[o:o + HD, hd, t], start=True, stop=True)
                        mm.then_inc(rw["m_psum"], 1)
                def values(part):
                    j = part // 2
                    for hd in (2 * (part % 2), 2 * (part % 2) + 1):
                        c = (HH * a + 2 * hd + q % 2) * HD
                        mm = nc.tensor.matmul(PS[:, 6 + j, hd * HD:(hd + 1) * HD], AakT[j][:, hd, :],
                                              v_s[:, j, c:c + HD], start=True, stop=True)
                    if part % 2:
                        mm.then_inc(rw["cy_psum"], 1)

                for l in range(LEVELS):
                    for j in range(NT):
                        if l == 0:
                            pe.wait_ge(rw["m_out"], 8 * q + 8)
                        elif l == 1:
                            pe.wait_ge(rw["w_out"], 12 * q + j + 1)
                        else:
                            pe.wait_ge(rw["x_out"], 8 * q + 2 * (l - 2) + j + 1)
                        for hd in range(4):
                            dst = PS[:, j, hd * P:(hd + 1) * P]
                            if l == 0:
                                mm = nc.tensor.transpose(dst, NT_[j][:, hd, :], ident[:, :])
                            else:
                                mm = nc.tensor.matmul(dst, NT_[j][:, hd, :], X[j][:, hd, :], start=True, stop=True)
                        mm.then_inc(rw["w_psum"], 1)
                    if l == 0:
                        continue
                    for j in range(NT):
                        pe.wait_ge(rw["w_out"], 12 * q + 2 * l + j + 1)
                        if l == 1:
                            pe.wait_ge(rw["x1"], 2 * q + j + 1)
                        else:
                            pe.wait_ge(rw["xt_out"], 10 * q + 2 * (l - 2) + j + 1)
                        if l < LEVELS - 1:
                            for hd in range(4):
                                mm = nc.tensor.matmul(PS[:, 2 + j, hd * P:(hd + 1) * P], XT[j][:, hd, :],
                                                      W_[j][:, hd, :], start=True, stop=True)
                            mm.then_inc(rw["p_psum"], 1)
                        else:
                            for hd in range(4):
                                mm = nc.tensor.matmul(PS[:, 4 + j, hd * P:(hd + 1) * P], W_[j][:, hd, :],
                                                      XT[j][:, hd, :], start=True, stop=True)
                            mm.then_inc(rw["pt_psum"], 1)
                    if l < LEVELS - 1:
                        for j in range(NT):
                            if j:
                                values(l - 1)
                            pe.wait_ge(rw["x_out"], 8 * q + 2 * (l - 1) + j + 1)
                            for hd in range(4):
                                mm = nc.tensor.transpose(PS[:, 4 + j, hd * P:(hd + 1) * P], X[j][:, hd, :], ident[:, :])
                            mm.then_inc(rw["pt_psum"], 1)
                for j in range(NT):
                    pe.wait_ge(rw["xt_out"], 10 * q + 2 * (LEVELS - 2) + j + 1)
                    for hd in range(4):
                        c = (HH * a + 2 * hd + q % 2) * HD
                        mm = nc.tensor.matmul(PS[o:o + HD, 2 + j, hd * P:(hd + 1) * P],
                                              kk[:, j, c:c + HD], XT[j][:, hd, :], start=True, stop=True)
                    mm.then_inc(rw["xa_psum"], 1)
                    if j == 0:
                        stay_warm(3, 4)
                for j in range(NT):
                    pe.wait_ge(rw["cy_out"], 2 * q + j + 1)
                    for hd in range(4):
                        mm = nc.tensor.matmul(PS[:, 6 + j, hd * HD:(hd + 1) * HD], XT[j][:, hd, :],
                                              W_[j][:, hd // 2, (hd % 2) * HD:(hd % 2 + 1) * HD],
                                              start=True, stop=True)
                    mm.then_inc(rw["u0_psum"], 1)
                stay_warm(4, 4)

            def chunks(a):
                pe.wait_ge(rw["u0_out"], 4 * a + 4)
                pe.wait_ge(rw["xa_out"], 4 * a + 4)
                def gate(j):
                    c = slice(a * HALF, (a + 1) * HALF)
                    nc.tensor.matmul(PS[:, 6 + j, :], zg[:, j * P:(j + 1) * P], g2a[:, c], start=True, stop=False)
                    nc.tensor.matmul(PS[:, 6 + j, :], zg2[:, j * P:(j + 1) * P], g2b[:, c], start=False, stop=True
                                     ).then_inc(rw["g_psum"], 1)

                def outputs(j, b):
                    dst = PS[:, 2 + j, b * P:(b + 1) * P]
                    for c in (2 * j, 2 * j + 1):
                        t0 = CH * (c % 2)
                        nc.tensor.matmul(dst[t0:t0 + CH, :], RT[:, b, c * CH:(c + 1) * CH], S[c][:, b, :],
                                         start=True, stop=False)
                    for par in range(2):
                        c = (HH * a + 2 * b + par) * HD
                        own = dst[:, par * HD:(par + 1) * HD]
                        nc.tensor.matmul(own, ArkT[par][j][:, b, :], v_s[:, j, c:c + HD], start=False, stop=False)
                        mm = nc.tensor.matmul(own, ArbT[par][j][:, b, :], U[:, j, 2 * b + par, :],
                                              start=False, stop=par == 1)
                    if b == 3:
                        mm.then_inc(rw["y_psum"], 1)

                for c in range(4):
                    j, p0 = c // 2, CH * (c % 2)
                    t = slice(p0, p0 + CH)
                    if c:
                        pe.wait_ge(rw["s_out"], 3 * a + c)
                        for b in range(4):
                            mm = nc.tensor.matmul(PS[t, 0, b * P:(b + 1) * P], XaT[j][:, b, t], S[c][:, b, :],
                                                  start=True, stop=True)
                        mm.then_inc(rw["u_psum"], 1)
                        if c == 1:
                            gate(1)
                        else:
                            outputs(0, 2 * c - 3)
                            stay_warm(1, 5)
                    if c < 3:
                        if c:
                            pe.wait_ge(rw["u_out"], 3 * a + c)
                        for b in range(4):
                            dst, ch = PS[:, 1, b * P:(b + 1) * P], slice((4 * a + b) * P, (4 * a + b + 1) * P)
                            nc.tensor.matmul(dst, a_s[t, j, ch],
                                             U[t, j, 2 * b:2 * b + 2, :].rearrange("p h n -> p (h n)"),
                                             start=True, stop=False)
                            mm = nc.tensor.matmul(dst, k_s[t, j, ch], v_s[t, j, ch], start=False, stop=True)
                        mm.then_inc(rw["s_psum"], 1)
                        if c == 0:
                            pe.wait_ge(rw["late_loaded"], 64)
                            gate(0)
                        else:
                            outputs(0, 2 * c - 2)
                            stay_warm(2, 5)
                pe.wait_ge(rw["u_out"], 3 * a + 3)
                for b in range(4):
                    outputs(1, b)
                stay_warm(30 if a == 0 else 20, 5)

            def attn_phase():
                s, nb = at_, base["attn"]
                nm = norms["attn"]
                norm(nm)
                for m in range(4):
                    pe.wait_ge(*nm.at("lo", min(m + 1, 2) * NC // 4))
                    channel_major(nb + m, xa_hi, xa_lo, 2 * (m // 2))
                pe.wait_ge(*nm.at("lo", NC))
                for m in range(4, 8):
                    token_major(nb + m, xa_hi, xa_lo, lambda j: 4 + 2 * ((m - 4) // 2) + j)
                for m in range(8, 12):
                    if m % 2 == 0:
                        pe.wait_ge(s["k"], (m - 8) // 2 + 1)
                    channel_major(nb + m, xb_hi, xb_lo, 2 * ((m - 8) // 2))

                def z(pr):
                    if pr >= 2:
                        pe.wait_ge(s["z"], pr - 1)
                    for hh in range(2):
                        o = hh * HD
                        bank = 2 * (pr % 2) + hh
                        nc.tensor.matmul(PS[:, bank, 0:T], kT[o:o + HD, pr, 0:P], qT[o:o + HD, pr, :],
                                         start=True, stop=True)
                        m = nc.tensor.matmul(PS[:, bank, T:ZW], kT[o:o + HD, pr, P:T], qT[o:o + HD, pr, P:T],
                                             start=True, stop=True)
                    m.then_inc(s["z_psum"], 1)

                def suffix_sums(pr):
                    pe.wait_ge(s["u"], pr + 1)
                    if pr >= 1:
                        pe.wait_ge(s["log_a"], pr)
                    for hh in range(2):
                        u = u_sp[pr % 2][:, hh, :]
                        nc.tensor.matmul(PS[:, 4 + hh, 0:ZW], from_s[:, :], u, start=True, stop=False)
                        m = nc.tensor.matmul(PS[:, 4 + hh, P:T], ones[:, :], u[:, T:ZW], start=False, stop=True)
                    m.then_inc(s["cs_psum"], 1)

                def mix_values(pr):
                    pe.wait_ge(s["att"], pr + 1)
                    if pr >= 2:
                        pe.wait_ge(s["o_lo"], pr - 1)
                    for hh in range(2):
                        o, c = hh * HD, (2 * pr + hh) * HD
                        a = att[pr % 3][:, hh, :]
                        dst = PS[o:o + HD, 6 + pr % 2, :]
                        nc.tensor.matmul(dst[:, 0:T], v_att[:, 0, c:c + HD], a[:, 0:T], start=True, stop=False)
                        m = nc.tensor.matmul(dst[:, P:T], v_att[:, 1, c:c + HD], a[:, T:ZW], start=False, stop=True)
                    m.then_inc(s["o_psum"], 1)

                pe.wait_ge(s["v"], 2)
                pe.wait_ge(s["q"], 2)
                z(0)
                z(1)
                for i in range(NC):
                    if i + 2 < NC:
                        z(i + 2)
                    suffix_sums(i)
                    if i >= 1:
                        mix_values(i - 1)
                mix_values(NC - 1)
                pe.wait_ge(s["o_lo"], NC)
                for m in range(12, 16):
                    token_major(nb + m, xa_hi, xa_lo, lambda j: 2 * j + (m - 12) // 2)

            def moe_phase(k):
                s, nm = moe_sems, norms[f"moe{k}"]
                norm(nm)
                stay_warm(5, 3)
                pe.wait_ge(s["xT_act"], k * PER["xT_act"] + 1)
                pe.wait_ge(s["xT_dve"], k * PER["xT_dve"] + 1)
                for j in range(NT):
                    for b in range(NC):
                        m = nc.tensor.matmul(PS[:, 0, j * NR:(j + 1) * NR], xT[:, b, j * P:(j + 1) * P],
                                             wr[k][:, b, :], start=b == 0, stop=b == NC - 1)
                m.then_inc(s["logits"], 1)
                stay_warm(8, 3)
                pe.wait_ge(s["groups"], k * PER["groups"] + 1)
                for j in range(NT + 1):
                    for i in range(min(j, NT - 1) + 1):
                        m = nc.tensor.matmul(PS[:, 1, j * G:(j + 1) * G], causal[:, :] if i == j else ones[:, :],
                                             groups[:, i, 0:G], start=i == 0, stop=i == min(j, NT - 1))
                m.then_inc(s["places"], 1)
                stay_warm(6, 3)
                pe.wait_ge(s["xt_lo"], k * PER["xt_lo"] + NT)
                gather(k, 0)
                pe.wait_ge(s["n_max"], k * PER["n_max"] + 1)
                most = pe.value_load(n_max_int[0:1, 0:1])
                with pe.If(most < P + 1):
                    packed_experts(k)
                with pe.Else():
                    all_experts(k)

            def gather(k, g):
                pe.wait_ge(packed_sems[k]["pick"], g + 1)
                for b in range(NC):
                    for j in range(NT):
                        for part, x_ in enumerate((xt_hi, xt_lo)):
                            m = nc.tensor.matmul(PS[:, 2 + b // 4, (b % 4) * P:(b % 4 + 1) * P],
                                                 x_[:, j, b * P:(b + 1) * P], pick[:, j, :],
                                                 start=j + part == 0, stop=j + part == 2)
                m.then_inc(packed_sems[k]["gather"], 1)

            def gather_gates(k):
                for j in range(NT):
                    for part, g_ in enumerate((gates_hi, gates_lo)):
                        m = nc.tensor.matmul(PS[:, 6, 256:256 + E], pick[:, j, :], g_[:, j, :],
                                             start=j + part == 0, stop=j + part == 2)
                m.then_inc(packed_sems[k]["slot_gates"], 1)

            def packed_experts(k):
                s, nb = packed_sems[k], base[f"moe{k}"]

                def gate_up(g, n, half):
                    wh, wl = whi[n % HI], wlo[n % LO]
                    pe.wait_ge(lo_ready, g * (3 * EG) + (n + 1))
                    for i in range(4):
                        b = 4 * half + i
                        m = three(PS[:, 4, :], xe_hi[:, b, :], xe_lo[:, b, :], wh[:, i, :], wl[:, i, :],
                                  b == 0, b == NC - 1)
                    m.then_inc(piece_used, 1)

                def down(g, n, done, first, last, half_done=None):
                    wh = whi[n % HI][:, :, :].rearrange("p (f a) c -> p f a c", f=NF)
                    wl = wlo[n % LO][:, :, :].rearrange("p (f a) c -> p f a c", f=NF)
                    pe.wait_ge(lo_ready, g * (3 * EG) + (n + 1))
                    pe.wait_ge(*ex(k, "hT_lo", done))
                    for a in range(2):
                        for f in range(NF):
                            m = three(PS[:, a, :], hs_hi[:, f, :], hs_lo[:, f, :], wh[:, f, a, :], wl[:, f, a, :],
                                      first and f == 0, last and f == NF - 1)
                        if half_done and a == 0:
                            m.then_inc(half_done, 1)
                    m.then_inc(piece_used, 1)

                def turn(e):
                    pe.wait_ge(*ex(k, "hact", e * 2 + 2))
                    for f in range(NF):
                        m = nc.tensor.transpose(PS[:, 5, f * P:(f + 1) * P], hact_s[:, f * P:(f + 1) * P], ident[:, :])
                    m.then_inc(expert_sems["hT_psum"], 1)

                def combine(j, a, bank):
                    for part, y_ in enumerate((y_hi, y_lo)):
                        m = nc.tensor.matmul(PS[:, bank, :], pick_t[:, j * P:(j + 1) * P], y_[:, a, :],
                                             start=part == 0, stop=part == 1)
                    m.then_inc(s["combined"], 1)

                def group(g):
                    later = not (isinstance(g, int) and g == 0)
                    for i in range(EG):
                        e, n0 = g * EG + i, nb - 1 + 3 * i
                        first = not later and i == 0
                        if i == 0:
                            pe.wait_ge(*ex(k, "x_lo", g + 1))
                        gate_up(g, n0 + first, 0)
                        gate_up(g, n0 + 1 + first, 1)
                        if i == 3 and not is_last(g):
                            pe.wait_ge(s["pt"], g + 1)
                            if later:
                                pe.wait_ge(s["added"], g * 4)
                            gather(k, g + 1)
                            gather_gates(k)
                        if not first:
                            if i == 1 and later:
                                pe.wait_ge(s["y_lo"], g)
                            down(g, n0 + 2, e, i == 1, i == 0)
                        turn(e)
                        if i in (1, 2) and later:
                            if i == 1:
                                pe.wait_ge(s["y_lo"], g)
                                pe.wait_ge(s["pt"], g)
                            else:
                                pe.wait_ge(s["added"], g * 4 - 2)
                            for a in range(2):
                                combine(i - 1, a, 6 + a)
                        if i == 2:
                            for j in range(NT):
                                m = nc.tensor.matmul(PS[:, 3, j * P:(j + 1) * P], pick[:, j, :], ident_r[:, :],
                                                     start=True, stop=True)
                            m.then_inc(s["pt_psum"], 1)

                stay_warm(8, 5)
                pe.wait_ge(moe_sems["gates_parts"], k * PER["gates_parts"] + 1)
                gather_gates(k)
                group(0)
                with pe.Fori(1, G - 1) as g:
                    group(g)
                group(G - 1)
                down(0, nb + 3 * E - 1, E, False, True, s["y_psum"])
                pe.wait_ge(s["pt"], G)
                pe.wait_ge(s["added"], (G - 1) * 4)
                for a in range(2):
                    pe.wait_ge(s["y_lo"], G + a)
                    for j in range(NT):
                        combine(j, a, 4 + 2 * j + a)

            def all_experts(k):
                nb = base[f"moe{k}"]
                pe.wait_ge(*ex(k, "x_lo", G))

                def gate_up(g, n, half):
                    wh, wl = whi[n % HI], wlo[n % LO]
                    pe.wait_ge(lo_ready, g * (3 * EG) + (n + 1))
                    for j in range(NT):
                        for i in range(4):
                            b = 4 * half + i
                            m = three(PS[:, 4 + j, :], xa_hi[:, b, j * P:(j + 1) * P], xa_lo[:, b, j * P:(j + 1) * P],
                                      wh[:, i, :], wl[:, i, :], b == 0, b == NC - 1)
                    m.then_inc(piece_used, 1)

                def down(g, n, done, first, last):
                    wh = whi[n % HI][:, :, :].rearrange("p (f a) c -> p f a c", f=NF)
                    wl = wlo[n % LO][:, :, :].rearrange("p (f a) c -> p f a c", f=NF)
                    pe.wait_ge(lo_ready, g * (3 * EG) + (n + 1))
                    pe.wait_ge(*ex(k, "hT_lo", done))
                    for j in range(NT):
                        for a in range(2):
                            for f in range(NF):
                                m = three(PS[:, 2 * j + a, :], hT_hi[:, f, j * P:(j + 1) * P],
                                          hT_lo[:, f, j * P:(j + 1) * P], wh[:, f, a, :], wl[:, f, a, :],
                                          first and f == 0, last and f == NF - 1)
                    m.then_inc(piece_used, 1)

                def turn(e):
                    for j in range(NT):
                        pe.wait_ge(*ex(k, "hact", e * 2 + (j + 1)))
                        for f in range(NF):
                            m = nc.tensor.transpose(PS[:, 6, f * T + j * P:f * T + (j + 1) * P],
                                                    hact[:, j, f * P:(f + 1) * P], ident[:, :])
                    m.then_inc(expert_sems["hT_psum"], 1)

                def group(g):
                    for i in range(EG):
                        e, n0 = g * EG + i, nb - 1 + 3 * i
                        first = isinstance(g, int) and i == 0
                        gate_up(g, n0 + first, 0)
                        gate_up(g, n0 + 1 + first, 1)
                        if not first:
                            down(g, n0 + 2, e, isinstance(g, int) and i == 1, False)
                        turn(e)

                group(0)
                with pe.Fori(1, G) as g:
                    group(g)
                down(0, nb + 3 * E - 1, E, False, True)

            for ph in PHASES:
                if ph.startswith("moe"):
                    moe_phase(int(ph[3]))
                if ph == "rwkv":
                    rwkv_phase()
                if ph == "attn":
                    attn_phase()


_INS = ["x", "norm_mix", "norm_ffn", "norm_kv", "norm_final", "rw_mix", "rw_w_rkv", "rw_w0", "rw_w1", "rw_w2",
        "rw_a0", "rw_a1", "rw_a2", "rw_g1", "rw_g2", "rw_k_k", "rw_k_a", "rw_r_k", "rw_lnx_w", "rw_lnx_b",
        "rw_w_out", "w_kv", "sb_w_q", "sb_w_out", "moe_w_group", "moe_b_group", "moe_w_inner", "moe_b_inner",
        "moe_w_gate", "moe_w_up", "moe_w_down"]


def kernel(**inputs):
    import numpy as _np
    import concourse.bacc as _bacc
    from concourse import mybir as _mybir
    from concourse.bass_utils import run_bass_kernel_spmd as _run

    nc = _bacc.Bacc("TRN2", target_bir_lowering=False, num_devices=1)
    arrays, args = {}, []
    for name in _INS:
        a = _np.ascontiguousarray(inputs[name])
        arrays[f"in_{name}_dram"] = a
        args.append(nc.dram_tensor(f"in_{name}_dram", a.shape, _mybir.dt.from_np(a.dtype), kind="ExternalInput").ap())
    args.append(nc.dram_tensor("out_0_dram", inputs["x"].shape, _mybir.dt.float32, kind="ExternalOutput").ap())
    trunk_program(nc, *args)
    r = _run(nc, [arrays], core_ids=[0])
    return r.results[0]["out_0_dram"]
```
